# Optimizing a Trainium2 kernel written in Bass

```python
import math
import jax, jax.numpy as jnp
from jax import lax
import numpy as np

D_MODEL = 1024
BATCH = 1
SEQ = 512
DEPTH = 1
DEC_BATCH = 8
DEC_SEQ = 1
PAST_LEN = 2048
PAGE_SIZE = 128

N_META = 16
N_HEADS = 16
N_KV_HEADS = 4
HEAD_DIM = 64
Q_PER_KV = N_HEADS // N_KV_HEADS
WINDOW = 128
BLOCK = 128
META_PAD = BLOCK - N_META
ROPE_THETA = 10000.0
SSM_INNER = D_MODEL
SSM_HEAD_DIM = 64
SSM_HEADS = SSM_INNER // SSM_HEAD_DIM
SSM_GROUPS = 4
HEADS_PER_GROUP = SSM_HEADS // SSM_GROUPS
SSM_STATE = 128
CONV_WIDTH = 4
CONV_DIM = SSM_INNER + 2 * SSM_GROUPS * SSM_STATE
Q_DIM = N_HEADS * HEAD_DIM
KV_DIM = N_KV_HEADS * HEAD_DIM
IN_DIM = Q_DIM + 2 * KV_DIM + SSM_INNER + CONV_DIM + SSM_HEADS + 2 * D_MODEL
N_EXPERT_GROUPS = 4
EXPERTS_PER_GROUP = 8
N_EXPERTS = N_EXPERT_GROUPS * EXPERTS_PER_GROUP
TOP_K_IN_GROUP = 2
D_EXPERT = 256
ALPHA = (2 * DEPTH) ** 0.25
BETA = (8 * DEPTH) ** -0.25
LN_EPS = 1e-5
RMS_EPS = 1e-5
NEG_INF = -1e30

kernel_name = 'hybrid_swa_ssd_hmoe_decoder_step'

def layer_norm(x, g, b):
    xf = x.astype(jnp.float32)
    mu = jnp.mean(xf, -1, keepdims=True)
    var = jnp.mean(jnp.square(xf - mu), -1, keepdims=True)
    y = (xf - mu) * lax.rsqrt(var + LN_EPS)
    return (y * g.astype(jnp.float32) + b.astype(jnp.float32)).astype(x.dtype)

def rope(x, pos):
    half = HEAD_DIM // 2
    inv_freq = jnp.exp(-math.log(ROPE_THETA) * jnp.arange(half, dtype=jnp.float32) * (2.0 / HEAD_DIM))
    ang = pos.astype(jnp.float32)[:, None] * inv_freq[None, :]
    cos = jnp.cos(ang)[:, None, :]
    sin = jnp.sin(ang)[:, None, :]
    xf = x.astype(jnp.float32)
    x1, x2 = xf[..., :half], xf[..., half:]
    return jnp.concatenate([x1 * cos - x2 * sin, x2 * cos + x1 * sin], -1).astype(x.dtype)

def split_in(u):
    sizes = (Q_DIM, KV_DIM, KV_DIM, SSM_INNER, CONV_DIM, SSM_HEADS, D_MODEL, D_MODEL)
    parts, start = [], 0
    for s in sizes:
        parts.append(u[..., start:start + s])
        start += s
    return parts

def split_xbc(t):
    gn = SSM_GROUPS * SSM_STATE
    return t[..., :SSM_INNER], t[..., SSM_INNER:SSM_INNER + gn], t[..., SSM_INNER + gn:]

def causal_conv(hist, xbc, w, b):
    s = xbc.shape[1]
    full = jnp.concatenate([hist.astype(xbc.dtype), xbc], axis=1)
    y = b
    for j in range(CONV_WIDTH):
        y = y + full[:, j:j + s] * w[j]
    return jax.nn.silu(y), full[:, -(CONV_WIDTH - 1):]

def gated_rmsnorm(y, z, w):
    yf = y.astype(jnp.float32) * jax.nn.silu(z.astype(jnp.float32))
    shp = yf.shape
    yg = yf.reshape(shp[:-1] + (SSM_GROUPS, SSM_INNER // SSM_GROUPS))
    yg = yg * lax.rsqrt(jnp.mean(jnp.square(yg), -1, keepdims=True) + RMS_EPS)
    return yg.reshape(shp) * w.astype(jnp.float32)

def segsum(a):
    t = a.shape[-1]
    cs = jnp.cumsum(a, -1)
    diff = cs[..., :, None] - cs[..., None, :]
    return jnp.where(jnp.tril(jnp.ones((t, t), dtype=bool)), diff, -jnp.inf)

def ssd_chunked(x, dt, a, bm, cm):
    b, seq = x.shape[:2]
    nc = seq // BLOCK
    xd = (x * dt[..., None]).reshape(b, nc, BLOCK, SSM_GROUPS, HEADS_PER_GROUP, SSM_HEAD_DIM)
    ad = (dt * a).reshape(b, nc, BLOCK, SSM_GROUPS, HEADS_PER_GROUP).transpose(0, 3, 4, 1, 2)
    bc = bm.reshape(b, nc, BLOCK, SSM_GROUPS, SSM_STATE)
    cc = cm.reshape(b, nc, BLOCK, SSM_GROUPS, SSM_STATE)
    a_cs = jnp.cumsum(ad, -1)
    lmat = jnp.exp(segsum(ad))
    cb = jnp.einsum('bclgn,bcsgn->bgcls', cc, bc)
    y_diag = jnp.einsum('bgcls,bgrcls,bcsgrp->bclgrp', cb, lmat, xd)
    decay_states = jnp.exp(a_cs[..., -1:] - a_cs)
    states = jnp.einsum('bclgn,bgrcl,bclgrp->bcgrpn', bc, decay_states, xd)
    states = jnp.concatenate([jnp.zeros_like(states[:, :1]), states], axis=1)
    chunk_tot = jnp.pad(a_cs[..., -1], ((0, 0), (0, 0), (0, 0), (1, 0)))
    decay_chunk = jnp.exp(segsum(chunk_tot))
    new_states = jnp.einsum('bgrzc,bcgrpn->bzgrpn', decay_chunk, states)
    states, final = new_states[:, :-1], new_states[:, -1]
    y_off = jnp.einsum('bclgn,bcgrpn,bgrcl->bclgrp', cc, states, jnp.exp(a_cs))
    y = (y_diag + y_off).reshape(b, seq, SSM_HEADS, SSM_HEAD_DIM)
    return y, final.reshape(b, SSM_HEADS, SSM_HEAD_DIM, SSM_STATE)

def ssd_recurrent(h0, x, dt, a, bm, cm):
    def step(h, inp):
        x_t, dt_t, b_t, c_t = inp
        b_h = jnp.repeat(b_t, HEADS_PER_GROUP, axis=1)
        c_h = jnp.repeat(c_t, HEADS_PER_GROUP, axis=1)
        h = h * jnp.exp(dt_t * a)[:, :, None, None] + jnp.einsum('nhp,nhs->nhps', x_t * dt_t[:, :, None], b_h)
        return h, jnp.einsum('nhps,nhs->nhp', h, c_h)
    seqs = (jnp.swapaxes(x, 0, 1), jnp.swapaxes(dt, 0, 1), jnp.swapaxes(bm, 0, 1), jnp.swapaxes(cm, 0, 1))
    h_last, ys = lax.scan(step, h0, seqs)
    return jnp.swapaxes(ys, 0, 1), h_last

def softmax_with_sink(logits, sinks):
    sink = jnp.broadcast_to(sinks.astype(jnp.float32).reshape(N_KV_HEADS, Q_PER_KV)[:, :, None, None],
                            logits.shape[:-1] + (1,))
    probs = jax.nn.softmax(jnp.concatenate([logits, sink], axis=-1), axis=-1)
    return probs[..., :-1]

def banded_attention(q, k, v, meta_k, meta_v, pos, sinks):
    b, lp = q.shape[:2]
    nb = lp // BLOCK
    scale = HEAD_DIM ** -0.5
    qb = q.reshape(b, nb, BLOCK, N_KV_HEADS, Q_PER_KV, HEAD_DIM)
    kb = k.reshape(b, nb, BLOCK, N_KV_HEADS, HEAD_DIM)
    vb = v.reshape(b, nb, BLOCK, N_KV_HEADS, HEAD_DIM)
    prev = lambda t: jnp.concatenate([jnp.zeros_like(t[:, :1]), t[:, :-1]], axis=1)
    k_band = jnp.concatenate([prev(kb), kb], axis=2)
    v_band = jnp.concatenate([prev(vb), vb], axis=2)
    pos_b = pos.reshape(nb, BLOCK)
    pos_prev = jnp.concatenate([jnp.full((1, BLOCK), -1, jnp.int32), pos_b[:-1]], axis=0)
    pk = jnp.concatenate([pos_prev, pos_b], axis=1)[:, None, :]
    pq = pos_b[:, :, None]
    band_mask = (pk >= N_META) & (pk <= pq) & (pq - pk < WINDOW)
    meta_mask = jnp.arange(N_META, dtype=jnp.int32)[None, None, :] <= pq
    s_band = jnp.einsum('bnqkgd,bnskd->bnkgqs', qb, k_band).astype(jnp.float32) * scale
    s_meta = jnp.einsum('bnqkgd,bmkd->bnkgqm', qb, meta_k).astype(jnp.float32) * scale
    s_band = jnp.where(band_mask[None, :, None, None], s_band, NEG_INF)
    s_meta = jnp.where(meta_mask[None, :, None, None], s_meta, NEG_INF)
    probs = softmax_with_sink(jnp.concatenate([s_band, s_meta], axis=-1), sinks).astype(v.dtype)
    out = (jnp.einsum('bnkgqs,bnskd->bnqkgd', probs[..., :2 * BLOCK], v_band)
           + jnp.einsum('bnkgqm,bmkd->bnqkgd', probs[..., 2 * BLOCK:], meta_v))
    return out.reshape(b, lp, Q_DIM)

def window_attention_step(q, k_new, v_new, meta_k, meta_v, win_k, win_v, sinks):
    n, t = q.shape[:2]
    w = win_k.shape[1]
    scale = HEAD_DIM ** -0.5
    qg = q.reshape(n, t, N_KV_HEADS, Q_PER_KV, HEAD_DIM)
    keys = jnp.concatenate([meta_k.astype(k_new.dtype), win_k.astype(k_new.dtype), k_new], axis=1)
    vals = jnp.concatenate([meta_v.astype(v_new.dtype), win_v.astype(v_new.dtype), v_new], axis=1)
    pq = (PAST_LEN + jnp.arange(t, dtype=jnp.int32))[:, None]
    pk = jnp.concatenate([jnp.arange(N_META, dtype=jnp.int32),
                          PAST_LEN - w + jnp.arange(w, dtype=jnp.int32),
                          PAST_LEN + jnp.arange(t, dtype=jnp.int32)])
    is_meta = (jnp.arange(pk.shape[0]) < N_META)[None, :]
    pk = pk[None, :]
    mask = (pk <= pq) & (is_meta | ((pk >= N_META) & (pq - pk < WINDOW)))
    s = jnp.einsum('ntkgd,nskd->nkgts', qg, keys).astype(jnp.float32) * scale
    s = jnp.where(mask[None, None, None], s, NEG_INF)
    probs = softmax_with_sink(s, sinks).astype(vals.dtype)
    return jnp.einsum('nkgts,nskd->ntkgd', probs, vals).reshape(n, t, Q_DIM)

def merge_branches(y_attn, y_ssd, g_a, g_s, w_o):
    return (jax.nn.sigmoid(g_a) * y_attn + jax.nn.sigmoid(g_s) * y_ssd) @ w_o

def mixer_prompt(h, pos, valid, w_in, attn_sinks, conv_w, conv_b, dt_bias, a_log, d_skip, ssm_norm_w, w_o):
    b, lp, _ = h.shape
    q, k, v, z, xbc, dt_raw, g_a, g_s = split_in(h @ w_in)
    q = rope(q.reshape(b, lp, N_HEADS, HEAD_DIM), pos)
    k = rope(k.reshape(b, lp, N_KV_HEADS, HEAD_DIM), pos)
    v = v.reshape(b, lp, N_KV_HEADS, HEAD_DIM)
    meta_k, meta_v = k[:, META_PAD:BLOCK], v[:, META_PAD:BLOCK]
    y_attn = banded_attention(q, k, v, meta_k, meta_v, pos, attn_sinks)
    xbc_c, conv_state = causal_conv(jnp.zeros((b, CONV_WIDTH - 1, CONV_DIM), xbc.dtype), xbc, conv_w, conv_b)
    xs, bm, cm = split_xbc(xbc_c)
    dt = jnp.where(valid[None, :, None],
                   jax.nn.softplus(dt_raw.astype(jnp.float32) + dt_bias.astype(jnp.float32)), 0.0)
    a = -jnp.exp(a_log.astype(jnp.float32))
    xs_h = xs.reshape(b, lp, SSM_HEADS, SSM_HEAD_DIM).astype(jnp.float32)
    y, ssm_state = ssd_chunked(xs_h, dt, a,
                               bm.reshape(b, lp, SSM_GROUPS, SSM_STATE).astype(jnp.float32),
                               cm.reshape(b, lp, SSM_GROUPS, SSM_STATE).astype(jnp.float32))
    y = y + d_skip.astype(jnp.float32)[:, None] * xs_h
    y_ssd = gated_rmsnorm(y.reshape(b, lp, SSM_INNER), z, ssm_norm_w).astype(h.dtype)
    mix = merge_branches(y_attn, y_ssd, g_a, g_s, w_o)
    return (mix, meta_k, meta_v, k[:, -WINDOW:], v[:, -WINDOW:], conv_state, ssm_state.astype(h.dtype))

def mixer_sample(h, meta_k, meta_v, win_k, win_v, conv_state, ssm_state,
                 w_in, attn_sinks, conv_w, conv_b, dt_bias, a_log, d_skip, ssm_norm_w, w_o):
    n, t, _ = h.shape
    pos = PAST_LEN + jnp.arange(t, dtype=jnp.int32)
    q, k, v, z, xbc, dt_raw, g_a, g_s = split_in(h @ w_in)
    q = rope(q.reshape(n, t, N_HEADS, HEAD_DIM), pos)
    k = rope(k.reshape(n, t, N_KV_HEADS, HEAD_DIM), pos)
    v = v.reshape(n, t, N_KV_HEADS, HEAD_DIM)
    y_attn = window_attention_step(q, k, v, meta_k, meta_v, win_k, win_v, attn_sinks)
    xbc_c, new_conv = causal_conv(conv_state, xbc, conv_w, conv_b)
    xs, bm, cm = split_xbc(xbc_c)
    dt = jax.nn.softplus(dt_raw.astype(jnp.float32) + dt_bias.astype(jnp.float32))
    a = -jnp.exp(a_log.astype(jnp.float32))
    xs_h = xs.reshape(n, t, SSM_HEADS, SSM_HEAD_DIM).astype(jnp.float32)
    y, new_ssm = ssd_recurrent(ssm_state.astype(jnp.float32), xs_h, dt, a,
                               bm.reshape(n, t, SSM_GROUPS, SSM_STATE).astype(jnp.float32),
                               cm.reshape(n, t, SSM_GROUPS, SSM_STATE).astype(jnp.float32))
    y = y + d_skip.astype(jnp.float32)[:, None] * xs_h
    y_ssd = gated_rmsnorm(y.reshape(n, t, SSM_INNER), z, ssm_norm_w).astype(h.dtype)
    mix = merge_branches(y_attn, y_ssd, g_a, g_s, w_o)
    return (mix, k, v, new_conv, new_ssm.astype(ssm_state.dtype))

def hier_moe(h, rg_w, rg_b, re_w, re_b, w_gate, w_up, w_down):
    shp = h.shape
    x = h.reshape(-1, D_MODEL)
    g_logits = (x @ rg_w).astype(jnp.float32) + rg_b.astype(jnp.float32)
    g_prob = jax.nn.softmax(g_logits, axis=-1)
    g_sel = jnp.argmax(g_logits, axis=-1)
    g_w = jnp.take_along_axis(g_prob, g_sel[:, None], axis=-1)[:, 0]
    e_logits = ((x @ re_w).astype(jnp.float32) + re_b.astype(jnp.float32)).reshape(-1, N_EXPERT_GROUPS, EXPERTS_PER_GROUP)
    e_in = jnp.take_along_axis(e_logits, g_sel[:, None, None], axis=1)[:, 0]
    top_v, top_i = lax.top_k(e_in, TOP_K_IN_GROUP)
    top_p = jax.nn.softmax(top_v, axis=-1) * g_w[:, None]
    comb = jnp.sum(jax.nn.one_hot(top_i, EXPERTS_PER_GROUP, dtype=jnp.float32) * top_p[..., None], axis=1)
    y = jnp.zeros_like(x)
    for g in range(N_EXPERT_GROUPS):
        sl = slice(g * EXPERTS_PER_GROUP, (g + 1) * EXPERTS_PER_GROUP)
        hid = jax.nn.silu(jnp.einsum('md,edf->mef', x, w_gate[sl])) * jnp.einsum('md,edf->mef', x, w_up[sl])
        wg = jnp.where((g_sel == g)[:, None], comb, 0.0).astype(x.dtype)
        y = y + jnp.einsum('mef,me,efd->md', hid, wg, w_down[sl])
    return y.reshape(shp)

def setup_inputs(seed: int = 0) -> dict:
    key = jax.random.key(seed)
    ks = jax.random.split(key, 32)
    nrm = lambda k, shape, s=1.0: jax.random.normal(k, shape, jnp.float32) * s
    w_buf = min(WINDOW, PAST_LEN)
    dt0 = jnp.exp(jax.random.uniform(ks[12], (DEPTH, SSM_HEADS), jnp.float32, math.log(1e-3), math.log(1e-1)))
    dt_bias = dt0 + jnp.log(-jnp.expm1(-dt0))
    a_log = jnp.log(jax.random.uniform(ks[13], (DEPTH, SSM_HEADS), jnp.float32, 1.0, 16.0))
    return {
        'x_prompt': nrm(ks[0], (BATCH, SEQ, D_MODEL)),
        'x_sample': nrm(ks[1], (DEC_BATCH, DEC_SEQ, D_MODEL)),
        'cache_meta_k': nrm(ks[2], (DEPTH, DEC_BATCH, N_META, N_KV_HEADS, HEAD_DIM)),
        'cache_meta_v': nrm(ks[3], (DEPTH, DEC_BATCH, N_META, N_KV_HEADS, HEAD_DIM)),
        'cache_win_k': nrm(ks[4], (DEPTH, DEC_BATCH, w_buf, N_KV_HEADS, HEAD_DIM)),
        'cache_win_v': nrm(ks[5], (DEPTH, DEC_BATCH, w_buf, N_KV_HEADS, HEAD_DIM)),
        'state_conv': nrm(ks[6], (DEPTH, DEC_BATCH, CONV_WIDTH - 1, CONV_DIM)),
        'state_ssm': nrm(ks[7], (DEPTH, DEC_BATCH, SSM_HEADS, SSM_HEAD_DIM, SSM_STATE), 0.5),
        'meta_tokens': nrm(ks[8], (N_META, D_MODEL)),
        'w_in': nrm(ks[9], (DEPTH, D_MODEL, IN_DIM), D_MODEL ** -0.5),
        'attn_sinks': nrm(ks[10], (DEPTH, N_HEADS)),
        'conv_w': nrm(ks[11], (DEPTH, CONV_WIDTH, CONV_DIM), CONV_WIDTH ** -0.5),
        'conv_b': nrm(ks[14], (DEPTH, CONV_DIM), 0.02),
        'dt_bias': dt_bias,
        'a_log': a_log,
        'd_skip': 1.0 + nrm(ks[15], (DEPTH, SSM_HEADS), 0.1),
        'ssm_norm_w': 1.0 + nrm(ks[16], (DEPTH, SSM_INNER), 0.1),
        'w_o': nrm(ks[17], (DEPTH, D_MODEL, D_MODEL), BETA * D_MODEL ** -0.5),
        'ln1_g': 1.0 + nrm(ks[18], (DEPTH, D_MODEL), 0.1),
        'ln1_b': nrm(ks[19], (DEPTH, D_MODEL), 0.02),
        'router_group_w': nrm(ks[20], (DEPTH, D_MODEL, N_EXPERT_GROUPS), D_MODEL ** -0.5),
        'router_group_b': nrm(ks[21], (DEPTH, N_EXPERT_GROUPS), 0.01),
        'router_expert_w': nrm(ks[22], (DEPTH, D_MODEL, N_EXPERTS), D_MODEL ** -0.5),
        'router_expert_b': nrm(ks[23], (DEPTH, N_EXPERTS), 0.01),
        'w_gate': nrm(ks[24], (DEPTH, N_EXPERTS, D_MODEL, D_EXPERT), D_MODEL ** -0.5),
        'w_up': nrm(ks[25], (DEPTH, N_EXPERTS, D_MODEL, D_EXPERT), D_MODEL ** -0.5),
        'w_down': nrm(ks[26], (DEPTH, N_EXPERTS, D_EXPERT, D_MODEL), BETA * D_EXPERT ** -0.5),
        'ln2_g': 1.0 + nrm(ks[27], (DEPTH, D_MODEL), 0.1),
        'ln2_b': nrm(ks[28], (DEPTH, D_MODEL), 0.02),
    }

def reference(x_prompt, x_sample, cache_meta_k, cache_meta_v, cache_win_k, cache_win_v, state_conv, state_ssm,
              meta_tokens, w_in, attn_sinks, conv_w, conv_b, dt_bias, a_log, d_skip, ssm_norm_w, w_o,
              ln1_g, ln1_b, router_group_w, router_group_b, router_expert_w, router_expert_b,
              w_gate, w_up, w_down, ln2_g, ln2_b):
    b = x_prompt.shape[0]
    lp = BLOCK + x_prompt.shape[1]
    pos = jnp.arange(lp, dtype=jnp.int32) - META_PAD
    valid = pos >= 0
    meta = jnp.broadcast_to(meta_tokens.astype(x_prompt.dtype)[None], (b, N_META, D_MODEL))
    hp = jnp.concatenate([jnp.zeros((b, META_PAD, D_MODEL), x_prompt.dtype), meta, x_prompt], axis=1)
    hs = x_sample
    pmk, pmv, pwk, pwv, pcv, pss, swk, swv, scv, sss = [], [], [], [], [], [], [], [], [], []
    for l in range(DEPTH):
        hp = jnp.where(valid[None, :, None], hp, 0.0).astype(x_prompt.dtype)
        mix, mk, mv, wk, wv, cs, ss = mixer_prompt(hp, pos, valid, w_in[l], attn_sinks[l], conv_w[l], conv_b[l],
                                                  dt_bias[l], a_log[l], d_skip[l], ssm_norm_w[l], w_o[l])
        hp = layer_norm(ALPHA * hp + mix, ln1_g[l], ln1_b[l])
        hp = layer_norm(ALPHA * hp + hier_moe(hp, router_group_w[l], router_group_b[l], router_expert_w[l],
                                              router_expert_b[l], w_gate[l], w_up[l], w_down[l]), ln2_g[l], ln2_b[l])
        mix_s, nk, nv, ncs, nss = mixer_sample(hs, cache_meta_k[l], cache_meta_v[l], cache_win_k[l], cache_win_v[l],
                                               state_conv[l], state_ssm[l], w_in[l], attn_sinks[l], conv_w[l],
                                               conv_b[l], dt_bias[l], a_log[l], d_skip[l], ssm_norm_w[l], w_o[l])
        hs = layer_norm(ALPHA * hs + mix_s, ln1_g[l], ln1_b[l])
        hs = layer_norm(ALPHA * hs + hier_moe(hs, router_group_w[l], router_group_b[l], router_expert_w[l],
                                              router_expert_b[l], w_gate[l], w_up[l], w_down[l]), ln2_g[l], ln2_b[l])
        pmk.append(mk); pmv.append(mv); pwk.append(wk); pwv.append(wv); pcv.append(cs); pss.append(ss)
        swk.append(nk); swv.append(nv); scv.append(ncs); sss.append(nss)
    y_prompt = hp[:, BLOCK:]
    y_sample = hs
    return (y_prompt, y_sample,
            jnp.stack(pmk), jnp.stack(pmv), jnp.stack(pwk), jnp.stack(pwv), jnp.stack(pcv), jnp.stack(pss),
            jnp.stack(swk), jnp.stack(swv), jnp.stack(scv), jnp.stack(sss))


_drawn_inputs = setup_inputs


def setup_inputs(seed=0):
    import zlib

    import numpy as np

    out = dict(_drawn_inputs(seed))
    spreads = {}
    factors = {'cache_meta_k': 6.45,
     'cache_meta_v': 4.961,
     'attn_sinks': 8.0,
     'd_skip': 10.419,
     'router_group_b': 42.549,
     'router_expert_b': 19.621,
     'ln2_b': 2.745,
     'cache_win_k': 8.0,
     'cache_win_v': 8.0}
    for name, (base, spread) in spreads.items():
        noise = np.random.default_rng([zlib.crc32(name.encode()), seed]).standard_normal(out[name].shape)
        drawn = base * np.exp(spread * noise) if base else spread * noise
        out[name] = __import__('jax').numpy.asarray(drawn.astype(out[name].dtype))
    for name, factor in factors.items():
        out[name] = (out[name] * factor).astype(out[name].dtype)
    return out
```

```python
from contextlib import ExitStack

import concourse.bass as bass
import numpy as np
from concourse import mybir

F32 = mybir.dt.float32
BF16 = mybir.dt.bfloat16
I32 = mybir.dt.int32
U32 = mybir.dt.uint32
ALU = mybir.AluOpType
ACT = mybir.ActivationFunctionType
AX = mybir.AxisListType.X

P = 128
D = 1024
KC = D // P
NSAMP, NMETA, NPROMPT = 8, 16, 512
SEQ0 = NSAMP
PR0 = NSAMP + NMETA
NTOK = PR0 + NPROMPT
NSEQ = NMETA + NPROMPT
HALF = NTOK // 2
NBLK = NPROMPT // P
NT = NBLK + 1
META = NT
H, KVH, HD = 16, 4, 64
QPK = H // KVH
NST = 128
WIN = 128
NWK = WIN - 1
PAST = 2048
CW = 4
XT_TILES = 16
QT_TILES, KT_TILES = 8, 2
FT = XT_TILES + QT_TILES + KT_TILES
VD = KVH * HD + H
NE, NG, EPG, DE = 32, 4, 8, 256
NPAIR = NE // 2
NOV = 8
NBT = NPAIR + NOV
ALPHA = 2.0 ** 0.25
LN_EPS = 1e-5
RMS_EPS = 1e-5
SCALE = HD ** -0.5
NEG = -1e30

PACK = {}
_at = 0
for _name, _n in (("ident", P), ("upper", P), ("ones", P), ("neg", P), ("strict", P), ("amask", P + NMETA + P),
                  ("iota_p", 1), ("iota4", NG), ("iota8", EPG), ("iota16", NPAIR), ("half32", NE), ("iota32", NE), ("valid", NT),
                  ("conv_w", XT_TILES * CW), ("conv_b", XT_TILES), ("dt_bias", H), ("a_log", H), ("d_skip", H),
                  ("sinks", H), ("sink_col", 1), ("d_col", KC), ("r_bias", NG + NE)):
    PACK[_name] = (_at, _at + _n)
    _at += _n
NPACK = _at


def tile_cols(t):
    return (0, NSAMP) if t == 0 else (PR0 + P * (t - 1), PR0 + P * t)


def row_cols(t):
    return (0, NSAMP) if t == 0 else (NSAMP + P * (t - 1), NSAMP + P * t)


def tile_rows(t):
    return NSAMP if t == 0 else P


def build(nc, io):
    ctx = ExitStack()
    with ctx:
        def sem(name):
            return ctx.enter_context(nc.semaphore(name))

        arena = ctx.enter_context(nc.sbuf_tensor("arena", [P, 53160], F32))

        def cut(at, *shape):
            n = 1
            for s in shape:
                n *= s
            v = arena[:, at:at + n]
            if len(shape) == 1:
                return v
            names = "abcd"[:len(shape)]
            return v.rearrange(f"p ({' '.join(names)}) -> p {' '.join(names)}",
                               **{c: s for c, s in zip(names[1:], shape[1:])})

        pack = cut(0, NPACK)

        def pk(name, rows=P):
            a, b = PACK[name]
            return pack[0:rows, a:b]

        ident, upper, onesf = pk("ident"), pk("upper"), pk("ones")
        wr = cut(1200, KC, NG + NE)
        bfc = cut(1488, 256).bitcast(BF16).rearrange("p (a b) -> p a b", a=4)
        identb, negb, strictb, onesb = (bfc[:, i, :] for i in range(4))
        C1 = 1744
        dtx, dab, dex, dt, adt, ncs, tot, tmc, ecs, dst, etot = (cut(C1 + 96 * i, NT + 1, H) for i in range(11))
        pconv = cut(C1 + 1056, XT_TILES, CW - 1)
        small = cut(2850, 150)

        R1, RY, RYA, RX, RQ, RV, RXT, RW = 3000, 13240, 18360, 23480, 32616, 39048, 40680, 44968
        Y = cut(RY, NT, D)
        YA = cut(RYA, NT, D)
        xbc = cut(RX, XT_TILES, 3 + NSEQ)
        xs4 = cut(RX + 8496, XT_TILES, CW, NSAMP)
        xcs = cut(RX + 9008, XT_TILES, NSAMP)
        qT = cut(RQ, QT_TILES, NTOK)
        kd = cut(RQ + 4288, KVH, NTOK)
        vd = cut(RV, NT + 1, VD)
        xT = cut(RXT, KC, NTOK)
        wf = [cut(RW + 1024 * i, KC, P) for i in range(4)]
        wvd = cut(RW + 4096, KC, VD)
        wt = [cut(RW + 4096 * i, KC, 512) for i in range(2)]

        acc = [cut(R1 + 528 * i, NSEQ) for i in range(2)]
        raw = [cut(R1 + 1056 + 536 * i, NTOK) for i in range(2)]
        swp, rcs = cut(R1 + 2128, NTOK), cut(R1 + 2664, NTOK)
        cosT, sinT = cut(R1 + 3200, NTOK), cut(R1 + 3736, NTOK)
        acc_s, tmp_s = cut(R1 + 4272, XT_TILES, NSAMP), cut(R1 + 4400, XT_TILES, NSAMP)
        xt = cut(R1, D)
        Bt = cut(R1 + 1024, KVH * NST)
        xd, xdd, Dx, Hs, Ht = (cut(R1 + 1536 + 1024 * i, D) for i in range(5))
        LG = [cut(R1 + 6656 + 512 * i, QPK * P) for i in range(4)]
        bcs = cut(R1 + 8704, P)
        ds = cut(R1 + 8832, 2, H)
        dd = cut(R1 + 8864, NSAMP, 2, H)
        dcol, dtcol, xdt = (cut(R1 + 9120 + 64 * i, KC, NSAMP) for i in range(3))
        ys = cut(R1 + 9312, KC, NSAMP)
        junk = cut(R1 + 6656, NSAMP, NST)
        bcg = cut(RYA, 2, NSAMP, NST)
        hst = [cut(RYA + 2048 + 1024 * i, NSAMP, NST) for i in range(3)]
        AW = P + NMETA + P
        sS = [cut(R1 + AW * i, AW) for i in range(4)]
        pS = [cut(R1 + AW * (4 + i), AW) for i in range(4)]
        pT = [cut(R1 + 8 * AW + 384 * i, 384) for i in range(3)]
        A1 = R1 + 8 * AW + 3 * 384
        amx, anm, als, aes, arv = ([cut(A1 + 32 * i + 16 * j, H) for j in range(2)] for i in range(5))
        Ks = cut(RX, NSAMP, KVH, P)
        Km = cut(RX + 4096, NSAMP, KVH, NMETA)
        Vs = cut(RX + 4608, NSAMP, KVH * HD)
        Vm = cut(RX + 6656, NSAMP, KVH * HD)
        A2 = R1 + 4000
        qs = cut(A2, H, NSAMP)
        sT, sTm, s2, pTs, pTm, oT = (cut(A2 + 128 + 144 * i, 144) for i in range(6))
        scol = cut(A2 + 1000, 8)

        lnr = cut(R1, 5, D)
        h1 = cut(R1 + 5120, NT, D)
        gate = [cut(RQ + 512 * i, 512) for i in range(4)]
        mT = cut(RQ + 2048, KC, NSAMP + NPROMPT)
        wo = cut(RX, KC, D)
        sqj = cut(RQ + 2048, NT, D)
        lg = cut(RY, NT, NG + NE)
        hT = cut(RYA, NT, KC, P)
        ssq, rstd = (small[:, 16 + 20 * i:36 + 20 * i].rearrange("p (t g) -> p t g", g=KVH) for i in range(2))
        lst = [small[:, 56 + 16 * i:68 + 16 * i] for i in range(2)]
        lmv = [small[:, 88 + 4 * i:92 + 4 * i] for i in range(2)]

        at = [RY + NT * (NG + NE)]

        def more(*shape, dtype=F32):
            v = cut(at[0], *shape)
            at[0] += int(np.prod(shape))
            return v if dtype == F32 else v.bitcast(dtype)

        geq, goh = more(NT, NG), more(NT, NG)
        gmx, gix, gws, gw = (more(NT) for _ in range(4))
        ein_g, ein, ein2 = more(NT, NG, EPG), more(NT, EPG), more(NT, EPG)
        eeq = [more(NT, EPG) for _ in range(2)]
        eoh = [more(NT, EPG) for _ in range(2)]
        emx, eix, eno = more(2, NT), more(2, NT), more(2, NT)
        ex = more(NT, NG + 1)
        den = more(NT)
        oh = more(2, NT, NE)
        chosen = cut(at[0], NT * NE // 2).bitcast(BF16)
        at[0] += NT * NE // 2
        cnt = more(NPAIR, 2)
        cpair, extra, obase, ccol, c128 = (more(NPAIR) for _ in range(5))
        over = more(NPAIR, EPG)
        scan = [more(2 * NPAIR) for _ in range(2)]
        odd, tb, tc = more(NPAIR, 2), more(NE), more(NPAIR, 2)
        rank = more(NT, NE)
        pick = [more(2, NT, NE) for _ in range(3)]
        sel = [more(2 * NT) for _ in range(3)]
        far = more(2 * NT)
        thr8 = more(EPG)
        below, thr_g = more(EPG, NPAIR), more(EPG, NPAIR)
        pair, thr = more(NBT), more(NBT)
        mask = more(NBT, 2)
        table = more(2 + 2 * NBT, dtype=I32)
        mcol = more(1, 2)
        assert at[0] <= RYA
        prob = small[:, 96:106].rearrange("p (k t) -> p k t", k=2)
        slot = small[:, 106:116].bitcast(I32)
        zeros = Y[:, NT - 1, :]
        wgu = [cut(RXT + 4096 * u, KC, 2 * DE) for u in range(2)]
        wdn = [cut(RXT + 8192 + 2048 * u, DE // P, D) for u in range(2)]
        X, XT, Yout = cut(RX, D), cut(RX + 1024, KC, P), cut(RX + 2048, D)
        sg = [cut(RX + 3072 + 256 * u, DE) for u in range(2)]
        hid = [cut(RX + 3584 + 256 * u, DE) for u in range(2)]
        hidT = [cut(RX + 4096 + 256 * u, DE // P, P) for u in range(2)]
        G = [cut(RY, NT, D), cut(RYA, NT, D)]

        pb = [ctx.enter_context(nc.psum_tensor(f"bank{i}", [P, 512], F32)) for i in range(8)]

        scr_bc = nc.dram_tensor("scr_bc", (2 * KVH * NSAMP, NST), F32).ap()
        scr_d = nc.dram_tensor("scr_d", (NSAMP, 2 * H), F32).ap()

        scr_x = nc.dram_tensor("scr_x", ((NBT + 1) * P, D), F32).ap()
        scr_y = nc.dram_tensor("scr_y", (NBT * P, D), F32).ap()

        block_pos = [SEQ0 - SEQ0, *(NMETA + P * b for b in range(NBLK))]

        def chunk(c):
            n = NMETA if c == 0 else P
            return slice(3 + block_pos[c], 3 + block_pos[c] + n)

        S = {}
        for name in ("pack_in x_in rope_in cst_in wr_in wvd_in meta_in cache_in "
                     "pool_init bf_dv f_mm f_ev conv_dv silu_ac sconv_dv ssilu_ac rope_dv vd_mm vd_ev "
                     "sp1_dv sp2_ac sp3_dv cs_mm sp4_dv sp5_ac "
                     "tr_mm tr_ev pre_pl cb_mm l_mm l_ac g_dv yd_mm yo_mm st_mm ht_pl h_dv ya_dv yx_pl "
                     "bct_mm bct_ev bcs_out ds_ac ds_out dd_in dcol_dv bcg_in bcg_fr sh_ac sh_dv ysx_dv yst_mm yst_ev "
                     "s_mm s_dv p_ac t_mm td_dv ta_ac pv_mm es_dv es_ac o_dv "
                     "qs_dv ss_mm ss_ev st2_mm sx_dv sp_ac spn_dv pt2_mm pt2_ev spv_mm so_ev sot_mm sya_dv "
                     "wt_in0 wt_in1 ln_in xt_in wo_in c_mm c_ac c_dv rms_ac mt_mm mt_ev w_mm ln_dv lnb_pl ht_mm ht_ev lg_mm lg_dv rms_dv lv_dv lv_ac "
                     "zero_pl zero_out rt1_dv rt_ac ch_dv rk_mm slot_dv tab_dv sc_out "
                     "xs_in xtr_mm xt_a xt_d gu_in0 gu_in1 dn_in0 dn_in1 gu_mm sg_ac hid_dv "
                     "htr_mm hte0 hte1 dn_mm y_a y_d yw_out mc_dv moe_ac "
                     "gt0 gt1 gt2 gt3 gt4 gp_ac o_pl o_out "
                     "small_out out_d dve_chain act_chain pool_chain").split():
            S[name] = sem(name)
        wf_in = [sem(f"wf_in{i}") for i in range(4)]
        hs_in = [sem(f"hs_in{i}") for i in range(3)]
        hs_out = [sem(f"hs_out{i}") for i in range(3)]

        def chained(eng, s):
            done = [0]

            def link(ins):
                done[0] += 1
                ins.then_inc(s, 1)
                eng.wait_ge(s, done[0])
            return link

        def bc(v, n):
            return v.unsqueeze(2).broadcast_to(tuple(v.shape) + (n,))

        block = ctx.enter_context(nc.Block())

        def sp_projection(sp):
            sp.dma_start(pack, io["pack"]).then_inc(S["pack_in"], 16)
            sp.dma_start(xT, io["x_t"]).then_inc(S["x_in"], 16)
            for i in range(FT):
                if i >= 4:
                    sp.wait_ge(S["f_mm"], i - 3)
                sp.dma_start(wf[i % 4], io["w_f"][i]).then_inc(wf_in[i % 4], 16)
                if i == 1:
                    sp.dma_start(cosT, io["rope"][0]).then_inc(S["rope_in"], 16)
                    sp.dma_start(sinT, io["rope"][1]).then_inc(S["rope_in"], 16)
                if i == 3:
                    sp.dma_start(xs4[:, :, 0:CW - 1, :], io["conv_state"]).then_inc(S["cst_in"], 16)
                    sp.dma_start(wvd, io["w_vd"]).then_inc(S["wvd_in"], 16)
                    sp.dma_start(wr, io["w_r"]).then_inc(S["wr_in"], 16)
            sp.wait_ge(S["vd_ev"], NT)
            sp.dma_start(vd[0:NMETA, META, :], vd[NSAMP:PR0, 0, :]).then_inc(S["meta_in"], 16)
            sp.wait_ge(S["zero_pl"], 1)
            sp.dma_start(scr_x.rearrange("(b p) d -> p b d", p=P),
                         zeros.unsqueeze(1).broadcast_to((P, NBT + 1, D))).then_inc(S["zero_out"], 16)
            sp.dma_start(scr_y[NPAIR * P:].rearrange("(b p) d -> p b d", p=P),
                         zeros.unsqueeze(1).broadcast_to((P, NOV, D))).then_inc(S["zero_out"], 16)

        def sp_sample_state(sp):
            for t in range(3):
                sp.dma_start(hst[t], io["state"][t]).then_inc(hs_in[t], 16)
            sp.wait_ge(S["ds_ac"], 1)
            sp.dma_start(scr_d, ds[0:NSAMP, :, :].rearrange("p a h -> p (a h)")).then_inc(S["ds_out"], 16)
            sp.wait_ge(S["ds_out"], 16)
            sp.dma_start(dd, scr_d.rearrange("(o n) h -> o (n h)", o=1).broadcast_to((P, NSAMP * 2 * H))
                         .rearrange("p (n a h) -> p n a h", n=NSAMP, a=2)).then_inc(S["dd_in"], 16)
            sp.wait_ge(S["bct_ev"], 1)
            sp.dma_start(scr_bc, bcs[0:2 * KVH * NSAMP, :]).then_inc(S["bcs_out"], 16)
            sp.wait_ge(S["bcs_out"], 16)
            rows = scr_bc.rearrange("(a g n) s -> a g (n s)", a=2, g=KVH)
            for t in range(KC):
                if t % 2 == 0:
                    g = t // 2
                    if g:
                        sp.wait_ge(S["bcg_fr"], g)
                    for a in range(2):
                        sp.dma_start(bcg[:, a, :, :].rearrange("p n s -> p (n s)"),
                                     rows[a, g:g + 1, :].broadcast_to((P, NSAMP * NST))).then_inc(S["bcg_in"], 16)
                if t >= 3:
                    sp.wait_ge(hs_out[t % 3], 16 * (t // 3))
                    sp.dma_start(hst[t % 3], io["state"][t]).then_inc(hs_in[t % 3], 16)

        def sp_caches(sp):
            sp.wait_ge(S["h_dv"], NBLK + 1)
            sp.wait_ge(S["yo_mm"], 2 * NBLK)
            sp.wait_ge(S["small_out"], 80)
            sp.wait_ge(S["dcol_dv"], 1)
            sp.wait_ge(S["bct_mm"], 1)
            for n in range(NSAMP):
                sp.dma_start(Ks[0:HD, n, :, 0:NWK], io["win_k"][:, n, :, :]).then_inc(S["cache_in"], 16)
            sp.dma_start(Km[0:HD, :, :, :], io["meta_k"]).then_inc(S["cache_in"], 16)
            sp.dma_start(Vs[0:NWK, :, :], io["win_v"]).then_inc(S["cache_in"], 16)
            sp.dma_start(Vm[0:NMETA, :, :], io["meta_v"]).then_inc(S["cache_in"], 16)
            for n in range(NSAMP):
                sp.dma_start(Vs[NWK:P, n, :], vd[n:n + 1, 0, 0:KVH * HD]).then_inc(S["cache_in"], 16)

        def sp_gates(sp):
            for j in range(6):
                if j == 0:
                    sp.wait_ge(S["f_mm"], FT)
                if j == 1:
                    sp.wait_ge(S["vd_mm"], NT)
                if j >= 2:
                    sp.wait_ge(S["c_mm"], NT * (j - 1))
                sp.dma_start(wt[j % 2], io["w_t"][j]).then_inc(S[f"wt_in{j % 2}"], 16)
                if j == 1:
                    sp_residual(sp)
                if j == 2:
                    sp.wait_ge(S["spv_mm"], 1)
                    sp.dma_start(wo, io["w_o"]).then_inc(S["wo_in"], 16)

        def sp_residual(sp):
            sp.wait_ge(S["sot_mm"], 1)
            sp.wait_ge(S["spn_dv"], 1)
            sp.wait_ge(S["o_dv"], NBLK)
            sp.wait_ge(S["ysx_dv"], 1)
            sp.dma_start(lnr.rearrange("p a d -> p (a d)"),
                         io["ln"].rearrange("(o a) d -> o (a d)", o=1).broadcast_to((P, 5 * D))).then_inc(S["ln_in"], 16)
            sp.dma_start(h1[0:NSAMP, 0, :], io["x_tok"][0:NSAMP]).then_inc(S["xt_in"], 16)
            sp.dma_start(h1[:, 1:NT, :], io["x_tok"][NSAMP:].rearrange("(t p) d -> p t d", p=P)).then_inc(S["xt_in"], 16)

        def load_expert(sp, u, e):
            sp.dma_start(wgu[u].rearrange("p (a k) n -> p a k n", a=1),
                         io["w_gu"][bass.ds(e, 1)].rearrange("a p k n -> p a k n")).then_inc(S[f"gu_in{u}"], 16)

        def load_down(sp, u, e):
            sp.dma_start(wdn[u].rearrange("p (a k) n -> p a k n", a=1),
                         io["w_d"][bass.ds(e, 1)].rearrange("a p k n -> p a k n")).then_inc(S[f"dn_in{u}"], 16)

        def load_x(sp, b):
            sp.dma_start(X.rearrange("p (b d) -> p b d", b=1),
                         scr_x.rearrange("(b p) d -> b p d", p=P)[bass.ds(b, 1)].rearrange("b p d -> p b d"))\
              .then_inc(S["xs_in"], 16)

        def sp_experts(sp):
            sp.wait_ge(S["c_mm"], 6 * NT)
            for u in range(2):
                load_expert(sp, u, u)
                load_down(sp, u, u)
            sp.wait_ge(S["sc_out"], 16 * 2 * NT)
            sp.wait_ge(S["w_mm"], NT)
            load_x(sp, 0)
            sp.wait_ge(S["tab_dv"], 1)
            blocks = sp.value_load(table[0:1, 1:2], min_val=NPAIR - 1, max_val=NBT - 1)
            with sp.Fori(0, blocks) as i:
                sp.wait_ge(S["xtr_mm"], i + 1)
                load_x(sp, i + 1)
                for u in range(2):
                    e = sp.value_load(table[0:1, bass.ds(i * 2 + (4 + u), 1)], min_val=0, max_val=NE - 1)
                    sp.wait_ge(S["gu_mm"], i * 2 + (u + 1))
                    load_expert(sp, u, e)
                for u in range(2):
                    e = sp.value_load(table[0:1, bass.ds(i * 2 + (4 + u), 1)], min_val=0, max_val=NE - 1)
                    sp.wait_ge(S["dn_mm"], i * 2 + (u + 1))
                    load_down(sp, u, e)
            sp.wait_ge(S["xtr_mm"], blocks + 1)
            load_x(sp, NBT)

        def sp_outputs(sp):
            for t in range(NT):
                sp.wait_ge(S["o_pl"], t + 1)
                out = io["o_sample"] if t == 0 else io["o_prompt"][P * (t - 1):P * t]
                sp.dma_start(out, h1[0:tile_rows(t), t, :]).then_inc(S["o_out"], 16)
            sp.wait_ge(S["o_out"], 16 * NT)

        def group(pe, out, pairs, last=None):
            for i, (lhsT, rhs) in enumerate(pairs):
                ins = pe.matmul(out, lhsT, rhs, start=(i == 0), stop=(i == len(pairs) - 1))
            if last is not None:
                ins.then_inc(S[last], 1)
            return ins

        def pe_projection(pe):
            pe.wait_ge(S["x_in"], 16)
            for i in range(FT):
                pe.wait_ge(wf_in[i % 4], 16 * (i // 4 + 1))
                if i >= 2:
                    pe.wait_ge(S["f_ev"], i - 1)
                for h in range(2):
                    ins = group(pe, pb[2 * (i % 2) + h][:, 0:HALF],
                                [(wf[i % 4][:, k, :], xT[:, k, h * HALF:(h + 1) * HALF]) for k in range(KC)])
                ins.then_inc(S["f_mm"], 1)
            pe.wait_ge(S["wvd_in"], 16)
            for t in range(NT):
                a, b = tile_cols(t) if t else (0, PR0)
                if t >= 2:
                    pe.wait_ge(S["vd_ev"], t - 1)
                group(pe, pb[4 + t % 2][0:b - a, 0:VD], [(xT[:, k, a:b], wvd[:, k, :]) for k in range(KC)], "vd_mm")

        def pe_decays(pe):
            pe.wait_ge(S["sp3_dv"], 1)
            for t in range(1, NT + 1):
                n = P if t < META else NMETA
                pe.matmul(pb[6][0:n, t * H:(t + 1) * H], upper[0:n, 0:n], adt[0:n, t, :], start=True, stop=True)
                ins = pe.matmul(pb[6][:, (NT + 1 + t) * H:(NT + 2 + t) * H], onesf[0:n, :], adt[0:n, t, :],
                                start=True, stop=True)
            ins.then_inc(S["cs_mm"], 1)

        def pe_ssd(pe):
            pe.wait_ge(S["silu_ac"], XT_TILES)
            pe.wait_ge(S["sp4_dv"], 1)
            pe.wait_ge(S["bf_dv"], 1)
            for c in range(NBLK + 1):
                cols, n = chunk(c), (P if c else NMETA)
                t = c if c else META
                if c:
                    pe.wait_ge(S["h_dv"], c)
                if c >= 2:
                    pe.wait_ge(S["ya_dv"], 2 * (c - 1))
                for k in range(12):
                    ins = pe.transpose(pb[k // 4][0:n, (k % 4) * P:(k % 4) * P + P], xbc[:, k, cols], ident)
                ins.then_inc(S["tr_mm"], 1)
                if c:
                    for g in range(KVH):
                        ins = pe.matmul(pb[3][:, g * P:(g + 1) * P], xbc[:, 8 + g, cols], xbc[:, 12 + g, cols],
                                        start=True, stop=True)
                    ins.then_inc(S["cb_mm"], 1)

                    def decay(g):
                        used = KVH * (c - 1) + g
                        if used >= 2:
                            pe.wait_ge(S["l_ac"], used - 1)
                        out = pb[4 + g % 2]
                        for r in range(QPK):
                            pe.matmul(out[:, r * P:(r + 1) * P], identb, negb, start=True, stop=False)
                            ins = pe.matmul(out[:, r * P:(r + 1) * P],
                                            adt[:, t, QPK * g + r:QPK * g + r + 1].broadcast_to((P, P)), upper,
                                            start=False, stop=True)
                        ins.then_inc(S["l_mm"], 1)

                    def diagonal(g):
                        pe.wait_ge(S["g_dv"], KVH * (c - 1) + g + 1)
                        for r in range(QPK):
                            h = QPK * g + r
                            ins = pe.matmul(pb[6 + g // 2][:, (g % 2) * 256 + r * HD:(g % 2) * 256 + (r + 1) * HD],
                                            LG[g][:, r * P:(r + 1) * P], xd[:, h * HD:(h + 1) * HD],
                                            start=True, stop=True)
                        ins.then_inc(S["yd_mm"], 1)

                    def carried(gp):
                        for g in (2 * gp, 2 * gp + 1):
                            ins = pe.matmul(pb[2 + gp][:, (g % 2) * 256:(g % 2) * 256 + 256], xbc[:, 12 + g, cols],
                                            Hs[:, g * 256:(g + 1) * 256], start=True, stop=True)
                        ins.then_inc(S["yo_mm"], 1)

                    decay(0)
                    decay(1)
                    pe.wait_ge(S["tr_ev"], c + 1)
                    carried(0)
                    decay(2)
                    pe.wait_ge(S["pre_pl"], c + 1)
                    diagonal(0)
                    decay(3)
                    diagonal(1)
                    diagonal(2)
                    diagonal(3)
                    carried(1)
                else:
                    pe.wait_ge(S["tr_ev"], 1)
                pe.wait_ge(S["pre_pl"], c + 1)
                for g in range(KVH):
                    ins = pe.matmul(pb[g // 2][:, (g % 2) * 256:(g % 2) * 256 + 256],
                                    Bt[0:n, g * P:(g + 1) * P], xdd[0:n, g * 256:(g + 1) * 256],
                                    start=True, stop=True)
                ins.then_inc(S["st_mm"], 1)

        def pe_sample_bc(pe):
            pe.wait_ge(S["ssilu_ac"], 1)
            pe.wait_ge(S["ya_dv"], 2 * NBLK)
            pe.transpose(pb[3][0:64, 0:P], xcs[:, 8:16, :].rearrange("p a n -> p (a n)"), ident).then_inc(S["bct_mm"], 1)

        def pe_sample_y(pe):
            pe.wait_ge(S["ysx_dv"], 1)
            pe.wait_ge(S["bct_ev"], 1)
            pe.wait_ge(S["h_dv"], NBLK + 1)
            for t in range(KC):
                ins = pe.transpose(pb[t // 4][0:NSAMP, (t % 4) * P:(t % 4) * P + P], ys[:, t, :], ident)
            ins.then_inc(S["yst_mm"], 1)

        def pe_attention(pe):
            pe.wait_ge(S["rope_dv"], QT_TILES + KT_TILES)
            pe.wait_ge(S["meta_in"], 16)
            pe.wait_ge(S["yst_ev"], 1)
            n_all = NBLK * H

            def scores(i):
                b, h = divmod(i, H)
                g, r0 = h // QPK, HD * (h % 2)
                q = qT[r0:r0 + HD, h // 2, PR0 + P * b:PR0 + P * (b + 1)]
                key = kd[r0:r0 + HD, g, :]
                if i >= 3:
                    pe.wait_ge(S["s_dv"], i - 2)
                out = pb[i % 3]
                if b == 0:
                    ins = pe.matmul(out[:, P:AW], q, key[:, SEQ0:PR0 + P], start=True, stop=True)
                else:
                    pe.matmul(out[:, 0:P], q, key[:, PR0 + P * (b - 1):PR0 + P * b], start=True, stop=True)
                    pe.matmul(out[:, P:P + NMETA], q, key[:, SEQ0:PR0], start=True, stop=True)
                    ins = pe.matmul(out[:, P + NMETA:AW], q, key[:, PR0 + P * b:PR0 + P * (b + 1)],
                                    start=True, stop=True)
                ins.then_inc(S["s_mm"], 1)

            def turn(i):
                b = i // H
                pe.wait_ge(S["p_ac"], i + 1)
                if i >= 3:
                    j = i - 3
                    pe.wait_ge(S["td_dv" if j % 2 == 0 else "ta_ac"], j // 2 + 1)
                out, pr = pb[3 + i % 3], pS[i % 4]
                if b:
                    pe.transpose(out[:, 0:P], pr[:, 0:P], ident)
                pe.transpose(out[0:NMETA, 2 * P:3 * P], pr[:, P:P + NMETA], ident)
                pe.transpose(out[:, P:2 * P], pr[:, P + NMETA:AW], ident).then_inc(S["t_mm"], 1)

            def values(i):
                b, h = divmod(i, H)
                g, t = h // QPK, b + 1
                pe.wait_ge(S["td_dv" if i % 2 == 0 else "ta_ac"], i // 2 + 1)
                if h == 0 and b:
                    pe.wait_ge(S["o_dv"], b)
                v = slice(g * HD, (g + 1) * HD)
                w = pT[i % 3]
                terms = [(w[:, P:2 * P], vd[:, t, v]), (w[0:NMETA, 2 * P:3 * P], vd[0:NMETA, META, v])]
                if b:
                    terms.insert(0, (w[:, 0:P], vd[:, t - 1, v]))
                group(pe, pb[6 + h // 8][:, (h % 8) * HD:(h % 8 + 1) * HD], terms, "pv_mm")

            for i in range(n_all + 4):
                if i < n_all:
                    scores(i)
                if 2 <= i < n_all + 2:
                    turn(i - 2)
                if i >= 4:
                    values(i - 4)

        def pe_sample_attention(pe):
            pe.wait_ge(S["qs_dv"], 1)
            pe.wait_ge(S["cache_in"], 16 * (2 * NSAMP + 3))
            pe.wait_ge(S["o_dv"], NBLK)
            for n in range(NSAMP):
                for g in range(KVH):
                    c = slice(n * H + QPK * g, n * H + QPK * (g + 1))
                    q = qs[0:HD, QPK * g:QPK * (g + 1), n]
                    pe.matmul(pb[0][:, c], Ks[0:HD, n, g, :], q, start=True, stop=True)
                    ins = pe.matmul(pb[1][0:NMETA, c], Km[0:HD, n, g, :], q, start=True, stop=True)
            ins.then_inc(S["ss_mm"], 1)
            pe.wait_ge(S["ss_ev"], 1)
            pe.transpose(pb[2][:, 0:P], sT[:, 0:P], ident)
            pe.transpose(pb[2][:, P:P + NMETA], sTm[0:NMETA, 0:P], ident[0:NMETA, 0:NMETA]).then_inc(S["st2_mm"], 1)
            pe.wait_ge(S["spn_dv"], 1)
            pe.transpose(pb[0][:, 0:P], s2[:, 0:P], ident)
            pe.transpose(pb[0][0:NMETA, P:2 * P], s2[:, P:P + NMETA], ident).then_inc(S["pt2_mm"], 1)
            pe.wait_ge(S["pt2_ev"], 1)
            pe.wait_ge(S["cache_in"], 16 * (2 * NSAMP + 3))
            for n in range(NSAMP):
                for g in range(KVH):
                    c = slice(n * H + QPK * g, n * H + QPK * (g + 1))
                    v = slice(g * HD, (g + 1) * HD)
                    ins = group(pe, pb[1][0:HD, c], [(Vs[:, n, v], pTs[:, c]), (Vm[0:NMETA, n, v], pTm[0:NMETA, c])])
            ins.then_inc(S["spv_mm"], 1)
            pe.wait_ge(S["so_ev"], 1)
            for h in range(H):
                ins = pe.transpose(pb[2 + h // 8][0:NSAMP, (h % 8) * HD:(h % 8 + 1) * HD], oT[0:HD, h:P:H],
                                   ident[0:HD, 0:HD])
            ins.then_inc(S["sot_mm"], 1)

        def pe_gates(pe):
            pe.wait_ge(S["o_dv"], NBLK)
            for j in range(6):
                pe.wait_ge(S[f"wt_in{j % 2}"], 16 * (j // 2 + 1))
                for t in range(NT):
                    i = j * NT + t
                    a, b = tile_cols(t)
                    if i >= 4:
                        pe.wait_ge(S["c_ac"], i - 3)
                    group(pe, pb[4 + i % 4][0:b - a, :], [(xT[:, k, a:b], wt[j % 2][:, k, :]) for k in range(KC)],
                          "c_mm")

        def pe_mix(pe):
            pe.wait_ge(S["sya_dv"], 1)
            pe.wait_ge(S["c_ac"], 6 * NT)

            def turn_merged(t):
                r = tile_rows(t)
                pe.wait_ge(S["c_dv"], 5 * NT + t + 1)
                if t:
                    pe.wait_ge(S["mt_ev"], t)
                for k in range(KC):
                    ins = pe.transpose(pb[k // 4][:, (k % 4) * P:(k % 4) * P + r], Y[0:r, t, k * P:(k + 1) * P],
                                       ident[0:r, 0:r])
                ins.then_inc(S["mt_mm"], 1)

            def mix(t):
                r, (a, b) = tile_rows(t), row_cols(t)
                pe.wait_ge(S["mt_ev"], t + 1)
                if t >= 2:
                    pe.wait_ge(S["lnb_pl"], t - 1)
                for n in range(2):
                    ins = group(pe, pb[2 + 2 * (t % 2) + n][0:r, :],
                                [(mT[:, k, a:b], wo[:, k, n * 512:(n + 1) * 512]) for k in range(KC)])
                ins.then_inc(S["w_mm"], 1)

            def turn_h1(t):
                r = tile_rows(t)
                pe.wait_ge(S["lnb_pl"], t + 1)
                if t:
                    pe.wait_ge(S["ht_ev"], t)
                else:
                    pe.wait_ge(S["mt_ev"], NT)
                for k in range(KC):
                    ins = pe.transpose(pb[k // 4][:, (k % 4) * P:(k % 4) * P + r], h1[0:r, t, k * P:(k + 1) * P],
                                       ident[0:r, 0:r])
                ins.then_inc(S["ht_mm"], 1)

            def logits(t):
                r = tile_rows(t)
                pe.wait_ge(S["ht_ev"], t + 1)
                if t >= 2:
                    pe.wait_ge(S["lg_dv"], t - 1)
                group(pe, pb[6 + t % 2][0:r, 0:NG + NE], [(hT[:, t, k, 0:r], wr[:, k, :]) for k in range(KC)], "lg_mm")

            pe.wait_ge(S["wo_in"], 16)
            pe.wait_ge(S["wr_in"], 16)
            turn_merged(0)
            turn_merged(1)
            mix(0)
            turn_merged(2)
            mix(1)
            turn_merged(3)
            mix(2)
            turn_merged(4)
            mix(3)
            turn_h1(0)
            turn_h1(1)
            logits(0)
            mix(4)
            turn_h1(2)
            logits(1)
            turn_h1(3)
            logits(2)
            turn_h1(4)
            logits(3)
            logits(4)

        def pe_rank(pe):
            pe.wait_ge(S["ch_dv"], 1)
            pe.wait_ge(S["lg_dv"], NT)
            m = [chosen[:, t * NE:(t + 1) * NE] for t in range(NT)]
            for t in range(NT):
                group(pe, pb[6][:, t * NE:(t + 1) * NE], [(strictb, m[t])] + [(onesb, m[s]) for s in range(t)])
            group(pe, pb[6][:, NT * NE:(NT + 1) * NE], [(onesb, m[s]) for s in range(NT)], "rk_mm")

        def pe_experts(pe):

            def turn_x():
                for k in range(KC):
                    ins = pe.transpose(pb[k // 4][:, (k % 4) * P:(k % 4 + 1) * P], X[:, k * P:(k + 1) * P], ident)
                ins.then_inc(S["xtr_mm"], 1)

            def turn_hidden(u):
                for k in range(DE // P):
                    ins = pe.transpose(pb[4 + u][:, k * P:(k + 1) * P], hid[u][:, k * P:(k + 1) * P], ident)
                ins.then_inc(S["htr_mm"], 1)

            def gate_up(u, ks):
                for k in ks:
                    ins = pe.matmul(pb[2 + u][:, :], XT[:, k, :], wgu[u][:, k, :], start=(k == 0), stop=(k == KC - 1))
                if k == KC - 1:
                    ins.then_inc(S["gu_mm"], 1)

            def down(u):
                last = DE // P - 1
                for k in range(DE // P):
                    for n in range(2):
                        ins = pe.matmul(pb[6 + n][:, :], hidT[u][:, k, :], wdn[u][:, k, n * 512:(n + 1) * 512],
                                        start=(u == 0 and k == 0), stop=(u == 1 and k == last))
                ins.then_inc(S["dn_mm"], 1)

            pe.wait_ge(S["xs_in"], 16)
            pe.wait_ge(S["ht_ev"], NT)
            turn_x()
            pe.wait_ge(S["slot_dv"], 1)
            pe.wait_ge(S["tab_dv"], 1)
            blocks = pe.value_load(table[0:1, 0:1], min_val=NPAIR, max_val=NBT)
            with pe.Fori(0, blocks) as i:
                pe.wait_ge(S["xt_a"], i + 1)
                pe.wait_ge(S["xt_d"], i + 1)
                pe.wait_ge(S["gu_in0"], i * 16 + 16)
                gate_up(0, range(KC))
                pe.wait_ge(S["gu_in1"], i * 16 + 16)
                gate_up(1, range(KC // 2))
                pe.wait_ge(S["hid_dv"], i * 2 + 1)
                turn_hidden(0)
                gate_up(1, range(KC // 2, KC))
                pe.wait_ge(S["hte0"], i + 1)
                pe.wait_ge(S["dn_in0"], i * 16 + 16)
                down(0)
                pe.wait_ge(S["hid_dv"], i * 2 + 2)
                turn_hidden(1)
                pe.wait_ge(S["xs_in"], i * 16 + 32)
                turn_x()
                pe.wait_ge(S["hte1"], i + 1)
                pe.wait_ge(S["dn_in1"], i * 16 + 16)
                down(1)

        act_link = []

        def act_projection(act):
            act.wait_ge(S["pool_init"], 3)
            act.wait_ge(S["cst_in"], 16)
            for i in range(FT + 1):
                if i < FT:
                    act.wait_ge(S["f_mm"], i + 1)
                    lo, hi = pb[2 * (i % 2)], pb[2 * (i % 2) + 1]
                    if i < XT_TILES:
                        act.copy(xs4[:, i, CW - 1, :], lo[:, 0:NSAMP])
                        act.copy(xbc[:, i, 3:3 + HALF - SEQ0], lo[:, SEQ0:HALF])
                        act.copy(xbc[:, i, 3 + HALF - SEQ0:3 + NSEQ], hi[:, 0:HALF]).then_inc(S["f_ev"], 1)
                    else:
                        j = i - XT_TILES
                        if j >= 2:
                            act.wait_ge(S["rope_dv"], j - 1)
                        act.copy(raw[j % 2][:, 0:HALF], lo[:, 0:HALF])
                        act.copy(raw[j % 2][:, HALF:NTOK], hi[:, 0:HALF]).then_inc(S["f_ev"], 1)
                if 1 <= i <= XT_TILES:
                    act.wait_ge(S["conv_dv"], i)
                    act.activation(xbc[:, i - 1, 3:3 + NSEQ], acc[(i - 1) % 2], ACT.Silu).then_inc(S["silu_ac"], 1)
                if i == XT_TILES + 1:
                    act.wait_ge(S["sconv_dv"], 1)
                    act.activation(xcs[:, :, :], acc_s[:, :, :], ACT.Silu).then_inc(S["ssilu_ac"], 1)
            for t in range(NT):
                n = P if t else PR0
                act.wait_ge(S["vd_mm"], t + 1)
                act.copy(vd[0:n, t, :], pb[4 + t % 2][0:n, 0:VD]).then_inc(S["vd_ev"], 1)

        def act_decays(act):
            link = act_link[0]
            act.wait_ge(S["sp1_dv"], 1)
            link(act.activation(dex[:, :, :], dab[:, :, :], ACT.Exp, scale=-1.0))
            act.activation(dex[:, :, :], dex[:, :, :], ACT.Ln, bias=1.0).then_inc(S["sp2_ac"], 1)
            act.activation(small[:, 0:H], pk("a_log"), ACT.Exp).then_inc(S["sp2_ac"], 1)
            act.wait_ge(S["sp3_dv"], 1)
            act.activation(ds[0:NSAMP, 0, :], adt[0:NSAMP, 0, :], ACT.Exp)
            act.copy(ds[0:NSAMP, 1, :], dt[0:NSAMP, 0, :]).then_inc(S["ds_ac"], 1)
            act.wait_ge(S["sp4_dv"], 1)
            act.activation(ecs[:, 1:NT, :], ncs[:, 1:NT, :], ACT.Exp, scale=-1.0)
            act.activation(dst[:, 1:NT, :], tmc[:, 1:NT, :], ACT.Exp)
            act.activation(dst[0:NMETA, META, :], tmc[0:NMETA, META, :], ACT.Exp)
            act.activation(etot[:, 1:NT + 1, :], tot[:, 1:NT + 1, :], ACT.Exp).then_inc(S["sp5_ac"], 1)

        def act_ssd(act):
            act.wait_ge(S["rope_dv"], QT_TILES + KT_TILES)
            for c in range(NBLK + 1):
                n = P if c else NMETA
                act.wait_ge(S["tr_mm"], c + 1)
                if c:
                    act.wait_ge(S["pre_pl"], c)
                    act.wait_ge(S["st_mm"], c)
                act.copy(xt[0:n, 0:512], pb[0][0:n, :])
                act.copy(xt[0:n, 512:1024], pb[1][0:n, :])
                act.copy(Bt[0:n, :], pb[2][0:n, :]).then_inc(S["tr_ev"], 1)
                if c:
                    for g in range(KVH):
                        act.wait_ge(S["l_mm"], KVH * (c - 1) + g + 1)
                        for r in range(QPK):
                            h = QPK * g + r
                            ins = act.activation(LG[g][:, r * P:(r + 1) * P], pb[4 + g % 2][:, r * P:(r + 1) * P],
                                                 ACT.Exp, bias=ncs[:, c, h:h + 1])
                        ins.then_inc(S["l_ac"], 1)

        def act_sample_state(act):
            act.wait_ge(S["bct_mm"], 1)
            act.copy(bcs[0:64, :], pb[3][0:64, 0:P]).then_inc(S["bct_ev"], 1)
            act.wait_ge(S["dcol_dv"], 1)
            for t in range(KC):
                act.wait_ge(hs_in[t % 3], 16 * (t // 3 + 1))
                for n in range(NSAMP):
                    ins = act.activation(hst[t % 3][:, n, :], hst[t % 3][:, n, :], ACT.Copy, scale=dcol[:, t, n:n + 1])
                ins.then_inc(S["sh_ac"], 1)
            act.wait_ge(S["yst_mm"], 1)
            act.copy(Y[0:NSAMP, 0, 0:512], pb[0][0:NSAMP, :])
            act.copy(Y[0:NSAMP, 0, 512:1024], pb[1][0:NSAMP, :]).then_inc(S["yst_ev"], 1)

        def act_attention(act):
            n_all = NBLK * H
            for i in range(n_all + 5):
                if i < n_all:
                    b, h = divmod(i, H)
                    lo = 0 if b else P
                    act.wait_ge(S["s_dv"], i + 1)
                    if i >= 4:
                        act.wait_ge(S["t_mm"], i - 3)
                    act.activation(pS[i % 4][:, lo:AW], sS[i % 4][:, lo:AW], ACT.Exp, bias=anm[b % 2][:, h:h + 1],
                                   accum_out=als[b % 2][:, h:h + 1]).then_inc(S["p_ac"], 1)
                j = i - 2
                if 0 <= j < n_all and j % 2:
                    act.wait_ge(S["t_mm"], j + 1)
                    if j >= 3:
                        act.wait_ge(S["pv_mm"], j - 2)
                    lo = 0 if j >= H else P
                    act.copy(pT[j % 3][0:NMETA, 2 * P:3 * P], pb[3 + j % 3][0:NMETA, 2 * P:3 * P])
                    act.copy(pT[j % 3][:, lo:2 * P], pb[3 + j % 3][:, lo:2 * P]).then_inc(S["ta_ac"], 1)
                if i % H == 3 and i > 3:
                    b = i // H - 1
                    act.wait_ge(S["es_dv"], b + 1)
                    act.activation(aes[b % 2], aes[b % 2], ACT.Exp).then_inc(S["es_ac"], 1)

        def act_sample_attention(act):
            link = act_link[0]
            act.wait_ge(S["sx_dv"], 1)
            act.activation(s2[:, 0:P + NMETA], s2[:, 0:P + NMETA], ACT.Exp, bias=scol[:, 1:2], accum_out=scol[:, 2:3])
            act.activation(scol[:, 3:4], pk("sink_col"), ACT.Exp, bias=scol[:, 1:2]).then_inc(S["sp_ac"], 1)
            act.wait_ge(S["pt2_mm"], 1)
            act.copy(pTs[:, 0:P], pb[0][:, 0:P])
            act.copy(pTm[0:NMETA, 0:P], pb[0][0:NMETA, P:2 * P]).then_inc(S["pt2_ev"], 1)
            act.wait_ge(S["spv_mm"], 1)
            act.copy(oT[0:HD, 0:P], pb[1][0:HD, 0:P]).then_inc(S["so_ev"], 1)

        def act_gates(act):
            act.wait_ge(S["qs_dv"], 1)
            act.wait_ge(S["small_out"], 80)
            act.wait_ge(S["cache_in"], 16 * (2 * NSAMP + 3))
            act.wait_ge(S["o_dv"], NBLK)
            for i in range(6 * NT):
                j, t = divmod(i, NT)
                r = tile_rows(t)
                act.wait_ge(S["c_mm"], i + 1)
                if i >= 4:
                    act.wait_ge(S["c_dv"], i - 3)
                act.activation(gate[i % 4][0:r, :], pb[4 + i % 4][0:r, :], ACT.Silu if j < 2 else ACT.Sigmoid)\
                   .then_inc(S["c_ac"], 1)
                if i == 2 * NT - 1:
                    act_rms(act)

        def act_rms(act):
            act.wait_ge(S["c_dv"], 2 * NT)
            for t in range(NT):
                r = tile_rows(t)
                for g in range(KVH):
                    ins = act.activation(sqj[0:r, t, g * 256:(g + 1) * 256], Y[0:r, t, g * 256:(g + 1) * 256], ACT.Square, accum_out=ssq[0:r, t, g:g + 1])
            ins.then_inc(S["rms_ac"], 1)
            act.wait_ge(S["rms_dv"], 1)
            act.activation(rstd[:, :, :], rstd[:, :, :], ACT.Sqrt).then_inc(S["rms_ac"], 1)

        def act_root(act, n):
            r, mv = tile_rows((n - 1) % NT), lmv[(n - 1) % 2]
            act.wait_ge(S["lv_dv"], n)
            act.activation(mv[0:r, 2:3], mv[0:r, 2:3], ACT.Sqrt).then_inc(S["lv_ac"], 1)

        def act_mix(act):
            act.wait_ge(S["c_dv"], 6 * NT)
            def empty(t, src, dst, done):
                r = tile_rows(t)
                act.wait_ge(S[src], t + 1)
                for n in range(2):
                    ins = act.copy(dst(n), pb[n][:, :].rearrange("p (k c) -> p k c", c=P)[:, :, 0:r])
                ins.then_inc(S[done], 1)

            def merged(t):
                a, b = row_cols(t)
                empty(t, "mt_mm", lambda n: mT[:, 4 * n:4 * n + 4, a:b], "mt_ev")

            def first(t):
                empty(t, "ht_mm", lambda n: hT[:, t, 4 * n:4 * n + 4, 0:tile_rows(t)], "ht_ev")

            for t in range(3):
                merged(t)
            act_root(act, 1)
            merged(3)
            act_root(act, 2)
            merged(4)
            act_root(act, 3)
            first(0)
            act_root(act, 4)
            first(1)
            first(2)
            act_root(act, 5)
            first(3)
            first(4)

        def act_route(act):
            act.wait_ge(S["rt1_dv"], 1)
            act.activation(ex[:, :, :], ex[:, :, :], ACT.Exp).then_inc(S["rt_ac"], 1)

        def act_experts(act):

            def empty_x():
                act.copy(XT[:, 0:4, :].rearrange("p k c -> p (k c)"), pb[0][:, :]).then_inc(S["xt_a"], 1)

            act.sem_inc(S["yw_out"], 16)
            act.wait_ge(S["xtr_mm"], 1)
            empty_x()
            act.wait_ge(S["tab_dv"], 1)
            blocks = act.value_load(table[0:1, 0:1], min_val=NPAIR, max_val=NBT)
            with act.Fori(0, blocks) as i:
                for u in range(2):
                    act.wait_ge(S["gu_mm"], i * 2 + (u + 1))
                    act.activation(sg[u], pb[2 + u][:, 0:DE], ACT.Silu).then_inc(S["sg_ac"], 1)
                    if u == 0:
                        act.wait_ge(S["htr_mm"], i * 2 + 1)
                        act.copy(hidT[0][:, :, :].rearrange("p k c -> p (k c)"), pb[4][:, 0:DE]).then_inc(S["hte0"], 1)
                act.wait_ge(S["xtr_mm"], i + 2)
                empty_x()
                act.wait_ge(S["dn_mm"], i * 2 + 2)
                act.wait_ge(S["yw_out"], i * 16 + 16)
                act.copy(Yout[:, 0:512], pb[6][:, :]).then_inc(S["y_a"], 1)
                act.wait_ge(S["y_a"], i + 1)
                act.wait_ge(S["y_d"], i + 1)
                act.dma_start(scr_y.rearrange("(b p) d -> b p d", p=P)[bass.ds(i, 1)].rearrange("b p d -> p b d"),
                              Yout.rearrange("p (b d) -> p b d", b=1)).then_inc(S["yw_out"], 16)
            act.wait_ge(S["yw_out"], blocks * 16 + 16)
            act.copy(small[:, 120:121], small[:, 0:1]).then_inc(S["moe_ac"], 1)

        def act_final(act):
            for t in range(NT + 1):
                if t < NT:
                    r = tile_rows(t)
                    act.wait_ge(S[f"gt{t}"], 32)
                    act.activation(G[0][0:r, t, :], G[0][0:r, t, :], ACT.Copy, scale=prob[0:r, 0, t:t + 1])\
                       .then_inc(S["gp_ac"], 1)
                if t:
                    act_root(act, NT + t)

        dve_link = []
        pool_link = []

        def dve_projection(v):
            link = dve_link[0]
            cw, cb = pk("conv_w"), pk("conv_b")
            v.wait_ge(S["pack_in"], 16)
            for j, name in enumerate(("ident", "neg", "strict", "ones")):
                ins = v.tensor_copy(bfc[:, j, :], pk(name))
            ins.then_inc(S["bf_dv"], 1)
            for i in range(XT_TILES):
                v.wait_ge(S["f_ev"], i + 1)
                if i >= 2:
                    v.wait_ge(S["silu_ac"], i - 1)
                v.tensor_copy(pconv[:, i, :], xbc[:, i, NSEQ:NSEQ + 3])
                a = acc[i % 2]
                link(v.tensor_scalar(a, xbc[:, i, 3:3 + NSEQ], cw[:, i * CW + 3:i * CW + 4], cb[:, i:i + 1],
                                     ALU.mult, ALU.add))
                for j in (0, 1):
                    link(v.scalar_tensor_tensor(a, xbc[:, i, j:j + NSEQ], cw[:, i * CW + j:i * CW + j + 1], a,
                                                ALU.mult, ALU.add))
                v.scalar_tensor_tensor(a, xbc[:, i, 2:2 + NSEQ], cw[:, i * CW + 2:i * CW + 3], a,
                                       ALU.mult, ALU.add).then_inc(S["conv_dv"], 1)
            v.wait_ge(S["cst_in"], 16)
            cwv = cw.rearrange("p (i j) -> p i j", j=CW)
            for j in range(CW):
                o = acc_s if j == 0 else tmp_s
                link(v.tensor_tensor(o[:, :, :], xs4[:, :, j, :], bc(cwv[:, :, j], NSAMP), ALU.mult))
                if j:
                    link(v.tensor_tensor(acc_s[:, :, :], acc_s[:, :, :], tmp_s[:, :, :], ALU.add))
            v.tensor_tensor(acc_s[:, :, :], acc_s[:, :, :], bc(cb, NSAMP), ALU.add).then_inc(S["sconv_dv"], 1)
            v.wait_ge(S["rope_in"], 32)
            for j in range(QT_TILES + KT_TILES):
                v.wait_ge(S["f_ev"], XT_TILES + j + 1)
                r = raw[j % 2]
                if j:
                    v.wait_ge(S["rope_dv"], j)
                for q in range(4):
                    o = q ^ 1
                    v.tensor_tensor(swp[32 * o:32 * o + 32, :], r[32 * q:32 * q + 32, :], sinT[32 * q:32 * q + 32, :],
                                    ALU.mult)
                link(v.tensor_tensor(rcs, r, cosT, ALU.mult))
                if j < QT_TILES:
                    v.tensor_tensor(qT[:, j, :], rcs, swp, ALU.add).then_inc(S["rope_dv"], 1)
                else:
                    for half in range(2):
                        g = 2 * (j - QT_TILES) + half
                        src = slice(64 * half, 64 * half + 64)
                        for dstp in range(2):
                            ins = v.tensor_tensor(kd[64 * dstp:64 * dstp + 64, g, :], rcs[src, :], swp[src, :], ALU.add)
                    ins.then_inc(S["rope_dv"], 1)

        def dve_decays(v):
            link = dve_link[0]
            v.wait_ge(S["vd_ev"], NT)
            v.wait_ge(S["meta_in"], 16)
            bias = pk("dt_bias").unsqueeze(1).broadcast_to((P, NT + 1, H))
            link(v.tensor_tensor(dtx[:, :, :], vd[:, :, KVH * HD:VD], bias, ALU.add))
            v.scalar_tensor_tensor(dab[:, :, :], dtx[:, :, :], -1.0, dtx[:, :, :], ALU.mult, ALU.max)\
             .then_inc(S["sp1_dv"], 1)
            v.wait_ge(S["sp2_ac"], 2)
            link(v.scalar_tensor_tensor(dt[:, :, :], dtx[:, :, :], 0.0, dex[:, :, :], ALU.max, ALU.add))
            v.scalar_tensor_tensor(adt[:, :, :], dt[:, :, :], -1.0,
                                   small[:, 0:H].unsqueeze(1).broadcast_to((P, NT + 1, H)), ALU.mult, ALU.mult)\
             .then_inc(S["sp3_dv"], 1)
            v.wait_ge(S["cs_mm"], 1)
            cs = pb[6][:, 0:(NT + 1) * H].rearrange("p (t h) -> p t h", h=H)
            total = pb[6][:, (NT + 1) * H:2 * (NT + 1) * H].rearrange("p (t h) -> p t h", h=H)
            v.tensor_scalar(ncs[:, 1:NT, :], cs[:, 1:NT, :], -1.0, None, ALU.mult)
            v.tensor_scalar(ncs[0:NMETA, META, :], cs[0:NMETA, META, :], -1.0, None, ALU.mult)
            link(v.tensor_copy(tot[:, 1:NT + 1, :], total[:, 1:NT + 1, :]))
            v.tensor_tensor(tmc[0:NMETA, META, :], tot[0:NMETA, META, :], ncs[0:NMETA, META, :], ALU.add)
            v.tensor_tensor(tmc[:, 1:NT, :], tot[:, 1:NT, :], ncs[:, 1:NT, :], ALU.add).then_inc(S["sp4_dv"], 1)

        def dve_ssd(v):
            link = dve_link[0]
            v.wait_ge(S["sp5_ac"], 1)
            for c in range(NBLK + 1):
                if c == NBLK:
                    v.wait_ge(S["zero_out"], 32)
                if c:
                    v.wait_ge(S["cb_mm"], c)
                    for g in range(KVH):
                        v.wait_ge(S["l_ac"], KVH * (c - 1) + g + 1)
                        o = LG[g].rearrange("p (r l) -> p r l", r=QPK)
                        v.tensor_tensor(o, o, pb[3][:, g * P:(g + 1) * P].unsqueeze(1).broadcast_to((P, QPK, P)),
                                        ALU.mult).then_inc(S["g_dv"], 1)
                    for gp in range(2):
                        y = Y[:, c, 512 * gp:512 * (gp + 1)]
                        v.wait_ge(S["yo_mm"], 2 * (c - 1) + gp + 1)
                        link(v.tensor_tensor(y.rearrange("p (h d) -> p h d", d=HD),
                                             pb[2 + gp][:, :].rearrange("p (h d) -> p h d", d=HD),
                                             bc(ecs[:, c, 8 * gp:8 * (gp + 1)], HD), ALU.mult))
                        v.wait_ge(S["yd_mm"], KVH * (c - 1) + 2 * gp + 2)
                        v.tensor_tensor(y, y, pb[6 + gp][:, :], ALU.add).then_inc(S["ya_dv"], 1)
                v.wait_ge(S["st_mm"], c + 1)
                if c:
                    v.wait_ge(S["ht_pl"], c)
                for i in range(2):
                    s = slice(512 * i, 512 * (i + 1))
                    if c:
                        ins = v.tensor_tensor(Hs[:, s], Ht[:, s], pb[i][:, :], ALU.add)
                    else:
                        ins = v.tensor_copy(Hs[:, s], pb[i][:, :])
                ins.then_inc(S["h_dv"], 1)

        def dve_sample_state(v):
            link = dve_link[0]
            v.wait_ge(S["dd_in"], 16)
            for hh in range(2):
                rows = slice(64 * hh, 64 * hh + 64)
                for a, o in ((0, dcol), (1, dtcol)):
                    ins = v.tensor_copy(o[rows, :, :].rearrange("p t n -> p n t"), dd[rows, :, a, hh:H:2])
            link(ins)
            link(v.tensor_tensor(xdt[:, :, :], xcs[:, 0:KC, :], dtcol[:, :, :], ALU.mult))
            v.tensor_tensor(dtcol[:, :, :], xcs[:, 0:KC, :], bc(pk("d_col"), NSAMP), ALU.mult)\
             .then_inc(S["dcol_dv"], 1)
            for t in range(KC):
                if t % 2 == 0:
                    v.wait_ge(S["bcg_in"], 32 * (t // 2 + 1))
                v.wait_ge(S["sh_ac"], t + 1)
                h = hst[t % 3]
                for n in range(NSAMP):
                    ins = v.scalar_tensor_tensor(h[:, n, :], bcg[:, 0, n, :], xdt[:, t, n:n + 1], h[:, n, :],
                                                 ALU.mult, ALU.add)
                ins.then_inc(S["sh_dv"], 1)
                v.wait_ge(S["sh_dv"], t + 1)
                for n in range(NSAMP):
                    ins = v.tensor_tensor_reduce(junk[:, n, :], h[:, n, :], bcg[:, 1, n, :], 1.0, 0.0, ALU.mult, ALU.add,
                                                 ys[:, t, n:n + 1])
                if t % 2:
                    ins.then_inc(S["bcg_fr"], 1)
            v.wait_ge(S["bcg_fr"], KC // 2)
            v.tensor_tensor(ys[:, :, :], ys[:, :, :], dtcol[:, :, :], ALU.add).then_inc(S["ysx_dv"], 1)

        def dve_attention(v):
            link = dve_link[0]
            mask = pk("amask")
            n_all = NBLK * H
            v.wait_ge(S["st_mm"], NBLK + 1)
            v.wait_ge(S["out_d"], 16)
            v.wait_ge(S["pre_pl"], NBLK + 1)
            v.wait_ge(S["yx_pl"], NBLK)
            for i in range(n_all + 5):
                if i < n_all:
                    b, h = divmod(i, H)
                    lo = 0 if b else P
                    v.wait_ge(S["s_mm"], i + 1)
                    if i >= 4:
                        v.wait_ge(S["p_ac"], i - 3)
                    if h == 0 and b >= 2:
                        v.wait_ge(S["es_ac"], b - 1)
                    link(v.tensor_tensor_reduce(sS[i % 4][:, lo:AW], pb[i % 3][:, lo:AW], mask[:, lo:AW], SCALE,
                                                pk("sinks")[:, h:h + 1], ALU.add, ALU.max, amx[b % 2][:, h:h + 1]))
                    v.tensor_scalar(anm[b % 2][:, h:h + 1], amx[b % 2][:, h:h + 1], -1.0, None, ALU.mult)\
                     .then_inc(S["s_dv"], 1)
                j = i - 2
                if 0 <= j < n_all and j % 2 == 0:
                    v.wait_ge(S["t_mm"], j + 1)
                    if j >= 3:
                        v.wait_ge(S["pv_mm"], j - 2)
                    lo = 0 if j >= H else P
                    v.tensor_copy(pT[j % 3][0:NMETA, 2 * P:3 * P], pb[3 + j % 3][0:NMETA, 2 * P:3 * P])
                    v.tensor_copy(pT[j % 3][:, lo:2 * P], pb[3 + j % 3][:, lo:2 * P]).then_inc(S["td_dv"], 1)
                if i % H == 2 and i > 2:
                    b = i // H - 1
                    v.wait_ge(S["s_dv"], H * (b + 1))
                    v.tensor_tensor(aes[b % 2], pk("sinks"), anm[b % 2], ALU.add).then_inc(S["es_dv"], 1)
                if i % H == 4 and i > 4:
                    b = i // H - 1
                    v.wait_ge(S["es_ac"], b + 1)
                    link(v.tensor_tensor(arv[b % 2], als[b % 2], aes[b % 2], ALU.add))
                    link(v.reciprocal(arv[b % 2], arv[b % 2]))
                    v.wait_ge(S["pv_mm"], H * (b + 1))
                    if b == 0:
                        for k in range(3):
                            v.wait_ge(hs_out[k], 16 * len(range(k, KC, 3)))
                    for k in range(2):
                        ins = v.tensor_tensor(YA[:, b + 1, 512 * k:512 * (k + 1)].rearrange("p (h d) -> p h d", d=HD),
                                              pb[6 + k][:, :].rearrange("p (h d) -> p h d", d=HD),
                                              bc(arv[b % 2][:, 8 * k:8 * (k + 1)], HD), ALU.mult)
                    ins.then_inc(S["o_dv"], 1)

        def dve_sample_attention(v):
            link = dve_link[0]
            v.wait_ge(S["cache_in"], 16 * (2 * NSAMP + 3))
            for par in range(2):
                v.tensor_copy(qs[0:HD, par:H:2, :], qT[64 * par:64 * par + 64, :, 0:NSAMP])
            for g in range(KVH):
                ins = v.tensor_copy(Ks[0:HD, :, g, NWK], kd[0:HD, g, 0:NSAMP])
            ins.then_inc(S["qs_dv"], 1)
            v.wait_ge(S["ss_mm"], 1)
            v.tensor_copy(sT[:, 0:P], pb[0][:, 0:P])
            v.tensor_copy(sTm[0:NMETA, 0:P], pb[1][0:NMETA, 0:P]).then_inc(S["ss_ev"], 1)
            v.wait_ge(S["st2_mm"], 1)
            link(v.tensor_scalar(s2[:, 0:P + NMETA], pb[2][:, 0:P + NMETA], SCALE, None, ALU.mult))
            link(v.tensor_reduce(scol[:, 0:1], s2[:, 0:P + NMETA], AX, ALU.max))
            link(v.tensor_tensor(scol[:, 0:1], scol[:, 0:1], pk("sink_col"), ALU.max))
            v.tensor_scalar(scol[:, 1:2], scol[:, 0:1], -1.0, None, ALU.mult).then_inc(S["sx_dv"], 1)
            v.wait_ge(S["sp_ac"], 1)
            link(v.tensor_tensor(scol[:, 4:5], scol[:, 2:3], scol[:, 3:4], ALU.add))
            link(v.reciprocal(scol[:, 5:6], scol[:, 4:5]))
            v.tensor_scalar(s2[:, 0:P + NMETA], s2[:, 0:P + NMETA], scol[:, 5:6], None, ALU.mult)\
             .then_inc(S["spn_dv"], 1)
            v.wait_ge(S["sot_mm"], 1)
            for k in range(2):
                ins = v.tensor_copy(YA[0:NSAMP, 0, 512 * k:512 * (k + 1)], pb[2 + k][0:NSAMP, :])
            ins.then_inc(S["sya_dv"], 1)

        def dve_gates(v):
            link = dve_link[0]
            v.wait_ge(S["yx_pl"], NBLK)
            v.wait_ge(S["yst_ev"], 1)
            v.wait_ge(S["sya_dv"], 1)
            v.wait_ge(S["o_dv"], NBLK)
            link(v.memset(ssq[:, :, :], 1.0))
            for i in range(6 * NT):
                j, t = divmod(i, NT)
                r, half = tile_rows(t), slice(512 * (j % 2), 512 * (j % 2) + 512)
                g, y = gate[i % 4][0:r, :], Y[0:r, t, half]
                v.wait_ge(S["c_ac"], i + 1)
                if i:
                    v.wait_ge(S["c_dv"], i)
                if j >= 4:
                    link(v.tensor_tensor(g, g, YA[0:r, t, half], ALU.mult))
                v.tensor_tensor(y, y, g, ALU.add if j >= 4 else ALU.mult).then_inc(S["c_dv"], 1)
                if i == 2 * NT - 1:
                    dve_rms(v)

        def dve_rms(v):
            link = dve_link[0]
            v.wait_ge(S["rms_ac"], 1)
            v.wait_ge(S["ln_in"], 16)
            v.tensor_scalar(rstd[:, :, :], ssq[:, :, :], 1.0 / (D // KVH), RMS_EPS, ALU.mult, ALU.add)\
             .then_inc(S["rms_dv"], 1)
            v.wait_ge(S["rms_ac"], 2)
            link(v.reciprocal(rstd[:, :, :], rstd[:, :, :]))
            for t in range(NT):
                r = tile_rows(t)
                for g in range(KVH):
                    s = slice(g * 256, (g + 1) * 256)
                    ins = v.scalar_tensor_tensor(Y[0:r, t, s], Y[0:r, t, s], rstd[0:r, t, g:g + 1], lnr[0:r, 0, s],
                                                 ALU.mult, ALU.mult)
            link(ins)

        def layer_norm(v, x, r, n, gain):
            link = dve_link[0]
            st, mv = lst[(n - 1) % 2], lmv[(n - 1) % 2]
            v.bn_stats(st[0:r, 0:6], x[:, 0:512])
            link(v.bn_stats(st[0:r, 6:12], x[:, 512:1024]))
            link(v.bn_aggr(mv[0:r, 0:2], st[0:r, :]))
            v.tensor_scalar(mv[0:r, 2:3], mv[0:r, 1:2], LN_EPS, None, ALU.add).then_inc(S["lv_dv"], 1)
            v.wait_ge(S["lv_ac"], n)
            link(v.reciprocal(mv[0:r, 3:4], mv[0:r, 2:3]))
            link(v.tensor_scalar(x, x, mv[0:r, 0:1], mv[0:r, 3:4], ALU.subtract, ALU.mult))
            return v.tensor_tensor(x, x, gain, ALU.mult)

        def dve_mix(v):
            link = dve_link[0]
            v.wait_ge(S["xt_in"], 32)

            def norm(t):
                r = tile_rows(t)
                v.wait_ge(S["w_mm"], t + 1)
                for n in range(2):
                    s = slice(512 * n, 512 * n + 512)
                    ins = v.scalar_tensor_tensor(h1[0:r, t, s], h1[0:r, t, s], ALPHA, pb[2 + 2 * (t % 2) + n][0:r, :],
                                                 ALU.mult, ALU.add)
                link(ins)
                layer_norm(v, h1[0:r, t, :], r, t + 1, lnr[0:r, 1, :]).then_inc(S["ln_dv"], 1)

            def logit(t):
                r = tile_rows(t)
                v.wait_ge(S["lg_mm"], t + 1)
                v.tensor_tensor(lg[0:r, t, :], pb[6 + t % 2][0:r, 0:NG + NE], pk("r_bias", r), ALU.add)\
                 .then_inc(S["lg_dv"], 1)

            for t in range(NT):
                norm(t)
                if t == NT - 2:
                    link(v.memset(lg[:, 0, :], 0.0))
                    logit(0)
            for t in range(1, NT):
                logit(t)

        def dve_route(v):
            link = dve_link[0]
            wide = lambda x, *shape: x.broadcast_to((P,) + shape)
            iota4 = wide(pk("iota4").unsqueeze(1), NT, NG)
            iota8 = wide(pk("iota8").unsqueeze(1), NT, EPG)
            iota16 = pk("iota16")

            def first_max(x, iota, n, mx, eq, ix, one):
                link(v.tensor_reduce(mx, x, AX, ALU.max))
                link(v.tensor_tensor(eq, x, bc(mx, n), ALU.is_equal))
                link(v.scalar_tensor_tensor(eq, eq, -64.0, iota, ALU.mult, ALU.add))
                link(v.tensor_reduce(ix, eq, AX, ALU.min))
                link(v.tensor_tensor(one, eq, bc(ix, n), ALU.is_equal))

            v.wait_ge(S["lg_dv"], NT)
            gl = lg[:, :, 0:NG]
            first_max(gl, iota4, NG, gmx, geq[:, :, :], gix, goh[:, :, :])
            v.tensor_tensor(ex[:, :, 0:NG], gl, bc(gmx, NG), ALU.subtract)
            link(v.tensor_tensor(ein_g[:, :, :, :], lg[:, :, NG:NG + NE].rearrange("p t (g j) -> p t g j", g=NG),
                                 wide(goh[:, :, :].unsqueeze(3), NT, NG, EPG), ALU.mult))
            link(v.tensor_reduce(ein[:, :, :], ein_g[:, :, :, :].rearrange("p t g j -> p t j g"), AX, ALU.add))
            first_max(ein[:, :, :], iota8, EPG, emx[:, 0, :], eeq[0][:, :, :], eix[:, 0, :], eoh[0][:, :, :])
            link(v.scalar_tensor_tensor(ein2[:, :, :], eoh[0][:, :, :], -3e38, ein[:, :, :], ALU.mult, ALU.add))
            first_max(ein2[:, :, :], iota8, EPG, emx[:, 1, :], eeq[1][:, :, :], eix[:, 1, :], eoh[1][:, :, :])
            v.tensor_tensor(ex[:, :, NG], emx[:, 1, :], emx[:, 0, :], ALU.subtract).then_inc(S["rt1_dv"], 1)
            link(v.scalar_tensor_tensor(eno[:, :, :], wide(gix.unsqueeze(1), 2, NT), float(EPG), eix[:, :, :],
                                        ALU.mult, ALU.add))
            link(v.tensor_scalar(eno[:, :, :], eno[:, :, :], 64.0 * EPG + 64.0, None, ALU.add))
            o10 = oh[:, :, :, :].rearrange("p k t e -> p (k t) e")
            e10 = eno[:, :, :].rearrange("p k t -> p (k t)")
            link(v.tensor_tensor(o10, wide(pk("iota32").unsqueeze(1), 2 * NT, NE), bc(e10, NE), ALU.is_equal))
            link(v.tensor_scalar(oh[:, :, 0, :], oh[:, :, 0, :], pk("valid")[:, 0:1], None, ALU.mult))
            v.tensor_tensor(chosen.rearrange("p (t e) -> p t e", e=NE), oh[:, 0, :, :], oh[:, 1, :, :], ALU.add)\
             .then_inc(S["ch_dv"], 1)
            for s in scan:
                v.memset(s, 0.0)
            v.memset(odd[:, :, :], 0.0)
            v.tensor_scalar(tb, pk("half32"), float(P), None, ALU.mult)
            v.tensor_scalar(thr8, pk("iota8"), float(P), float(P), ALU.mult, ALU.add)
            v.wait_ge(S["rt_ac"], 1)
            link(v.tensor_reduce(gws, ex[:, :, 0:NG], AX, ALU.add))
            link(v.tensor_scalar(den, ex[:, :, NG], 1.0, None, ALU.add))
            link(v.tensor_tensor(den, den, gws, ALU.mult))
            link(v.reciprocal(prob[:, 0, :], den))
            v.tensor_tensor(prob[:, 1, :], prob[:, 0, :], ex[:, :, NG], ALU.mult)
            v.wait_ge(S["rk_mm"], 1)
            link(v.tensor_copy(cnt[:, :, :].rearrange("p a b -> p (a b)"), pb[6][:, NT * NE:(NT + 1) * NE]))
            v.tensor_copy(odd[:, :, 1], cnt[:, :, 0])
            link(v.tensor_tensor(cpair, cnt[:, :, 0], cnt[:, :, 1], ALU.add))
            link(v.tensor_tensor(over[:, :, :], bc(cpair, EPG), wide(thr8.unsqueeze(1), NPAIR, EPG), ALU.is_gt))
            link(v.tensor_reduce(extra, over[:, :, :], AX, ALU.add))
            link(v.tensor_copy(scan[0][:, NPAIR:], extra))
            for n, step in enumerate((1, 2, 4, 8)):
                a, b = scan[n % 2], scan[(n + 1) % 2]
                link(v.tensor_tensor(b[:, NPAIR:], a[:, NPAIR:], a[:, NPAIR - step:2 * NPAIR - step], ALU.add))
            cum = scan[0][:, NPAIR:]
            link(v.tensor_tensor(obase, cum, extra, ALU.subtract))
            link(v.tensor_tensor(ccol, obase, iota16, ALU.subtract))
            link(v.tensor_scalar(ccol, ccol, float(P), float(P * (NPAIR - 1)), ALU.mult, ALU.add))
            v.tensor_copy(tc[:, :, :], bc(ccol, 2))
            link(v.tensor_tensor(rank[:, :, :], pb[6][:, 0:NT * NE].rearrange("p (t e) -> p t e", e=NE),
                                 wide(odd[:, :, :].rearrange("p a b -> p (a b)").unsqueeze(1), NT, NE), ALU.add))
            for n, w in enumerate((wide(rank[:, :, :].unsqueeze(1), 2, NT, NE), None, None)):
                if n == 0:
                    ins = v.tensor_tensor(pick[0][:, :, :, :], oh[:, :, :, :], w, ALU.mult)
                else:
                    w = (tb, tc[:, :, :].rearrange("p a b -> p (a b)"))[n - 1]
                    ins = v.tensor_tensor(pick[n][:, :, :, :].rearrange("p k t e -> p (k t) e"), o10,
                                          wide(w.unsqueeze(1), 2 * NT, NE), ALU.mult)
            link(ins)
            for n in range(3):
                ins = v.tensor_reduce(sel[n], pick[n][:, :, :, :].rearrange("p k t e -> p (k t) e"), AX, ALU.add)
            link(ins)
            v.tensor_tensor(sel[1], sel[1], sel[0], ALU.add)
            link(v.tensor_scalar(far, sel[0], float(P), None, ALU.is_ge))
            link(v.tensor_tensor(far, far, sel[2], ALU.mult))
            v.tensor_tensor(slot, far, sel[1], ALU.add).then_inc(S["slot_dv"], 1)
            link(v.tensor_tensor(below[:, :, :], wide(cum.unsqueeze(1), EPG, NPAIR), bc(pk("iota8"), NPAIR), ALU.is_le))
            v.tensor_copy(pair[:, 0:NPAIR], iota16)
            link(v.tensor_reduce(pair[:, NPAIR:], below[:, :, :], AX, ALU.add))
            link(v.tensor_scalar(pair[:, NPAIR:], pair[:, NPAIR:], float(NPAIR - 1), None, ALU.min))
            v.tensor_scalar(table[:, 0:1], cum[:, NPAIR - 1:NPAIR], float(NPAIR), None, ALU.add)
            v.tensor_scalar(table[:, 1:2], cum[:, NPAIR - 1:NPAIR], float(NPAIR - 1), None, ALU.add)
            two = table[:, 2:].rearrange("p (b u) -> p b u", u=2)
            v.tensor_scalar(two[:, :, 0], pair, 2.0, None, ALU.mult)
            v.tensor_scalar(two[:, :, 1], pair, 2.0, 1.0, ALU.mult, ALU.add).then_inc(S["tab_dv"], 1)
            v.scalar_tensor_tensor(c128, obase, float(P), cnt[:, :, 0], ALU.mult, ALU.add)
            link(v.tensor_tensor(thr_g[:, :, :], wide(iota16.unsqueeze(1), EPG, NPAIR), bc(pair[:, NPAIR:], NPAIR),
                                 ALU.is_equal))
            link(v.tensor_tensor(thr_g[:, :, :], thr_g[:, :, :], wide(c128.unsqueeze(1), EPG, NPAIR), ALU.mult))
            v.tensor_copy(thr[:, 0:NPAIR], cnt[:, :, 0])
            link(v.tensor_reduce(thr[:, NPAIR:], thr_g[:, :, :], AX, ALU.add))
            link(v.tensor_tensor(thr[:, NPAIR:], thr[:, NPAIR:], thr8, ALU.subtract))
            link(v.tensor_scalar(mask[:, :, 0], thr, pk("iota_p"), None, ALU.is_gt))
            link(v.tensor_scalar(mask[:, :, 1], mask[:, :, 0], -1.0, 1.0, ALU.mult, ALU.add))

        def dve_experts(v):

            def empty_x():
                v.tensor_copy(XT[:, 4:8, :].rearrange("p k c -> p (k c)"), pb[1][:, :]).then_inc(S["xt_d"], 1)

            v.wait_ge(S["xtr_mm"], 1)
            empty_x()
            v.wait_ge(S["tab_dv"], 1)
            blocks = v.value_load(table[0:1, 0:1], min_val=NPAIR, max_val=NBT)
            with v.Fori(0, blocks) as i:
                v.tensor_copy(mcol[:, :, :], mask[:, bass.ds(i, 1), :]).then_inc(S["mc_dv"], 1)
                v.wait_ge(S["mc_dv"], i + 1)
                for u in range(2):
                    v.wait_ge(S["sg_ac"], i * 2 + (u + 1))
                    v.scalar_tensor_tensor(hid[u], pb[2 + u][:, DE:2 * DE], mcol[:, 0, u:u + 1], sg[u],
                                           ALU.mult, ALU.mult).then_inc(S["hid_dv"], 1)
                v.wait_ge(S["htr_mm"], i * 2 + 2)
                v.tensor_copy(hidT[1][:, :, :].rearrange("p k c -> p (k c)"), pb[5][:, 0:DE]).then_inc(S["hte1"], 1)
                v.wait_ge(S["xtr_mm"], i + 2)
                empty_x()
                v.wait_ge(S["dn_mm"], i * 2 + 2)
                v.wait_ge(S["yw_out"], i * 16 + 16)
                v.tensor_copy(Yout[:, 512:1024], pb[7][:, :]).then_inc(S["y_d"], 1)
                v.wait_ge(S["y_d"], i + 1)

        def dve_final(v):
            link = dve_link[0]
            for t in range(NT):
                r = tile_rows(t)
                h = h1[0:r, t, :]
                v.wait_ge(S["gp_ac"], t + 1)
                link(v.scalar_tensor_tensor(h, h, ALPHA, G[0][0:r, t, :], ALU.mult, ALU.add))
                link(v.scalar_tensor_tensor(h, G[1][0:r, t, :], prob[0:r, 1, t:t + 1], h, ALU.mult, ALU.add))
                layer_norm(v, h, r, NT + t + 1, lnr[0:r, 3, :]).then_inc(S["ln_dv"], 1)

        def pool_projection(p):
            p.memset(xbc[:, :, 0:3], 0.0).then_inc(S["pool_init"], 1)
            p.memset(vd[:, 0, :], 0.0).then_inc(S["pool_init"], 1)
            p.memset(vd[:, META, :], 0.0).then_inc(S["pool_init"], 1)
            p.memset(zeros, 0.0).then_inc(S["zero_pl"], 1)
            p.wait_ge(S["sconv_dv"], 1)
            p.dma_start(io["o_pconv"], pconv).then_inc(S["small_out"], 16)
            p.dma_start(io["o_sconv"], xs4[:, :, 1:CW, :]).then_inc(S["small_out"], 16)
            p.wait_ge(S["rope_dv"], QT_TILES + KT_TILES)
            p.dma_start(io["o_k"], kd[0:HD, :, :]).then_inc(S["small_out"], 16)
            p.wait_ge(S["vd_ev"], NT)
            p.dma_start(io["o_v0"], vd[0:PR0, 0, 0:KVH * HD]).then_inc(S["small_out"], 16)
            p.dma_start(io["o_v1"], vd[:, NT - 1, 0:KVH * HD]).then_inc(S["small_out"], 16)

        def pool_ssd(p):
            link = pool_link[0]
            p.wait_ge(S["sp5_ac"], 1)
            for c in range(NBLK + 1):
                t, n = (c, P) if c else (META, NMETA)
                h3 = lambda a: a[0:n, :].rearrange("p (h d) -> p h d", d=HD)
                p.wait_ge(S["tr_ev"], c + 1)
                if c:
                    p.wait_ge(S["st_mm"], c)
                link(p.tensor_tensor(h3(xd), h3(xt), bc(dt[0:n, t, :], HD), ALU.mult))
                if c:
                    if c > 1:
                        p.wait_ge(S["yx_pl"], c - 1)
                    p.tensor_tensor(h3(Dx), h3(xt), bc(pk("d_skip"), HD), ALU.mult)
                p.tensor_tensor(h3(xdd), h3(xd), bc(dst[0:n, t, :], HD), ALU.mult).then_inc(S["pre_pl"], 1)
                if c:
                    p.wait_ge(S["h_dv"], c)
                    p.tensor_tensor(Ht.rearrange("p (h d) -> p h d", d=HD), Hs.rearrange("p (h d) -> p h d", d=HD),
                                    bc(etot[:, t, :], HD), ALU.mult).then_inc(S["ht_pl"], 1)
                    p.wait_ge(S["ya_dv"], 2 * c)
                    p.tensor_tensor(Y[:, c, :], Y[:, c, :], Dx, ALU.add).then_inc(S["yx_pl"], 1)
            p.wait_ge(S["h_dv"], NBLK + 1)
            p.dma_start(io["o_pssm"], Hs).then_inc(S["out_d"], 16)

        def pool_sample_state(p):
            for t in range(KC):
                p.wait_ge(S["sh_dv"], t + 1)
                p.dma_start(io["o_sssm"][t], hst[t % 3]).then_inc(hs_out[t % 3], 16)

        def pool_mix(p):
            p.wait_ge(S["ln_in"], 16)
            for t in range(NT):
                r = tile_rows(t)
                p.wait_ge(S["ln_dv"], t + 1)
                p.tensor_tensor(h1[0:r, t, :], h1[0:r, t, :], lnr[0:r, 2, :], ALU.add).then_inc(S["lnb_pl"], 1)

        def pool_scatter(p):
            p.wait_ge(S["slot_dv"], 1)
            p.wait_ge(S["lnb_pl"], NT)
            p.wait_ge(S["zero_out"], 32)
            for k in range(2):
                for t in range(NT):
                    r, c = tile_rows(t), k * NT + t
                    p.indirect_dma_start(scr_x, bass.IndirectOffsetOnAxis(ap=slot[0:r, c:c + 1].bitcast(U32), axis=0),
                                         h1[0:r, t, :], None).then_inc(S["sc_out"], 16)

        def pool_final(p):
            p.wait_ge(S["moe_ac"], 1)
            for t in range(NT):
                for k in range(2):
                    r, c = tile_rows(t), k * NT + t
                    p.indirect_dma_start(G[k][0:r, t, :], None, scr_y,
                                         bass.IndirectOffsetOnAxis(ap=slot[0:r, c:c + 1].bitcast(U32), axis=0))\
                     .then_inc(S[f"gt{t}"], 16)
            for t in range(NT):
                r = tile_rows(t)
                p.wait_ge(S["ln_dv"], NT + t + 1)
                p.tensor_tensor(h1[0:r, t, :], h1[0:r, t, :], lnr[0:r, 4, :], ALU.add).then_inc(S["o_pl"], 1)

        @block.sync
        def _(sp):
            sp_projection(sp)
            sp_sample_state(sp)
            sp_caches(sp)
            sp_gates(sp)
            sp_experts(sp)
            sp_outputs(sp)

        @block.tensor
        def _(pe):
            pe_projection(pe)
            pe_decays(pe)
            pe_ssd(pe)
            pe_sample_bc(pe)
            pe_sample_y(pe)
            pe_attention(pe)
            pe_sample_attention(pe)
            pe_gates(pe)
            pe_mix(pe)
            pe_rank(pe)
            pe_experts(pe)

        @block.scalar
        def _(act):
            act_link.append(chained(act, S["act_chain"]))
            act_projection(act)
            act_decays(act)
            act_ssd(act)
            act_sample_state(act)
            act_attention(act)
            act_sample_attention(act)
            act_gates(act)
            act_mix(act)
            act_route(act)
            act_experts(act)
            act_final(act)

        @block.vector
        def _(v):
            dve_link.append(chained(v, S["dve_chain"]))
            dve_projection(v)
            dve_decays(v)
            dve_ssd(v)
            dve_sample_state(v)
            dve_attention(v)
            dve_sample_attention(v)
            dve_gates(v)
            dve_mix(v)
            dve_route(v)
            dve_experts(v)
            dve_final(v)

        @block.gpsimd
        def _(p):
            pool_link.append(chained(p, S["pool_chain"]))
            pool_projection(p)
            pool_ssd(p)
            pool_sample_state(p)
            p.wait_ge(S["small_out"], 80)
            p.wait_ge(S["out_d"], 16)
            for k in range(3):
                p.wait_ge(hs_out[k], 16 * len(range(k, KC, 3)))
            pool_mix(p)
            pool_scatter(p)
            pool_final(p)


def constants():
    i = np.arange(P)
    tri = (i[:, None] <= i[None, :]).astype(np.float32)
    c = {
        "ident": np.eye(P), "upper": tri, "ones": np.ones((P, P)),
        "neg": np.where(tri > 0, 0.0, NEG), "strict": tri - np.eye(P),
        "amask": np.concatenate([np.where(i[None, :] > i[:, None], 0.0, NEG), np.zeros((P, NMETA)),
                                 np.where(i[None, :] <= i[:, None], 0.0, NEG)], 1),
        "iota_p": i[:, None], "iota4": np.tile(np.arange(NG), (P, 1)), "iota8": np.tile(np.arange(EPG), (P, 1)),
        "iota16": np.tile(np.arange(NPAIR), (P, 1)), "half32": np.tile(np.arange(NE) // 2, (P, 1)),
        "iota32": np.tile(np.arange(NE), (P, 1)),
        "valid": np.concatenate([(i[:, None] < NSAMP), np.ones((P, NBLK))], 1),
    }
    pos = np.concatenate([np.full(NSAMP, PAST), np.arange(NSEQ)]).astype(np.float32)
    half = HD // 2
    freq = np.exp(np.float32(-np.log(10000.0)) * np.arange(half, dtype=np.float32) * np.float32(2.0 / HD))
    ang = (pos[None, :] * freq[:, None].astype(np.float32)).astype(np.float32)
    cos, sin = np.cos(ang), np.sin(ang)
    rope = np.stack([np.concatenate([cos] * 4), np.concatenate([sin, -sin] * 2)]).astype(np.float32)
    return {k: np.asarray(v, np.float32) for k, v in c.items()}, rope


def lay_out(x):
    def cols(w):
        return w.reshape(KC, P, -1).transpose(1, 0, 2)

    def rows(v):
        return np.broadcast_to(v[None, :], (P, v.shape[0]))

    c, rope = constants()
    w = x["w_in"][0]
    edge = np.cumsum([0, H * HD, KVH * HD, KVH * HD, D, 2048, H, D, D])
    q, k, v, z, xbc, dt, ga, gs = (w[:, edge[i]:edge[i + 1]] for i in range(8))
    c["conv_w"] = x["conv_w"][0].reshape(CW, XT_TILES, P).transpose(2, 1, 0).reshape(P, -1)
    c["conv_b"] = x["conv_b"][0].reshape(XT_TILES, P).T
    for name in ("dt_bias", "a_log", "d_skip"):
        c[name] = rows(x[name][0])
    c["sinks"] = rows(x["attn_sinks"][0])
    c["sink_col"] = np.tile(x["attn_sinks"][0], NSAMP)[:, None]
    c["d_col"] = np.repeat(x["d_skip"][0], HD).reshape(KC, P).T
    c["r_bias"] = rows(np.concatenate([x["router_group_b"][0], x["router_expert_b"][0]]))
    tok = np.concatenate([x["x_sample"][:, 0], x["meta_tokens"], x["x_prompt"][0]])
    f = np.concatenate([xbc, q, k], 1)
    a = {
        "pack": np.concatenate([c[n] for n in PACK], 1),
        "x_t": tok.T.reshape(KC, P, NTOK).transpose(1, 0, 2),
        "x_tok": np.concatenate([x["x_sample"][:, 0], x["x_prompt"][0]]),
        "rope": rope,
        "w_f": f.reshape(KC, P, FT, P).transpose(2, 1, 0, 3),
        "w_vd": cols(np.concatenate([v, dt], 1)),
        "w_t": np.concatenate([z, gs, ga], 1).reshape(KC, P, 6, 512).transpose(2, 1, 0, 3),
        "w_o": cols(x["w_o"][0]),
        "w_r": cols(np.concatenate([x["router_group_w"][0], x["router_expert_w"][0]], 1)),
        "conv_state": x["state_conv"][0].reshape(NSAMP, CW - 1, XT_TILES, P).transpose(3, 2, 1, 0),
        "state": x["state_ssm"][0].reshape(NSAMP, KC, P, NST).transpose(1, 2, 0, 3),
        "win_k": x["cache_win_k"][0][:, 1:].transpose(3, 0, 2, 1),
        "win_v": x["cache_win_v"][0][:, 1:].reshape(NSAMP, NWK, KVH * HD).transpose(1, 0, 2),
        "meta_k": x["cache_meta_k"][0].transpose(3, 0, 2, 1),
        "meta_v": x["cache_meta_v"][0].reshape(NSAMP, NMETA, KVH * HD).transpose(1, 0, 2),
        "ln": np.stack([x[n][0] for n in ("ssm_norm_w", "ln1_g", "ln1_b", "ln2_g", "ln2_b")]),
        "w_gu": np.concatenate([x["w_gate"][0], x["w_up"][0]], 2).reshape(NE, KC, P, 2 * DE).transpose(0, 2, 1, 3),
        "w_d": x["w_down"][0].reshape(NE, DE // P, P, D).transpose(0, 2, 1, 3),
    }
    return {k: np.ascontiguousarray(v, dtype=np.float32) for k, v in a.items()}


OUTS = {
    "o_prompt": (NPROMPT, D), "o_sample": (NSAMP, D), "o_k": (HD, KVH, NTOK), "o_v0": (PR0, KVH * HD),
    "o_v1": (P, KVH * HD), "o_pconv": (P, XT_TILES, CW - 1), "o_sconv": (P, XT_TILES, CW - 1, NSAMP),
    "o_pssm": (P, D), "o_sssm": (KC, P, NSAMP, NST),
}


def kernel(**inputs):
    import concourse.bacc as bacc
    from concourse.bass_utils import run_bass_kernel_spmd as run

    arrays = lay_out({k: np.asarray(v) for k, v in inputs.items()})
    nc = bacc.Bacc("TRN2", target_bir_lowering=False, num_devices=1)
    io = {n: nc.dram_tensor(f"in_{n}", a.shape, F32, kind="ExternalInput").ap() for n, a in arrays.items()}
    io |= {n: nc.dram_tensor(n, s, F32, kind="ExternalOutput").ap() for n, s in OUTS.items()}
    build(nc, io)
    r = run(nc, [{f"in_{n}": a for n, a in arrays.items()}], core_ids=[0]).results[0]
    k = r["o_k"]
    head = lambda a: a.transpose(2, 1, 0)
    v4 = lambda a: a.reshape(-1, KVH, HD)
    conv = lambda a: a.transpose(2, 1, 0).reshape(CW - 1, XT_TILES * P)
    sconv = r["o_sconv"].transpose(3, 2, 1, 0).reshape(NSAMP, CW - 1, XT_TILES * P)
    pssm = r["o_pssm"].reshape(NST, H, HD).transpose(1, 2, 0)
    sssm = r["o_sssm"].reshape(H, HD, NSAMP, NST).transpose(2, 0, 1, 3)
    return (
        r["o_prompt"][None], r["o_sample"][:, None],
        head(k[:, :, SEQ0:PR0])[None, None], v4(r["o_v0"][SEQ0:])[None, None],
        head(k[:, :, NTOK - WIN:])[None, None], v4(r["o_v1"])[None, None],
        conv(r["o_pconv"])[None, None], pssm[None, None],
        head(k[:, :, :NSAMP])[None, :, None], v4(r["o_v0"][:SEQ0])[None, :, None],
        sconv[None], sssm[None],
    )
```

```python
from contextlib import ExitStack

import concourse.bass as bass
import numpy as np
from concourse import mybir

F32 = mybir.dt.float32
F32R = mybir.dt.float32r
BF16 = mybir.dt.bfloat16
I32 = mybir.dt.int32
U32 = mybir.dt.uint32
ALU = mybir.AluOpType
ACT = mybir.ActivationFunctionType
AX = mybir.AxisListType.X

P = 128
D = 1024
KC = D // P
NSAMP, NMETA, NPROMPT = 8, 16, 512
SEQ0 = NSAMP
PR0 = NSAMP + NMETA
NTOK = PR0 + NPROMPT
NSEQ = NMETA + NPROMPT
HALF = NTOK // 2
NBLK = NPROMPT // P
NT = NBLK + 1
META = NT
H, KVH, HD = 16, 4, 64
QPK = H // KVH
NST = 128
WIN = 128
NWK = WIN - 1
PAST = 2048
CW = 4
XT_TILES = 16
QT_TILES, KT_TILES = 8, 2
FT = XT_TILES + QT_TILES + KT_TILES
VD = KVH * HD + H
NE, NG, EPG, DE = 32, 4, 8, 256
NPAIR = NE // 2
NOV = 8
NBT = NPAIR + NOV
ALPHA = 2.0 ** 0.25
LN_EPS = 1e-5
RMS_EPS = 1e-5
SCALE = HD ** -0.5
NEG = -1e30

PACK = {}
_at = 0
for _name, _n in (("ident", P), ("upper", P), ("ones", P), ("neg", P), ("strict", P), ("amask", P + NMETA + P),
                  ("iota_p", 1), ("iota4", NG), ("iota8", EPG), ("iota16", NPAIR), ("half32", NE), ("iota32", NE), ("valid", NT),
                  ("conv_w", XT_TILES * CW), ("conv_b", XT_TILES), ("dt_bias", H), ("a_log", H), ("d_skip", H),
                  ("sinks", H), ("sink_col", 1), ("d_col", KC), ("r_bias", NG + NE)):
    PACK[_name] = (_at, _at + _n)
    _at += _n
NPACK = _at


def tile_cols(t):
    return (0, NSAMP) if t == 0 else (PR0 + P * (t - 1), PR0 + P * t)


GATES = ([(j, t) for j in range(2) for t in range(1, NT)] + [(0, 0), (1, 0)]
         + [(j, t) for j in range(2, 6) for t in range(NT)])
N_Z = 2 * NT


def row_cols(t):
    return (0, NSAMP) if t == 0 else (NSAMP + P * (t - 1), NSAMP + P * t)


def tile_rows(t):
    return NSAMP if t == 0 else P


def build(nc, io):
    ctx = ExitStack()
    with ctx:
        def sem(name):
            return ctx.enter_context(nc.semaphore(name))

        pieces = {"small": 3000, "r1": 10240, "y": 10240, "x": 17200, "w": 12480}
        with ExitStack() as views:
            rounded = [views.enter_context(nc.sbuf_tensor(f"{k}_r", [P, n], F32R)) for k, n in pieces.items()]
        arena = [ctx.enter_context(nc.sbuf_tensor(f"{k}_f", [P, n], F32)) for k, n in pieces.items()]

        def cut(at, *shape, whole=arena):
            n, i = int(np.prod(shape)), 0
            while at >= whole[i].shape[1]:
                at -= whole[i].shape[1]
                i += 1
            v = whole[i][:, at:at + n]
            if len(shape) == 1:
                return v
            names = "abcde"[:len(shape)]
            return v.rearrange(f"p ({' '.join(names)}) -> p {' '.join(names)}",
                               **{c: s for c, s in zip(names[1:], shape[1:])})

        pack = cut(0, NPACK)

        def pk(name, rows=P):
            a, b = PACK[name]
            return pack[0:rows, a:b]

        ident, upper, onesf = pk("ident"), pk("upper"), pk("ones")
        wr = cut(1200, KC, NG + NE)
        bfc = cut(1488, 256).bitcast(BF16).rearrange("p (a b) -> p a b", a=4)
        identb, negb, strictb, onesb = (bfc[:, i, :] for i in range(4))
        C1 = 1744
        dtx, dab, dex, dt, adt, ncs, tot, tmc, ecs, dst, etot = (cut(C1 + 96 * i, NT + 1, H) for i in range(11))
        pconv = cut(C1 + 1056, XT_TILES, CW - 1)
        small = cut(2850, 150)

        R1, RY, RYA, RX, RQ, RV, RXT, RW = 3000, 13240, 18360, 23480, 32616, 39048, 40680, 44968
        Y = cut(RY, NT, D)
        YA = cut(RYA, NT, D)
        xbc = cut(RX, XT_TILES, 3 + NSEQ)
        xs4 = cut(RX + 8496, XT_TILES, CW, NSAMP)
        xcs = cut(RX + 9008, XT_TILES, NSAMP)
        qT = cut(RQ, QT_TILES, NTOK)
        kd = cut(RQ + 4288, KVH, NTOK)
        vd = cut(RV, NT + 1, VD)
        xT = cut(RXT, KC, NTOK)
        wf = [cut(RW + 1024 * i, KC, P) for i in range(4)]
        wfh = [cut(RW + 4096 + 1024 * i, KC, P, whole=rounded) for i in range(4)]
        wfl = [cut(RW + 1024 * i, KC, P, whole=rounded) for i in range(4)]
        xh, xl = cut(R1 + 4528, KC, NTOK, whole=rounded), cut(RYA, KC, NTOK, whole=rounded)
        wvd = cut(RY, KC, VD)
        wt = [cut(RW + 4096 * i, KC, 512) for i in range(2)]

        acc = [cut(R1 + 528 * i, NSEQ) for i in range(2)]
        raw = [cut(R1 + 1056 + 536 * i, NTOK) for i in range(2)]
        swp, rcs = cut(R1 + 2128, NTOK), cut(R1 + 2664, NTOK)
        cosT, sinT = cut(R1 + 3200, NTOK), cut(R1 + 3736, NTOK)
        acc_s, tmp_s = cut(R1 + 4272, XT_TILES, NSAMP), cut(R1 + 4400, XT_TILES, NSAMP)
        xt = cut(R1, D)
        Bt = cut(R1 + 1024, KVH * NST)
        xd, xdd, Dx, Hs, Ht = (cut(R1 + 1536 + 1024 * i, D) for i in range(5))
        au = [cut(RYA + 512 * i, QPK * P) for i in range(KVH)]
        LG = [cut(R1 + 6656 + 512 * i, QPK * P) for i in range(4)]
        bcs = cut(R1 + 8704, P)
        ds = cut(R1 + 8832, 2, H)
        dd = cut(R1 + 8864, NSAMP, 2, H)
        dcol, dtcol, xdt = (cut(R1 + 9120 + 64 * i, KC, NSAMP) for i in range(3))
        ys = cut(R1 + 9312, KC, NSAMP)
        junk = cut(R1 + 6656, NSAMP, NST)
        bcg = cut(RYA, 2, NSAMP, NST)
        hst = [cut(RYA + 2048 + 1024 * i, NSAMP, NST) for i in range(3)]
        AW = P + NMETA + P
        sS = [cut(R1 + AW * i, AW) for i in range(4)]
        pS = [cut(R1 + AW * (4 + i), AW) for i in range(8)]
        pS4 = [cut(R1 + AW * (4 + 4 * i), QPK, AW) for i in range(2)]
        pT = [cut(R1 + 12 * AW + 256 * i, 256) for i in range(3)]
        pTg = [cut(R1 + 12 * AW + 768 + P * i, P) for i in range(2)]
        A1 = R1 + 12 * AW + 768 + 2 * P
        kl = [cut(at, KVH, AW, whole=rounded) for at in (RX + 2048, RX + 2048 + KVH * AW, A1 + 160)]
        qh = [cut(RW + 4096 + D * b, QT_TILES, P, whole=rounded) for b in range(NBLK - 1)]
        ql = cut(RQ, QT_TILES, NTOK, whole=rounded)
        assert A1 + 160 + KVH * AW <= R1 + 5632
        pM = [cut(R1 + 9920 + 64 * i, QPK * NMETA) for i in range(2)]
        vm = cut(R1 + 8896, KVH, QPK * HD)
        amx, anm, als, aes, arv = ([cut(A1 + 32 * i + 16 * j, H) for j in range(2)] for i in range(5))
        Ks = cut(RX, NSAMP, KVH // 2, P)
        Km = cut(RX + 8704, NSAMP, KVH // 2, NMETA)
        Vs = cut(RX + 4608, NSAMP, KVH * HD)
        Vm = cut(RX + 6656, NSAMP, KVH * HD)
        kx = [cut(R1 + 5632 + KVH * AW * b, KVH, AW, whole=rounded) for b in range(NBLK - 1)]
        A2 = R1 + 3264
        qs = cut(A2, KVH // 2, 2, QPK, NSAMP)
        sT, sTm, s2, pTs, pTm, oT = (cut(A2 + 128 + 144 * i, 144) for i in range(6))
        scol = cut(A2 + 1000, 8)

        lnr = cut(R1, 5, D)
        h1 = cut(R1 + 5120, NT, D)
        gate = [cut(RQ + 512 * i, 512) for i in range(4)]
        gate_z = [cut(at, 512) for at in (R1 + 5632, R1 + 6144, RY, RY + 512)]
        mT = cut(RQ + 2048, KC, NSAMP + NPROMPT)
        wo_a, wo_b = cut(RX, KC // 2, D), cut(RW, KC // 2, D)
        sqj = cut(RV, D)
        gxh = [cut(R1, KC, NTOK, whole=rounded), cut(R1 + 5120, KC, NTOK, whole=rounded)]
        gxl = cut(RXT, KC, NTOK, whole=rounded)
        gwl = [cut(RW + 4096 * i, KC, 512, whole=rounded) for i in range(2)]
        gwh = [cut(at, KC, 512, whole=rounded)
               for at in (RX, RX + 4096, RQ + 2048, RX + 4096, RQ + 2048, RX + 4096)]
        lg = cut(RY, NT, NG + NE)
        hT = cut(RYA, NT, KC, P)
        ssq, rstd = (small[:, 16 + 20 * i:36 + 20 * i].rearrange("p (t g) -> p t g", g=KVH) for i in range(2))
        lst = [small[:, 56 + 16 * i:68 + 16 * i] for i in range(2)]
        lmv = [small[:, 88 + 4 * i:92 + 4 * i] for i in range(2)]

        at = [RY + NT * (NG + NE)]

        def more(*shape, dtype=F32):
            v = cut(at[0], *shape)
            at[0] += int(np.prod(shape))
            return v if dtype == F32 else v.bitcast(dtype)

        geq, goh = more(NT, NG), more(NT, NG)
        gmx, gix, gws, gw = (more(NT) for _ in range(4))
        ein_g, ein, ein2 = more(NT, NG, EPG), more(NT, EPG), more(NT, EPG)
        eeq = [more(NT, EPG) for _ in range(2)]
        eoh = [more(NT, EPG) for _ in range(2)]
        emx, eix, eno = more(2, NT), more(2, NT), more(2, NT)
        ex = more(NT, NG + 1)
        den = more(NT)
        oh = more(2, NT, NE)
        chosen = cut(at[0], NT * NE // 2).bitcast(BF16)
        at[0] += NT * NE // 2
        cnt = more(NPAIR, 2)
        cpair, extra, obase, ccol, c128 = (more(NPAIR) for _ in range(5))
        over = more(NPAIR, EPG)
        scan = [more(2 * NPAIR) for _ in range(2)]
        odd, tb, tc = more(NPAIR, 2), more(NE), more(NPAIR, 2)
        rank = more(NT, NE)
        pick = [more(2, NT, NE) for _ in range(3)]
        sel = [more(2 * NT) for _ in range(3)]
        far = more(2 * NT)
        thr8 = more(EPG)
        below, thr_g = more(EPG, NPAIR), more(EPG, NPAIR)
        pair, thr = more(NBT), more(NBT)
        mask = more(NBT, 2)
        table = more(2 + 2 * NBT, dtype=I32)
        mcol = more(1, 2)
        assert at[0] <= RYA
        prob = small[:, 96:106].rearrange("p (k t) -> p k t", k=2)
        slot = small[:, 106:116].bitcast(I32)
        zeros = Y[:, NT - 1, :]
        wgu = [cut(RXT + 4096 * u, KC, 2 * DE) for u in range(2)]
        wdn = [cut(RXT + 8192 + 2048 * u, DE // P, D) for u in range(2)]
        X, XT, Yout = cut(RX, D), cut(RX + 1024, KC, P), cut(RX + 2048, D)
        sg = [cut(RX + 3072 + 256 * u, DE) for u in range(2)]
        hid = [cut(RX + 3584 + 256 * u, DE) for u in range(2)]
        hidT = [cut(RX + 4096 + 256 * u, DE // P, P) for u in range(2)]
        G = [cut(RY, NT, D), cut(RYA, NT, D)]

        pb = [ctx.enter_context(nc.psum_tensor(f"bank{i}", [P, 512], F32)) for i in range(8)]

        scr_bc = nc.dram_tensor("scr_bc", (2 * KVH * NSAMP, NST), F32).ap()
        scr_d = nc.dram_tensor("scr_d", (NSAMP, 2 * H), F32).ap()

        scr_x = nc.dram_tensor("scr_x", ((NBT + 1) * P, D), F32).ap()
        scr_y = nc.dram_tensor("scr_y", (NBT * P, D), F32).ap()

        block_pos = [SEQ0 - SEQ0, *(NMETA + P * b for b in range(NBLK))]

        def chunk(c):
            n = NMETA if c == 0 else P
            return slice(3 + block_pos[c], 3 + block_pos[c] + n)

        S = {}
        for name in ("pack_in x_in x2_in xh_ac xl_dv wh_ac wl_dv rope_in cst_in wr_in wvd_in meta_in cache_in "
                     "pool_init bf_dv f_mm f_ev conv_dv silu_ac sconv_dv ssilu_ac rope_dv rc_pl pm_pl vd_mm vd_ev "
                     "sp1_dv sp2_ac sp3_dv cs_mm sp4_dv sp5_ac "
                     "tr_mm tr_ev pre_pl cb_mm l_mm l_ac g_dv au_dv yd_mm yo_mm st_mm ht_pl h_dv ya_dv yx_pl "
                     "bct_mm bct_ev bcs_out ds_ac ds_out dd_in dcol_dv bcg_in bcg_fr sh_ac sh_dv ysx_dv yst_mm yst_ev "
                     "s_mm s_dv p_ac t_mm td_dv ta_ac pv_mm es_dv es_ac o_dv "
                     "qs_dv ss_mm ss_ev st2_mm sx_dv sp_ac spn_dv pt2_mm pt2_ev spv_mm so_ev sot_mm sya_dv "
                     "wt_in0 wt_in1 ln_in xt_in wo_in c_mm c_ac c_dv kx_pl xr_in rms_ac mt_mm mt_ev w_mm ln_dv lnb_pl lg_mm lg_dv rms_dv lv_dv lv_ac "
                     "zero_pl zero_out rt1_dv rt_ac ch_dv rk_mm slot_dv tab_dv sc_out "
                     "xs_in xtr_mm xt_a xt_d gu_in0 gu_in1 dn_in0 dn_in1 gu_mm sg_ac hid_dv "
                     "htr_mm hte0 hte1 dn_mm y_a y_d yw_out mc_dv moe_ac "
                     "gt0 gt1 gt2 gt3 gt4 gp_ac o_pl o_out "
                     "small_out out_d dve_chain act_chain pool_chain").split():
            S[name] = sem(name)
        wf_in = [sem(f"wf_in{i}") for i in range(4)]
        hs_in = [sem(f"hs_in{i}") for i in range(3)]
        hs_out = [sem(f"hs_out{i}") for i in range(3)]

        def chained(eng, s):
            done = [0]

            def link(ins):
                done[0] += 1
                ins.then_inc(s, 1)
                eng.wait_ge(s, done[0])
            return link

        def bc(v, n):
            return v.unsqueeze(2).broadcast_to(tuple(v.shape) + (n,))

        block = ctx.enter_context(nc.Block())

        def sp_projection(sp):
            sp.dma_start(xT[:, 0:4, :], io["x_t"][:, 0:4, :]).then_inc(S["x_in"], 16)
            for i in range(FT):
                if i >= 4:
                    sp.wait_ge(S["f_mm"], i - 3)
                if i == XT_TILES + 4:
                    sp.wait_ge(S["vd_ev"], NT)
                    sp.dma_start(vd[0:NMETA, META, :], vd[NSAMP:PR0, 0, :]).then_inc(S["meta_in"], 16)
                sp.dma_start(wf[i % 4], io["w_f"][i]).then_inc(wf_in[i % 4], 16)
                if i == 0:
                    sp.dma_start(xT[:, 4:8, :], io["x_t"][:, 4:8, :]).then_inc(S["x2_in"], 16)
                    sp.dma_start(pack, io["pack"]).then_inc(S["pack_in"], 16)
                if i == 1:
                    sp.dma_start(cosT, io["rope"][0]).then_inc(S["rope_in"], 16)
                    sp.dma_start(sinT, io["rope"][1]).then_inc(S["rope_in"], 16)
                if i == 3:
                    sp.dma_start(xs4[:, :, 0:CW - 1, :], io["conv_state"]).then_inc(S["cst_in"], 16)
                    sp.dma_start(wvd, io["w_vd"]).then_inc(S["wvd_in"], 16)
                    sp.dma_start(wr, io["w_r"]).then_inc(S["wr_in"], 16)
            sp_gate_weights(sp, 0)
            sp_gate_weights(sp, 1)
            sp.wait_ge(S["zero_pl"], 1)
            sp.dma_start(scr_x.rearrange("(b p) d -> p b d", p=P),
                         zeros.unsqueeze(1).broadcast_to((P, NBT + 1, D))).then_inc(S["zero_out"], 16)
            sp.dma_start(scr_y[NPAIR * P:].rearrange("(b p) d -> p b d", p=P),
                         zeros.unsqueeze(1).broadcast_to((P, NOV, D))).then_inc(S["zero_out"], 16)

        def sp_sample_state(sp):
            for t in range(3):
                sp.dma_start(hst[t], io["state"][t]).then_inc(hs_in[t], 16)
            sp.wait_ge(S["ds_ac"], 1)
            sp.dma_start(scr_d, ds[0:NSAMP, :, :].rearrange("p a h -> p (a h)")).then_inc(S["ds_out"], 16)
            sp.wait_ge(S["ds_out"], 16)
            sp.dma_start(dd, scr_d.rearrange("(o n) h -> o (n h)", o=1).broadcast_to((P, NSAMP * 2 * H))
                         .rearrange("p (n a h) -> p n a h", n=NSAMP, a=2)).then_inc(S["dd_in"], 16)
            sp.wait_ge(S["bct_ev"], 1)
            sp.dma_start(scr_bc, bcs[0:2 * KVH * NSAMP, :]).then_inc(S["bcs_out"], 16)
            sp.wait_ge(S["bcs_out"], 16)
            rows = scr_bc.rearrange("(a g n) s -> a g (n s)", a=2, g=KVH)
            for t in range(KC):
                if t % 2 == 0:
                    g = t // 2
                    if g:
                        sp.wait_ge(S["bcg_fr"], g)
                    for a in range(2):
                        sp.dma_start(bcg[:, a, :, :].rearrange("p n s -> p (n s)"),
                                     rows[a, g:g + 1, :].broadcast_to((P, NSAMP * NST))).then_inc(S["bcg_in"], 16)
                if t >= 3:
                    sp.wait_ge(hs_out[t % 3], 16 * (t // 3))
                    sp.dma_start(hst[t % 3], io["state"][t]).then_inc(hs_in[t % 3], 16)

        def sp_caches(sp):
            sp.wait_ge(S["c_mm"], N_Z)
            sp.wait_ge(S["h_dv"], NBLK + 1)
            sp.wait_ge(S["yo_mm"], 2 * NBLK)
            sp.wait_ge(S["small_out"], 80)
            sp.wait_ge(S["dcol_dv"], 1)
            sp.wait_ge(S["bct_mm"], 1)
            for n in range(NSAMP):
                sp.dma_start(Ks[:, n, :, 0:NWK], io["win_k"][:, n, :, :]).then_inc(S["cache_in"], 16)
            sp.dma_start(Km[:, :, :, :], io["meta_k"]).then_inc(S["cache_in"], 16)
            sp.dma_start(Vs[0:NWK, :, :], io["win_v"]).then_inc(S["cache_in"], 16)
            sp.dma_start(Vm[0:NMETA, :, :], io["meta_v"]).then_inc(S["cache_in"], 16)
            for n in range(NSAMP):
                sp.dma_start(Vs[NWK:P, n, :], vd[n:n + 1, 0, 0:KVH * HD]).then_inc(S["cache_in"], 16)

        def sp_gate_weights(sp, j):
            if j < 2:
                sp.wait_ge(S["f_mm"], FT)
            else:
                sp.wait_ge(S["c_mm"], N_Z - 1 + j - 2 if j < 4 else N_Z + NT * (j - 3))
            sp.dma_start(wt[j % 2], io["w_t"][j]).then_inc(S[f"wt_in{j % 2}"], 16)

        def sp_gates(sp):
            sp.wait_ge(S["kx_pl"], 1)
            for r in range(QPK):
                sp.dma_start(vm[NMETA * r:NMETA * (r + 1), :, HD * r:HD * (r + 1)],
                             vd[0:NMETA, META, 0:KVH * HD].rearrange("m (g d) -> m g d", g=KVH)).then_inc(S["meta_in"], 16)
            sp.wait_ge(S["c_mm"], N_Z)
            sp.dma_start(xT, io["x_t"]).then_inc(S["xr_in"], 16)
            sp_gate_weights(sp, 2)
            sp_caches(sp)
            sp.wait_ge(S["s_mm"], NBLK * H)
            sp_gate_weights(sp, 3)
            sp_residual(sp)
            sp_gate_weights(sp, 4)
            sp.wait_ge(S["spv_mm"], 1)
            sp.dma_start(wo_a, io["w_o"][:, 0:KC // 2, :]).then_inc(S["wo_in"], 16)
            sp_gate_weights(sp, 5)
            sp.wait_ge(S["c_mm"], N_Z + 3 * NT)
            sp.dma_start(wo_b, io["w_o"][:, KC // 2:, :]).then_inc(S["wo_in"], 16)
            sp.wait_ge(S["c_mm"], 6 * NT)
            sp.dma_start(h1[0:NSAMP, 0, :], io["x_tok"][0:NSAMP]).then_inc(S["xt_in"], 16)
            sp.dma_start(h1[:, 1:NT, :], io["x_tok"][NSAMP:].rearrange("(t p) d -> p t d", p=P)).then_inc(S["xt_in"], 16)

        def sp_residual(sp):
            sp.wait_ge(S["sot_mm"], 1)
            sp.wait_ge(S["spn_dv"], 1)
            sp.wait_ge(S["o_dv"], NBLK)
            sp.wait_ge(S["ysx_dv"], 1)
            sp.dma_start(lnr.rearrange("p a d -> p (a d)"),
                         io["ln"].rearrange("(o a) d -> o (a d)", o=1).broadcast_to((P, 5 * D))).then_inc(S["ln_in"], 16)

        def load_expert(sp, u, e):
            sp.dma_start(wgu[u].rearrange("p (a k) n -> p a k n", a=1),
                         io["w_gu"][bass.ds(e, 1)].rearrange("a p k n -> p a k n")).then_inc(S[f"gu_in{u}"], 16)

        def load_down(sp, u, e):
            sp.dma_start(wdn[u].rearrange("p (a k) n -> p a k n", a=1),
                         io["w_d"][bass.ds(e, 1)].rearrange("a p k n -> p a k n")).then_inc(S[f"dn_in{u}"], 16)

        def load_x(sp, b):
            sp.dma_start(X.rearrange("p (b d) -> p b d", b=1),
                         scr_x.rearrange("(b p) d -> b p d", p=P)[bass.ds(b, 1)].rearrange("b p d -> p b d"))\
              .then_inc(S["xs_in"], 16)

        def sp_experts(sp):
            sp.wait_ge(S["c_mm"], 6 * NT)
            load_expert(sp, 0, 0)
            sp.wait_ge(S["w_mm"], NT)
            load_expert(sp, 1, 1)
            for u in range(2):
                load_down(sp, u, u)
            sp.wait_ge(S["sc_out"], 16 * 2 * NT)
            sp.wait_ge(S["w_mm"], NT)
            load_x(sp, 0)
            sp.wait_ge(S["tab_dv"], 1)
            blocks = sp.value_load(table[0:1, 1:2], min_val=NPAIR - 1, max_val=NBT - 1)
            with sp.Fori(0, blocks) as i:
                sp.wait_ge(S["xtr_mm"], i + 1)
                load_x(sp, i + 1)
                for u in range(2):
                    e = sp.value_load(table[0:1, bass.ds(i * 2 + (4 + u), 1)], min_val=0, max_val=NE - 1)
                    sp.wait_ge(S["gu_mm"], i * 2 + (u + 1))
                    load_expert(sp, u, e)
                for u in range(2):
                    e = sp.value_load(table[0:1, bass.ds(i * 2 + (4 + u), 1)], min_val=0, max_val=NE - 1)
                    sp.wait_ge(S["dn_mm"], i * 2 + (u + 1))
                    load_down(sp, u, e)
            sp.wait_ge(S["xtr_mm"], blocks + 1)
            load_x(sp, NBT)

        def sp_outputs(sp):
            for t in range(NT):
                sp.wait_ge(S["o_pl"], t + 1)
                out = io["o_sample"] if t == 0 else io["o_prompt"][P * (t - 1):P * t]
                sp.dma_start(out, h1[0:tile_rows(t), t, :]).then_inc(S["o_out"], 16)
            sp.wait_ge(S["o_out"], 16 * NT)

        def group(pe, out, pairs, last=None):
            for i, (lhsT, rhs) in enumerate(pairs):
                ins = pe.matmul(out, lhsT, rhs, start=(i == 0), stop=(i == len(pairs) - 1))
            if last is not None:
                ins.then_inc(S[last], 1)
            return ins

        def split_product(pe, out, ah, al, bh, bl, start, stop):
            pe.matmul(out, ah, bh, start=start, stop=False)
            pe.matmul(out, ah, bl, start=False, stop=False)
            return pe.matmul(out, al, bh, start=False, stop=stop)

        def pe_projection(pe):
            for i in range(FT):
                if i == XT_TILES:
                    pe_values(pe)
                if i == XT_TILES + 5:
                    pe_decays(pe)
                pe.wait_ge(S["wl_dv"], i + 1)
                if i >= 2:
                    pe.wait_ge(S["f_ev"], i - 1)
                for h in range(2):
                    for k in range(KC):
                        if i == 0 and h == 0:
                            pe.wait_ge(S["xl_dv"], k + 1)
                        c = slice(h * HALF, (h + 1) * HALF)
                        ins = split_product(pe, pb[2 * (i % 2) + h][:, 0:HALF], wfh[i % 4][:, k, :], wfl[i % 4][:, k, :],
                                            xh[:, k, c], xl[:, k, c], k == 0, k == KC - 1)
                ins.then_inc(S["f_mm"], 1)

        def pe_values(pe):
            pe.wait_ge(S["wvd_in"], 16)
            for t in range(NT):
                a, b = tile_cols(t) if t else (0, PR0)
                if t >= 2:
                    pe.wait_ge(S["vd_ev"], t - 1)
                group(pe, pb[4 + t % 2][0:b - a, 0:VD], [(xT[:, k, a:b], wvd[:, k, :]) for k in range(KC)], "vd_mm")

        def pe_decays(pe):
            pe.wait_ge(S["sp3_dv"], 1)
            for t in range(1, NT + 1):
                n = P if t < META else NMETA
                pe.matmul(pb[6][0:n, t * H:(t + 1) * H], upper[0:n, 0:n], adt[0:n, t, :], start=True, stop=True)
                ins = pe.matmul(pb[6][:, (NT + 1 + t) * H:(NT + 2 + t) * H], onesf[0:n, :], adt[0:n, t, :],
                                start=True, stop=True)
            ins.then_inc(S["cs_mm"], 1)

        def pe_ssd(pe):
            pe.wait_ge(S["silu_ac"], XT_TILES)
            pe.wait_ge(S["f_ev"], FT)
            pe.wait_ge(S["sp4_dv"], 1)
            pe.wait_ge(S["bf_dv"], 1)
            for c in range(NBLK + 1):
                cols, n = chunk(c), (P if c else NMETA)
                t = c if c else META
                if c:
                    pe.wait_ge(S["h_dv"], c)
                if c >= 2:
                    pe.wait_ge(S["ya_dv"], 2 * (c - 1))
                for k in range(12):
                    ins = pe.transpose(pb[k // 4][0:n, (k % 4) * P:(k % 4) * P + P], xbc[:, k, cols], ident)
                ins.then_inc(S["tr_mm"], 1)
                if c:
                    for g in range(KVH):
                        ins = pe.matmul(pb[3][:, g * P:(g + 1) * P], xbc[:, 8 + g, cols], xbc[:, 12 + g, cols],
                                        start=True, stop=True)
                    ins.then_inc(S["cb_mm"], 1)

                    def decay(g):
                        used = KVH * (c - 1) + g
                        if used >= 2:
                            pe.wait_ge(S["l_ac"], used - 1)
                        out = pb[4 + g % 2]
                        pe.wait_ge(S["au_dv"], used + 1)
                        pe.matmul(out[:, :], identb, negb.unsqueeze(1).broadcast_to((P, QPK, P)), start=True, stop=False)
                        pe.matmul(out[:, :], onesf, au[g], start=False, stop=True).then_inc(S["l_mm"], 1)

                    def diagonal(g):
                        pe.wait_ge(S["g_dv"], KVH * (c - 1) + g + 1)
                        for r in range(QPK):
                            h = QPK * g + r
                            ins = pe.matmul(pb[6 + g // 2][:, (g % 2) * 256 + r * HD:(g % 2) * 256 + (r + 1) * HD],
                                            LG[g][:, r * P:(r + 1) * P], xd[:, h * HD:(h + 1) * HD],
                                            start=True, stop=True)
                        ins.then_inc(S["yd_mm"], 1)

                    def carried(gp):
                        for g in (2 * gp, 2 * gp + 1):
                            ins = pe.matmul(pb[2 + gp][:, (g % 2) * 256:(g % 2) * 256 + 256], xbc[:, 12 + g, cols],
                                            Hs[:, g * 256:(g + 1) * 256], start=True, stop=True)
                        ins.then_inc(S["yo_mm"], 1)

                    decay(0)
                    decay(1)
                    pe.wait_ge(S["tr_ev"], c + 1)
                    carried(0)
                    decay(2)
                    pe.wait_ge(S["pre_pl"], 2 * c + 1)
                    diagonal(0)
                    decay(3)
                    diagonal(1)
                    diagonal(2)
                    diagonal(3)
                    carried(1)
                else:
                    pe.wait_ge(S["tr_ev"], 1)
                pe.wait_ge(S["pre_pl"], 2 * c + 2)
                for g in range(KVH):
                    ins = pe.matmul(pb[g // 2][:, (g % 2) * 256:(g % 2) * 256 + 256],
                                    Bt[0:n, g * P:(g + 1) * P], xdd[0:n, g * 256:(g + 1) * 256],
                                    start=True, stop=True)
                ins.then_inc(S["st_mm"], 1)

        def pe_sample_bc(pe):
            pe.wait_ge(S["ssilu_ac"], 1)
            pe.wait_ge(S["ya_dv"], 2 * NBLK)
            pe.transpose(pb[3][0:64, 0:P], xcs[:, 8:16, :].rearrange("p a n -> p (a n)"), ident).then_inc(S["bct_mm"], 1)

        def pe_sample_y(pe):
            pe.wait_ge(S["ysx_dv"], 1)
            pe.wait_ge(S["bct_ev"], 1)
            pe.wait_ge(S["h_dv"], NBLK + 1)
            for t in range(KC):
                ins = pe.transpose(pb[t // 4][0:NSAMP, (t % 4) * P:(t % 4) * P + P], ys[:, t, :], ident)
            ins.then_inc(S["yst_mm"], 1)

        def pe_attention(pe):
            pe.wait_ge(S["rope_dv"], QT_TILES + KT_TILES)
            pe.wait_ge(S["meta_in"], 16)
            pe.wait_ge(S["yst_ev"], 1)
            pe.wait_ge(S["c_ac"], N_Z)
            n_all = NBLK * H

            def scores(i):
                b, h = divmod(i, H)
                g, r0 = h // QPK, HD * (h % 2)
                q = qT[r0:r0 + HD, h // 2, PR0 + P * b:PR0 + P * (b + 1)]
                key = kd[r0:r0 + HD, g, :]
                if i >= 3:
                    pe.wait_ge(S["s_dv"], i - 2)
                out = pb[i % 3]
                if b == 0:
                    ins = pe.matmul(out[:, P:AW], q, key[:, SEQ0:PR0 + P], start=True, stop=True)
                else:
                    pe.wait_ge(S["kx_pl"], 2 * b + 1)
                    ins = split_product(pe, out[:, 0:AW], qh[b - 1][r0:r0 + HD, h // 2, :],
                                        ql[r0:r0 + HD, h // 2, PR0 + P * b:PR0 + P * (b + 1)],
                                        kx[b - 1][r0:r0 + HD, g, :], kl[b - 1][r0:r0 + HD, g, :], True, True)
                ins.then_inc(S["s_mm"], 1)

            def turn(i):
                b = i // H
                pe.wait_ge(S["p_ac"], i + 1)
                if i >= 3:
                    j = i - 3
                    pe.wait_ge(S["td_dv" if j % 2 == 0 else "ta_ac"], j // 2 + 1)
                out, pr = pb[3 + i % 3], pS[i % 8]
                if b:
                    pe.transpose(out[:, 0:P], pr[:, 0:P], ident)
                if i % QPK == QPK - 1:
                    pe.wait_ge(S["pm_pl"], i // QPK + 1)
                    pe.transpose(out[0:QPK * NMETA, 2 * P:3 * P], pM[i // QPK % 2], ident)
                pe.transpose(out[:, P:2 * P], pr[:, P + NMETA:AW], ident).then_inc(S["t_mm"], 1)

            def values(i):
                b, h = divmod(i, H)
                g, t = h // QPK, b + 1
                pe.wait_ge(S["td_dv" if i % 2 == 0 else "ta_ac"], i // 2 + 1)
                if h == 0 and b:
                    pe.wait_ge(S["o_dv"], b)
                v = slice(g * HD, (g + 1) * HD)
                w = pT[i % 3]
                out = pb[6 + h // 8]
                own = out[:, (h % 8) * HD:(h % 8 + 1) * HD]
                new = h % 8 == 0
                if b:
                    pe.matmul(own, w[:, 0:P], vd[:, t - 1, v], start=new, stop=False, skip_group_check=True)
                ins = pe.matmul(own, w[:, P:2 * P], vd[:, t, v], start=new and b == 0, stop=False,
                                skip_group_check=True)
                if h % QPK == QPK - 1:
                    pe.wait_ge(S["meta_in"], 16 + 16 * QPK)
                    ins = pe.matmul(out[:, (g % 2) * 256:(g % 2) * 256 + 256], pTg[g % 2][0:QPK * NMETA, :],
                                    vm[0:QPK * NMETA, g, :], start=False, stop=True, skip_group_check=True)
                ins.then_inc(S["pv_mm"], 1)

            for i in range(n_all + 4):
                if i < n_all:
                    scores(i)
                if 2 <= i < n_all + 2:
                    turn(i - 2)
                if i >= 4:
                    values(i - 4)

        def pe_sample_attention(pe):
            pe.wait_ge(S["qs_dv"], 1)
            pe.wait_ge(S["cache_in"], 16 * (2 * NSAMP + 3))
            pe.wait_ge(S["o_dv"], NBLK)
            for n in range(NSAMP):
                for pair in range(KVH // 2):
                    c = slice(n * H + 8 * pair, n * H + 8 * (pair + 1))
                    q = qs[:, pair, :, :, n].rearrange("q p r -> q (p r)")
                    pe.matmul(pb[0][:, c], Ks[:, n, pair, :], q, start=True, stop=True)
                    ins = pe.matmul(pb[1][0:NMETA, c], Km[:, n, pair, :], q, start=True, stop=True)
            ins.then_inc(S["ss_mm"], 1)
            pe.wait_ge(S["ss_ev"], 1)
            pe.transpose(pb[2][:, 0:P], sT[:, 0:P], ident)
            pe.transpose(pb[2][:, P:P + NMETA], sTm[0:NMETA, 0:P], ident[0:NMETA, 0:NMETA]).then_inc(S["st2_mm"], 1)
            pe_gates(pe, N_Z, N_Z + 1)
            pe.wait_ge(S["spn_dv"], 1)
            pe.transpose(pb[0][:, 0:P], s2[:, 0:P], ident)
            pe.transpose(pb[0][0:NMETA, P:2 * P], s2[:, P:P + NMETA], ident).then_inc(S["pt2_mm"], 1)
            pe_gates(pe, N_Z + 1, N_Z + 2)
            pe.wait_ge(S["pt2_ev"], 1)
            pe.wait_ge(S["cache_in"], 16 * (2 * NSAMP + 3))
            for n in range(NSAMP):
                for pair in range(KVH // 2):
                    c = slice(n * H + 8 * pair, n * H + 8 * (pair + 1))
                    v = slice(2 * pair * HD, 2 * (pair + 1) * HD)
                    ins = group(pe, pb[1][:, c], [(Vs[:, n, v], pTs[:, c]), (Vm[0:NMETA, n, v], pTm[0:NMETA, c])])
            ins.then_inc(S["spv_mm"], 1)
            pe_gates(pe, N_Z + 2, N_Z + 3)
            pe.wait_ge(S["so_ev"], 1)
            for h in range(H):
                ins = pe.transpose(pb[2 + h // 8][0:NSAMP, (h % 8) * HD:(h % 8 + 1) * HD], oT[0:HD, h:P:H],
                                   ident[0:HD, 0:HD])
            ins.then_inc(S["sot_mm"], 1)

        def pe_gates(pe, first, last):
            for i in range(first, last):
                j, t = GATES[i]
                a, b = tile_cols(t)
                if i >= 4:
                    pe.wait_ge(S["c_ac"], i - 3)
                part, first_of = (0, i == 0) if i < N_Z else (1, i == N_Z)
                if i and j in (1, 3, 4, 5) and j != GATES[i - 1][0]:
                    pe.wait_ge(S["wl_dv"], FT + {1: 1, 3: 2, 4: 3, 5: 4}[j])
                rows = slice(0, P) if t == 0 else slice(a, b)
                for k in range(KC):
                    if first_of:
                        pe.wait_ge(S["xl_dv"], KC * (part + 1) + k + 1)
                    ins = split_product(pe, pb[4 + i % 4][:, :], gxh[part][:, k, rows], gxl[:, k, rows],
                                        gwh[j][:, k, :], gwl[j % 2][:, k, :], k == 0, k == KC - 1)
                ins.then_inc(S["c_mm"], 1)

        def pe_mix(pe):
            pe.wait_ge(S["sya_dv"], 1)
            pe.wait_ge(S["c_ac"], 6 * NT)

            def turn_merged(t):
                r = tile_rows(t)
                pe.wait_ge(S["c_dv"], 5 * NT + t + 1)
                if t:
                    pe.wait_ge(S["mt_ev"], t)
                for k in range(KC):
                    ins = pe.transpose(pb[k // 4][:, (k % 4) * P:(k % 4) * P + r], Y[0:r, t, k * P:(k + 1) * P],
                                       ident[0:r, 0:r])
                ins.then_inc(S["mt_mm"], 1)

            def mix(t):
                r, (a, b) = tile_rows(t), row_cols(t)
                pe.wait_ge(S["mt_ev"], t + 1)
                if t >= 2:
                    pe.wait_ge(S["lnb_pl"], t - 1)
                for n in range(2):
                    ins = group(pe, pb[2 + 2 * (t % 2) + n][0:r, :],
                                [(mT[:, k, a:b], (wo_a if k < KC // 2 else wo_b)[:, k % (KC // 2), n * 512:(n + 1) * 512]) for k in range(KC)])
                ins.then_inc(S["w_mm"], 1)

            def turn_h1(t):
                r = tile_rows(t)
                pe.wait_ge(S["lnb_pl"], t + 1)
                pe.wait_ge(S["mt_ev"], NT + t)
                for k in range(KC):
                    ins = pe.transpose(pb[k // 4][:, (k % 4) * P:(k % 4) * P + r], h1[0:r, t, k * P:(k + 1) * P],
                                       ident[0:r, 0:r])
                ins.then_inc(S["mt_mm"], 1)

            def logits(t):
                r = tile_rows(t)
                pe.wait_ge(S["mt_ev"], NT + t + 1)
                if t >= 2:
                    pe.wait_ge(S["lg_dv"], t - 1)
                group(pe, pb[6 + t % 2][0:r, 0:NG + NE], [(hT[:, t, k, 0:r], wr[:, k, :]) for k in range(KC)], "lg_mm")

            pe.wait_ge(S["wo_in"], 32)
            pe.wait_ge(S["wr_in"], 16)
            turn_merged(0)
            turn_merged(1)
            mix(0)
            turn_merged(2)
            mix(1)
            turn_merged(3)
            mix(2)
            turn_merged(4)
            mix(3)
            turn_h1(0)
            turn_h1(1)
            logits(0)
            mix(4)
            turn_h1(2)
            logits(1)
            turn_h1(3)
            logits(2)
            turn_h1(4)
            logits(3)
            logits(4)

        def pe_rank(pe):
            pe.wait_ge(S["ch_dv"], 1)
            pe.wait_ge(S["lg_dv"], NT)
            m = [chosen[:, t * NE:(t + 1) * NE] for t in range(NT)]
            for t in range(NT):
                group(pe, pb[6][:, t * NE:(t + 1) * NE], [(strictb, m[t])] + [(onesb, m[s]) for s in range(t)])
            group(pe, pb[6][:, NT * NE:(NT + 1) * NE], [(onesb, m[s]) for s in range(NT)], "rk_mm")

        def pe_experts(pe):

            def turn_x():
                for k in range(KC):
                    ins = pe.transpose(pb[k // 4][:, (k % 4) * P:(k % 4 + 1) * P], X[:, k * P:(k + 1) * P], ident)
                ins.then_inc(S["xtr_mm"], 1)

            def turn_hidden(u):
                for k in range(DE // P):
                    ins = pe.transpose(pb[4 + u][:, k * P:(k + 1) * P], hid[u][:, k * P:(k + 1) * P], ident)
                ins.then_inc(S["htr_mm"], 1)

            def gate_up(u, ks):
                for k in ks:
                    ins = pe.matmul(pb[2 + u][:, :], XT[:, k, :], wgu[u][:, k, :], start=(k == 0), stop=(k == KC - 1))
                if k == KC - 1:
                    ins.then_inc(S["gu_mm"], 1)

            def down(u):
                last = DE // P - 1
                for k in range(DE // P):
                    for n in range(2):
                        ins = pe.matmul(pb[6 + n][:, :], hidT[u][:, k, :], wdn[u][:, k, n * 512:(n + 1) * 512],
                                        start=(u == 0 and k == 0), stop=(u == 1 and k == last))
                ins.then_inc(S["dn_mm"], 1)

            pe.wait_ge(S["xs_in"], 16)
            pe.wait_ge(S["mt_ev"], 2 * NT)
            turn_x()
            pe.wait_ge(S["slot_dv"], 1)
            pe.wait_ge(S["tab_dv"], 1)
            blocks = pe.value_load(table[0:1, 0:1], min_val=NPAIR, max_val=NBT)
            with pe.Fori(0, blocks) as i:
                pe.wait_ge(S["xt_a"], i + 1)
                pe.wait_ge(S["xt_d"], i + 1)
                pe.wait_ge(S["gu_in0"], i * 16 + 16)
                gate_up(0, range(KC))
                pe.wait_ge(S["gu_in1"], i * 16 + 16)
                gate_up(1, range(KC // 2))
                pe.wait_ge(S["hid_dv"], i * 2 + 1)
                turn_hidden(0)
                gate_up(1, range(KC // 2, KC))
                pe.wait_ge(S["hte0"], i + 1)
                pe.wait_ge(S["dn_in0"], i * 16 + 16)
                down(0)
                pe.wait_ge(S["hid_dv"], i * 2 + 2)
                turn_hidden(1)
                pe.wait_ge(S["xs_in"], i * 16 + 32)
                turn_x()
                pe.wait_ge(S["hte1"], i + 1)
                pe.wait_ge(S["dn_in1"], i * 16 + 16)
                down(1)

        act_link = []

        def act_projection(act):
            act.wait_ge(S["pool_init"], 3)

            def high(i):
                act.wait_ge(wf_in[i % 4], 16 * (i // 4 + 1))
                act.copy(wfh[i % 4][:, :, :], wf[i % 4][:, :, :]).then_inc(S["wh_ac"], 1)

            for k in range(KC):
                if k % 4 == 0:
                    act.wait_ge(S["x2_in" if k else "x_in"], 16)
                act.copy(xh[:, k, :], xT[:, k, :]).then_inc(S["xh_ac"], 1)
                if k == 0:
                    high(0)
            high(1)
            high(2)
            act.wait_ge(S["cst_in"], 16)
            for i in range(FT + 1):
                if i + 3 < FT:
                    high(i + 3)
                if i == XT_TILES:
                    act_values(act)
                if i == XT_TILES + 2:
                    act_softplus(act)
                if i == XT_TILES + 3:
                    act_sample_decay(act)
                if i == XT_TILES + 6:
                    act_chunk_decays(act)
                if i < FT:
                    act.wait_ge(S["f_mm"], i + 1)
                    lo, hi = pb[2 * (i % 2)], pb[2 * (i % 2) + 1]
                    if i < XT_TILES:
                        act.copy(xs4[:, i, CW - 1, :], lo[:, 0:NSAMP])
                        act.copy(xbc[:, i, 3:3 + HALF - SEQ0], lo[:, SEQ0:HALF])
                        act.copy(xbc[:, i, 3 + HALF - SEQ0:3 + NSEQ], hi[:, 0:HALF]).then_inc(S["f_ev"], 1)
                    else:
                        j = i - XT_TILES
                        if j >= 2:
                            act.wait_ge(S["rope_dv"], j - 1)
                        act.copy(raw[j % 2][:, 0:HALF], lo[:, 0:HALF])
                        act.copy(raw[j % 2][:, HALF:NTOK], hi[:, 0:HALF]).then_inc(S["f_ev"], 1)
                if 1 <= i <= XT_TILES:
                    act.wait_ge(S["conv_dv"], i)
                    act.activation(xbc[:, i - 1, 3:3 + NSEQ], acc[(i - 1) % 2], ACT.Silu).then_inc(S["silu_ac"], 1)
                if i == XT_TILES + 1:
                    act.wait_ge(S["sconv_dv"], 1)
                    act.activation(xcs[:, :, :], acc_s[:, :, :], ACT.Silu).then_inc(S["ssilu_ac"], 1)

        def act_values(act):
            for t in range(NT):
                n = P if t else PR0
                act.wait_ge(S["vd_mm"], t + 1)
                act.copy(vd[0:n, t, :], pb[4 + t % 2][0:n, 0:VD]).then_inc(S["vd_ev"], 1)

        def act_softplus(act):
            link = act_link[0]
            act.wait_ge(S["sp1_dv"], 1)
            link(act.activation(dex[:, :, :], dab[:, :, :], ACT.Exp, scale=-1.0))
            act.activation(dex[:, :, :], dex[:, :, :], ACT.Ln, bias=1.0).then_inc(S["sp2_ac"], 1)
            act.activation(small[:, 0:H], pk("a_log"), ACT.Exp).then_inc(S["sp2_ac"], 1)

        def act_sample_decay(act):
            act.wait_ge(S["sp3_dv"], 1)
            act.activation(ds[0:NSAMP, 0, :], adt[0:NSAMP, 0, :], ACT.Exp)
            act.copy(ds[0:NSAMP, 1, :], dt[0:NSAMP, 0, :]).then_inc(S["ds_ac"], 1)

        def act_chunk_decays(act):
            act.wait_ge(S["sp4_dv"], 1)
            act.activation(ecs[:, 1:NT, :], ncs[:, 1:NT, :], ACT.Exp, scale=-1.0)
            act.activation(dst[:, 1:NT, :], tmc[:, 1:NT, :], ACT.Exp)
            act.activation(dst[0:NMETA, META, :], tmc[0:NMETA, META, :], ACT.Exp)
            act.activation(etot[:, 1:NT + 1, :], tot[:, 1:NT + 1, :], ACT.Exp).then_inc(S["sp5_ac"], 1)

        def act_ssd(act):
            act.wait_ge(S["rope_dv"], QT_TILES + KT_TILES)
            for c in range(NBLK + 1):
                n = P if c else NMETA
                act.wait_ge(S["tr_mm"], c + 1)
                if c:
                    if c == 1:
                        act.wait_ge(S["pre_pl"], 2)
                    else:
                        act.wait_ge(S["ht_pl"], c - 1)
                    act.wait_ge(S["st_mm"], c)
                act.copy(xt[0:n, 0:512], pb[0][0:n, :])
                act.copy(xt[0:n, 512:1024], pb[1][0:n, :])
                act.copy(Bt[0:n, :], pb[2][0:n, :]).then_inc(S["tr_ev"], 1)
                if c:
                    for g in range(KVH):
                        act.wait_ge(S["l_mm"], KVH * (c - 1) + g + 1)
                        for r in range(QPK):
                            h = QPK * g + r
                            ins = act.activation(LG[g][:, r * P:(r + 1) * P], pb[4 + g % 2][:, r * P:(r + 1) * P],
                                                 ACT.Exp, bias=ncs[:, c, h:h + 1])
                        ins.then_inc(S["l_ac"], 1)

        def act_sample_state(act):
            act.wait_ge(S["pre_pl"], 2 * NBLK + 2)
            act.wait_ge(S["yx_pl"], NBLK)
            act.wait_ge(S["st_mm"], NBLK + 1)
            act.wait_ge(S["bct_mm"], 1)
            act.copy(bcs[0:64, :], pb[3][0:64, 0:P]).then_inc(S["bct_ev"], 1)
            act.wait_ge(S["h_dv"], NBLK + 1)
            act_high(act, 0)
            act.wait_ge(S["dcol_dv"], 1)
            for t in range(KC):
                act.wait_ge(hs_in[t % 3], 16 * (t // 3 + 1))
                for n in range(NSAMP):
                    ins = act.activation(hst[t % 3][:, n, :], hst[t % 3][:, n, :], ACT.Copy, scale=dcol[:, t, n:n + 1])
                ins.then_inc(S["sh_ac"], 1)
                if t == 2:
                    act_high_weights(act, 1)
                act_gate(act, t)
            act.wait_ge(S["yst_mm"], 1)
            act.copy(Y[0:NSAMP, 0, 0:512], pb[0][0:NSAMP, :])
            act.copy(Y[0:NSAMP, 0, 512:1024], pb[1][0:NSAMP, :]).then_inc(S["yst_ev"], 1)
            act_gate(act, N_Z - 2)
            act_gate(act, N_Z - 1)

        def act_attention(act):
            n_all = NBLK * H
            for i in range(n_all + 5):
                if i < n_all:
                    b, h = divmod(i, H)
                    lo = 0 if b else P
                    act.wait_ge(S["s_dv"], i + 1)
                    if i >= 8:
                        act.wait_ge(S["pm_pl"], i // QPK - 1)
                        act.wait_ge(S["t_mm"], i // QPK * QPK - 4)
                    act.activation(pS[i % 8][:, lo:AW], sS[i % 4][:, lo:AW], ACT.Exp, bias=anm[b % 2][:, h:h + 1],
                                   accum_out=als[b % 2][:, h:h + 1]).then_inc(S["p_ac"], 1)
                j = i - 2
                if 0 <= j < n_all and j % 2:
                    act.wait_ge(S["t_mm"], j + 1)
                    if j >= 3:
                        act.wait_ge(S["pv_mm"], j - 2)
                    lo = 0 if j >= H else P
                    if j % QPK == QPK - 1:
                        act.copy(pTg[j // QPK % 2][0:QPK * NMETA, :], pb[3 + j % 3][0:QPK * NMETA, 2 * P:3 * P])
                    act.copy(pT[j % 3][:, lo:2 * P], pb[3 + j % 3][:, lo:2 * P]).then_inc(S["ta_ac"], 1)
                if i % H == 3 and i > 3:
                    b = i // H - 1
                    act.wait_ge(S["es_dv"], b + 1)
                    act.activation(aes[b % 2], aes[b % 2], ACT.Exp).then_inc(S["es_ac"], 1)

        def act_sample_attention(act):
            act.wait_ge(S["qs_dv"], 1)
            act.wait_ge(S["small_out"], 80)
            act.wait_ge(S["o_dv"], NBLK)
            act_high(act, 1)
            act.wait_ge(S["sx_dv"], 1)
            act.activation(s2[:, 0:P + NMETA], s2[:, 0:P + NMETA], ACT.Exp, bias=scol[:, 1:2], accum_out=scol[:, 2:3])
            act.activation(scol[:, 3:4], pk("sink_col"), ACT.Exp, bias=scol[:, 1:2]).then_inc(S["sp_ac"], 1)
            act_gate(act, N_Z)
            act.wait_ge(S["pt2_mm"], 1)
            act.copy(pTs[:, 0:P], pb[0][:, 0:P])
            act.copy(pTm[0:NMETA, 0:P], pb[0][0:NMETA, P:2 * P]).then_inc(S["pt2_ev"], 1)
            act_gate(act, N_Z + 1)
            act.wait_ge(S["spv_mm"], 1)
            for p in range(2):
                heads = lambda a: a.rearrange("q (m p r) -> q m p r", p=2, r=QPK)[:, :, p, :]
                ins = act.copy(heads(oT[0:HD, 0:P]), heads(pb[1][HD * p:HD * p + HD, 0:P]))
            ins.then_inc(S["so_ev"], 1)
            act_gate(act, N_Z + 2)
            act_gate(act, N_Z + 3)

        def act_high(act, part):
            j = 2 * part
            act.wait_ge(S[f"wt_in0"], 16 * (part + 1))
            if part:
                act.wait_ge(S["xr_in"], 16)
            for k in range(KC):
                act.copy(gxh[part][:, k, :], xT[:, k, :])
                act.copy(gwh[j][:, k, :], wt[0][:, k, :]).then_inc(S["xh_ac"], 1)

        def act_high_weights(act, j):
            act.wait_ge(S[f"wt_in{j % 2}"], 16 * (j // 2 + 1))
            act.copy(gwh[j][:, :, :], wt[j % 2][:, :, :]).then_inc(S["wh_ac"], 1)

        def act_gate(act, i):
            j, t = GATES[i]
            r = tile_rows(t)
            buf = gate_z if i < N_Z else gate
            act.wait_ge(S["c_mm"], i + 1)
            if i >= 4:
                act.wait_ge(S["c_dv"], i - 3)
            act.activation(buf[i % 4][0:r, :], pb[4 + i % 4][0:r, :], ACT.Silu if j < 2 else ACT.Sigmoid)\
               .then_inc(S["c_ac"], 1)

        def act_gates(act):
            act.wait_ge(S["cache_in"], 16 * (2 * NSAMP + 3))
            act_high_weights(act, 3)
            act_rms(act)
            for i in range(N_Z + 4, len(GATES)):
                if GATES[i] in ((3, 1), (4, 1)):
                    act_high_weights(act, GATES[i][0] + 1)
                act_gate(act, i)

        def act_rms(act):
            act.wait_ge(S["c_dv"], N_Z)
            for t in range(NT):
                r = tile_rows(t)
                for g in range(KVH):
                    ins = act.activation(sqj[0:r, g * 256:(g + 1) * 256], Y[0:r, t, g * 256:(g + 1) * 256], ACT.Square, accum_out=ssq[0:r, t, g:g + 1])
                act_link[0](ins)
            act.copy(small[:, 122:123], small[:, 0:1]).then_inc(S["rms_ac"], 1)
            act.wait_ge(S["rms_dv"], 1)
            act.activation(rstd[:, :, :], rstd[:, :, :], ACT.Sqrt).then_inc(S["rms_ac"], 1)

        def act_root(act, n):
            r, mv = tile_rows((n - 1) % NT), lmv[(n - 1) % 2]
            act.wait_ge(S["lv_dv"], n)
            act.activation(mv[0:r, 2:3], mv[0:r, 2:3], ACT.Sqrt).then_inc(S["lv_ac"], 1)

        def act_mix(act):
            act.wait_ge(S["c_dv"], 6 * NT)
            def empty(t, n_turned, dst):
                r = tile_rows(t)
                act.wait_ge(S["mt_mm"], n_turned)
                for n in range(2):
                    ins = act.copy(dst(n), pb[n][:, :].rearrange("p (k c) -> p k c", c=P)[:, :, 0:r])
                ins.then_inc(S["mt_ev"], 1)

            def merged(t):
                a, b = row_cols(t)
                empty(t, t + 1, lambda n: mT[:, 4 * n:4 * n + 4, a:b])

            def first(t):
                empty(t, NT + t + 1, lambda n: hT[:, t, 4 * n:4 * n + 4, 0:tile_rows(t)])

            for t in range(3):
                merged(t)
            act_root(act, 1)
            merged(3)
            act_root(act, 2)
            merged(4)
            act_root(act, 3)
            first(0)
            act_root(act, 4)
            first(1)
            first(2)
            act_root(act, 5)
            first(3)
            first(4)

        def act_route(act):
            act.wait_ge(S["rt1_dv"], 1)
            act.activation(ex[:, :, :], ex[:, :, :], ACT.Exp).then_inc(S["rt_ac"], 1)

        def act_experts(act):

            def empty_x():
                act.copy(XT[:, 0:4, :].rearrange("p k c -> p (k c)"), pb[0][:, :]).then_inc(S["xt_a"], 1)

            act.sem_inc(S["yw_out"], 16)
            act.wait_ge(S["xtr_mm"], 1)
            empty_x()
            act.wait_ge(S["tab_dv"], 1)
            blocks = act.value_load(table[0:1, 0:1], min_val=NPAIR, max_val=NBT)
            with act.Fori(0, blocks) as i:
                for u in range(2):
                    act.wait_ge(S["gu_mm"], i * 2 + (u + 1))
                    act.activation(sg[u], pb[2 + u][:, 0:DE], ACT.Silu).then_inc(S["sg_ac"], 1)
                    if u == 0:
                        act.wait_ge(S["htr_mm"], i * 2 + 1)
                        act.copy(hidT[0][:, :, :].rearrange("p k c -> p (k c)"), pb[4][:, 0:DE]).then_inc(S["hte0"], 1)
                act.wait_ge(S["xtr_mm"], i + 2)
                empty_x()
                act.wait_ge(S["dn_mm"], i * 2 + 2)
                act.wait_ge(S["yw_out"], i * 16 + 16)
                act.copy(Yout[:, 0:512], pb[6][:, :]).then_inc(S["y_a"], 1)
                act.wait_ge(S["y_a"], i + 1)
                act.wait_ge(S["y_d"], i + 1)
                act.dma_start(scr_y.rearrange("(b p) d -> b p d", p=P)[bass.ds(i, 1)].rearrange("b p d -> p b d"),
                              Yout.rearrange("p (b d) -> p b d", b=1)).then_inc(S["yw_out"], 16)
            act.wait_ge(S["yw_out"], blocks * 16 + 16)
            act.copy(small[:, 120:121], small[:, 0:1]).then_inc(S["moe_ac"], 1)

        def act_final(act):
            for t in range(NT + 1):
                if t < NT:
                    r = tile_rows(t)
                    act.wait_ge(S[f"gt{t}"], 32)
                    act.activation(G[0][0:r, t, :], G[0][0:r, t, :], ACT.Copy, scale=prob[0:r, 0, t:t + 1])\
                       .then_inc(S["gp_ac"], 1)
                if t:
                    act_root(act, NT + t)

        dve_link = []
        pool_link = []

        def dve_projection(v):
            link = dve_link[0]
            cw, cb = pk("conv_w"), pk("conv_b")

            def low(i):
                v.wait_ge(S["wh_ac"], i + 1)
                v.tensor_tensor(wfl[i % 4][:, :, :], wf[i % 4][:, :, :], wfh[i % 4][:, :, :].bitcast(F32),
                                ALU.subtract).then_inc(S["wl_dv"], 1)

            for k in range(KC):
                v.wait_ge(S["xh_ac"], k + 1)
                v.tensor_tensor(xl[:, k, :], xT[:, k, :], xh[:, k, :].bitcast(F32), ALU.subtract)\
                 .then_inc(S["xl_dv"], 1)
                if k == 0:
                    low(0)
            low(1)
            low(2)
            v.wait_ge(S["pack_in"], 16)
            for j, name in enumerate(("ident", "neg", "strict", "ones")):
                ins = v.tensor_copy(bfc[:, j, :], pk(name))
            ins.then_inc(S["bf_dv"], 1)
            for i in range(XT_TILES):
                low(i + 3)
                v.wait_ge(S["f_ev"], i + 1)
                if i >= 2:
                    v.wait_ge(S["silu_ac"], i - 1)
                v.tensor_copy(pconv[:, i, :], xbc[:, i, NSEQ:NSEQ + 3])
                a = acc[i % 2]
                link(v.tensor_scalar(a, xbc[:, i, 3:3 + NSEQ], cw[:, i * CW + 3:i * CW + 4], cb[:, i:i + 1],
                                     ALU.mult, ALU.add))
                for j in (0, 1):
                    link(v.scalar_tensor_tensor(a, xbc[:, i, j:j + NSEQ], cw[:, i * CW + j:i * CW + j + 1], a,
                                                ALU.mult, ALU.add))
                v.scalar_tensor_tensor(a, xbc[:, i, 2:2 + NSEQ], cw[:, i * CW + 2:i * CW + 3], a,
                                       ALU.mult, ALU.add).then_inc(S["conv_dv"], 1)
            v.wait_ge(S["cst_in"], 16)
            cwv = cw.rearrange("p (i j) -> p i j", j=CW)
            for j in range(CW):
                o = acc_s if j == 0 else tmp_s
                link(v.tensor_tensor(o[:, :, :], xs4[:, :, j, :], bc(cwv[:, :, j], NSAMP), ALU.mult))
                if j:
                    link(v.tensor_tensor(acc_s[:, :, :], acc_s[:, :, :], tmp_s[:, :, :], ALU.add))
            v.tensor_tensor(acc_s[:, :, :], acc_s[:, :, :], bc(cb, NSAMP), ALU.add).then_inc(S["sconv_dv"], 1)
            v.wait_ge(S["rope_in"], 32)
            dve_softplus(v)
            for j in range(QT_TILES + KT_TILES):
                if j == 5:
                    dve_chunk_decays(v)
                v.wait_ge(S["f_ev"], XT_TILES + j + 1)
                r = raw[j % 2]
                if j:
                    v.wait_ge(S["rope_dv"], j)
                for q in range(4):
                    o = q ^ 1
                    ins = v.tensor_tensor(swp[32 * o:32 * o + 32, :], r[32 * q:32 * q + 32, :],
                                          sinT[32 * q:32 * q + 32, :], ALU.mult)
                link(ins)
                v.wait_ge(S["rc_pl"], j + 1)
                if j < QT_TILES:
                    v.tensor_tensor(qT[:, j, :], rcs, swp, ALU.add).then_inc(S["rope_dv"], 1)
                else:
                    for half in range(2):
                        g = 2 * (j - QT_TILES) + half
                        src = slice(64 * half, 64 * half + 64)
                        for dstp in range(2):
                            ins = v.tensor_tensor(kd[64 * dstp:64 * dstp + 64, g, :], rcs[src, :], swp[src, :], ALU.add)
                    ins.then_inc(S["rope_dv"], 1)

        def dve_softplus(v):
            link = dve_link[0]
            v.wait_ge(S["vd_ev"], NT)
            v.wait_ge(S["meta_in"], 16)
            bias = pk("dt_bias").unsqueeze(1).broadcast_to((P, NT + 1, H))
            link(v.tensor_tensor(dtx[:, :, :], vd[:, :, KVH * HD:VD], bias, ALU.add))
            v.scalar_tensor_tensor(dab[:, :, :], dtx[:, :, :], -1.0, dtx[:, :, :], ALU.mult, ALU.max)\
             .then_inc(S["sp1_dv"], 1)
            v.wait_ge(S["sp2_ac"], 2)
            link(v.scalar_tensor_tensor(dt[:, :, :], dtx[:, :, :], 0.0, dex[:, :, :], ALU.max, ALU.add))
            v.scalar_tensor_tensor(adt[:, :, :], dt[:, :, :], -1.0,
                                   small[:, 0:H].unsqueeze(1).broadcast_to((P, NT + 1, H)), ALU.mult, ALU.mult)\
             .then_inc(S["sp3_dv"], 1)

        def dve_chunk_decays(v):
            link = dve_link[0]
            v.wait_ge(S["cs_mm"], 1)
            cs = pb[6][:, 0:(NT + 1) * H].rearrange("p (t h) -> p t h", h=H)
            total = pb[6][:, (NT + 1) * H:2 * (NT + 1) * H].rearrange("p (t h) -> p t h", h=H)
            v.tensor_scalar(ncs[:, 1:NT, :], cs[:, 1:NT, :], -1.0, None, ALU.mult)
            v.tensor_scalar(ncs[0:NMETA, META, :], cs[0:NMETA, META, :], -1.0, None, ALU.mult)
            link(v.tensor_copy(tot[:, 1:NT + 1, :], total[:, 1:NT + 1, :]))
            v.tensor_tensor(tmc[0:NMETA, META, :], tot[0:NMETA, META, :], ncs[0:NMETA, META, :], ALU.add)
            v.tensor_tensor(tmc[:, 1:NT, :], tot[:, 1:NT, :], ncs[:, 1:NT, :], ALU.add).then_inc(S["sp4_dv"], 1)

        def dve_decay_rows(v, c, g):
            o = au[g].rearrange("p (r l) -> p r l", r=QPK)
            v.tensor_tensor(o, upper.unsqueeze(1).broadcast_to((P, QPK, P)), bc(adt[:, c, QPK * g:QPK * (g + 1)], P),
                            ALU.mult).then_inc(S["au_dv"], 1)

        def dve_ssd(v):
            link = dve_link[0]
            v.wait_ge(S["sp3_dv"], 1)
            for g in range(KVH):
                dve_decay_rows(v, 1, g)
            v.wait_ge(S["sp5_ac"], 1)
            for c in range(NBLK + 1):
                if c == NBLK:
                    v.wait_ge(S["zero_out"], 32)
                if c:
                    v.wait_ge(S["cb_mm"], c)
                    for g in range(KVH):
                        v.wait_ge(S["l_ac"], KVH * (c - 1) + g + 1)
                        o = LG[g].rearrange("p (r l) -> p r l", r=QPK)
                        v.tensor_tensor(o, o, pb[3][:, g * P:(g + 1) * P].unsqueeze(1).broadcast_to((P, QPK, P)),
                                        ALU.mult).then_inc(S["g_dv"], 1)
                        if c < NBLK:
                            dve_decay_rows(v, c + 1, g)
                    for gp in range(2):
                        y = Y[:, c, 512 * gp:512 * (gp + 1)]
                        v.wait_ge(S["yo_mm"], 2 * (c - 1) + gp + 1)
                        link(v.tensor_tensor(y.rearrange("p (h d) -> p h d", d=HD),
                                             pb[2 + gp][:, :].rearrange("p (h d) -> p h d", d=HD),
                                             bc(ecs[:, c, 8 * gp:8 * (gp + 1)], HD), ALU.mult))
                        v.wait_ge(S["yd_mm"], KVH * (c - 1) + 2 * gp + 2)
                        v.tensor_tensor(y, y, pb[6 + gp][:, :], ALU.add).then_inc(S["ya_dv"], 1)
                v.wait_ge(S["st_mm"], c + 1)
                if c:
                    v.wait_ge(S["ht_pl"], c)
                for i in range(2):
                    s = slice(512 * i, 512 * (i + 1))
                    if c:
                        ins = v.tensor_tensor(Hs[:, s], Ht[:, s], pb[i][:, :], ALU.add)
                    else:
                        ins = v.tensor_copy(Hs[:, s], pb[i][:, :])
                ins.then_inc(S["h_dv"], 1)

        def dve_sample_state(v):
            link = dve_link[0]
            v.wait_ge(S["dd_in"], 16)
            for hh in range(2):
                rows = slice(64 * hh, 64 * hh + 64)
                for a, o in ((0, dcol), (1, dtcol)):
                    ins = v.tensor_copy(o[rows, :, :].rearrange("p t n -> p n t"), dd[rows, :, a, hh:H:2])
            link(ins)
            link(v.tensor_tensor(xdt[:, :, :], xcs[:, 0:KC, :], dtcol[:, :, :], ALU.mult))
            v.tensor_tensor(dtcol[:, :, :], xcs[:, 0:KC, :], bc(pk("d_col"), NSAMP), ALU.mult)\
             .then_inc(S["dcol_dv"], 1)
            dve_low(v, 0)
            for t in range(KC):
                if t % 2 == 0:
                    v.wait_ge(S["bcg_in"], 32 * (t // 2 + 1))
                v.wait_ge(S["sh_ac"], t + 1)
                h = hst[t % 3]
                for n in range(NSAMP):
                    ins = v.scalar_tensor_tensor(h[:, n, :], bcg[:, 0, n, :], xdt[:, t, n:n + 1], h[:, n, :],
                                                 ALU.mult, ALU.add)
                ins.then_inc(S["sh_dv"], 1)
                v.wait_ge(S["sh_dv"], t + 1)
                for n in range(NSAMP):
                    ins = v.tensor_tensor_reduce(junk[:, n, :], h[:, n, :], bcg[:, 1, n, :], 1.0, 0.0, ALU.mult, ALU.add,
                                                 ys[:, t, n:n + 1])
                if t % 2:
                    ins.then_inc(S["bcg_fr"], 1)
                if t == 2:
                    dve_low_weights(v, 1)
                dve_gate(v, t)
            v.wait_ge(S["bcg_fr"], KC // 2)
            v.tensor_tensor(ys[:, :, :], ys[:, :, :], dtcol[:, :, :], ALU.add).then_inc(S["ysx_dv"], 1)
            dve_gate(v, N_Z - 2)
            dve_gate(v, N_Z - 1)

        def dve_attention(v):
            link = dve_link[0]
            mask = pk("amask")
            n_all = NBLK * H
            v.wait_ge(S["st_mm"], NBLK + 1)
            v.wait_ge(S["out_d"], 16)
            v.wait_ge(S["c_dv"], N_Z)
            v.wait_ge(S["pre_pl"], 2 * NBLK + 2)
            v.wait_ge(S["yx_pl"], NBLK)
            for i in range(n_all + 5):
                if i < n_all:
                    b, h = divmod(i, H)
                    lo = 0 if b else P
                    v.wait_ge(S["s_mm"], i + 1)
                    if i >= 4:
                        v.wait_ge(S["p_ac"], i - 3)
                    if h == 0 and b >= 2:
                        v.wait_ge(S["es_ac"], b - 1)
                    link(v.tensor_tensor_reduce(sS[i % 4][:, lo:AW], pb[i % 3][:, lo:AW], mask[:, lo:AW], SCALE,
                                                pk("sinks")[:, h:h + 1], ALU.add, ALU.max, amx[b % 2][:, h:h + 1]))
                    v.tensor_scalar(anm[b % 2][:, h:h + 1], amx[b % 2][:, h:h + 1], -1.0, None, ALU.mult)\
                     .then_inc(S["s_dv"], 1)
                j = i - 2
                if 0 <= j < n_all and j % 2 == 0:
                    v.wait_ge(S["t_mm"], j + 1)
                    if j >= 3:
                        v.wait_ge(S["pv_mm"], j - 2)
                    lo = 0 if j >= H else P
                    v.tensor_copy(pT[j % 3][:, lo:2 * P], pb[3 + j % 3][:, lo:2 * P]).then_inc(S["td_dv"], 1)
                if i % H == 2 and i > 2:
                    b = i // H - 1
                    v.wait_ge(S["s_dv"], H * (b + 1))
                    v.tensor_tensor(aes[b % 2], pk("sinks"), anm[b % 2], ALU.add).then_inc(S["es_dv"], 1)
                if i % H == 4 and i > 4:
                    b = i // H - 1
                    v.wait_ge(S["es_ac"], b + 1)
                    link(v.tensor_tensor(arv[b % 2], als[b % 2], aes[b % 2], ALU.add))
                    link(v.reciprocal(arv[b % 2], arv[b % 2]))
                    v.wait_ge(S["pv_mm"], H * (b + 1))
                    if b == 0:
                        for k in range(3):
                            v.wait_ge(hs_out[k], 16 * len(range(k, KC, 3)))
                    for k in range(2):
                        ins = v.tensor_tensor(YA[:, b + 1, 512 * k:512 * (k + 1)].rearrange("p (h d) -> p h d", d=HD),
                                              pb[6 + k][:, :].rearrange("p (h d) -> p h d", d=HD),
                                              bc(arv[b % 2][:, 8 * k:8 * (k + 1)], HD), ALU.mult)
                    ins.then_inc(S["o_dv"], 1)

        def dve_sample_attention(v):
            link = dve_link[0]
            v.wait_ge(S["cache_in"], 16 * (2 * NSAMP + 3))
            link(v.memset(qs[:, :, :, :, :], 0.0))
            for p in range(2):
                half = slice(HD * p, HD * p + HD)
                for odd in range(2):
                    v.tensor_copy(qs[half, :, p, odd:QPK:2, :],
                                  qT[HD * odd:HD * odd + HD, :, :].rearrange("q (g p j) n -> q g p j n", g=2, p=2)
                                  [:, :, p, :, 0:NSAMP])
                for pair in range(KVH // 2):
                    ins = v.tensor_copy(Ks[half, :, pair, NWK], kd[half, 2 * pair + p, 0:NSAMP])
            ins.then_inc(S["qs_dv"], 1)
            dve_low(v, 1)
            v.wait_ge(S["ss_mm"], 1)
            v.tensor_copy(sT[:, 0:P], pb[0][:, 0:P])
            v.tensor_copy(sTm[0:NMETA, 0:P], pb[1][0:NMETA, 0:P]).then_inc(S["ss_ev"], 1)
            v.wait_ge(S["st2_mm"], 1)
            link(v.tensor_scalar(s2[:, 0:P + NMETA], pb[2][:, 0:P + NMETA], SCALE, None, ALU.mult))
            link(v.tensor_reduce(scol[:, 0:1], s2[:, 0:P + NMETA], AX, ALU.max))
            link(v.tensor_tensor(scol[:, 0:1], scol[:, 0:1], pk("sink_col"), ALU.max))
            v.tensor_scalar(scol[:, 1:2], scol[:, 0:1], -1.0, None, ALU.mult).then_inc(S["sx_dv"], 1)
            v.wait_ge(S["sp_ac"], 1)
            link(v.tensor_tensor(scol[:, 4:5], scol[:, 2:3], scol[:, 3:4], ALU.add))
            link(v.reciprocal(scol[:, 5:6], scol[:, 4:5]))
            v.tensor_scalar(s2[:, 0:P + NMETA], s2[:, 0:P + NMETA], scol[:, 5:6], None, ALU.mult)\
             .then_inc(S["spn_dv"], 1)
            v.wait_ge(S["sot_mm"], 1)
            for k in range(2):
                ins = v.tensor_copy(YA[0:NSAMP, 0, 512 * k:512 * (k + 1)], pb[2 + k][0:NSAMP, :])
            ins.then_inc(S["sya_dv"], 1)

        def dve_low(v, part):
            for k in range(KC):
                v.wait_ge(S["xh_ac"], KC * (part + 1) + k + 1)
                v.tensor_tensor(gxl[:, k, :], xT[:, k, :], gxh[part][:, k, :].bitcast(F32), ALU.subtract)
                v.tensor_tensor(gwl[0][:, k, :], wt[0][:, k, :], gwh[2 * part][:, k, :].bitcast(F32), ALU.subtract)\
                 .then_inc(S["xl_dv"], 1)

        def dve_low_weights(v, j):
            v.wait_ge(S["wh_ac"], FT + {1: 1, 3: 2, 4: 3, 5: 4}[j])
            v.tensor_tensor(gwl[j % 2][:, :, :], wt[j % 2][:, :, :], gwh[j][:, :, :].bitcast(F32), ALU.subtract)\
             .then_inc(S["wl_dv"], 1)

        def dve_gate(v, i):
            link = dve_link[0]
            j, t = GATES[i]
            r, half = tile_rows(t), slice(512 * (j % 2), 512 * (j % 2) + 512)
            g, y = (gate_z if i < N_Z else gate)[i % 4][0:r, :], Y[0:r, t, half]
            if i == 0:
                v.wait_ge(S["yx_pl"], NBLK)
                link(v.memset(ssq[:, :, :], 1.0))
            if i == N_Z - 2:
                v.wait_ge(S["yst_ev"], 1)
            v.wait_ge(S["c_ac"], i + 1)
            if i:
                v.wait_ge(S["c_dv"], i)
            if j >= 4:
                link(v.tensor_tensor(g, g, YA[0:r, t, half], ALU.mult))
            v.tensor_tensor(y, y, g, ALU.add if j >= 4 else ALU.mult).then_inc(S["c_dv"], 1)

        def dve_gates(v):
            v.wait_ge(S["sya_dv"], 1)
            v.wait_ge(S["o_dv"], NBLK)
            dve_low_weights(v, 3)
            dve_rms(v)
            for i in range(N_Z, len(GATES)):
                if GATES[i] in ((3, 1), (4, 1)):
                    dve_low_weights(v, GATES[i][0] + 1)
                dve_gate(v, i)

        def dve_rms(v):
            link = dve_link[0]
            v.wait_ge(S["c_dv"], N_Z)
            v.wait_ge(S["rms_ac"], 1)
            v.wait_ge(S["ln_in"], 16)
            v.tensor_scalar(rstd[:, :, :], ssq[:, :, :], 1.0 / (D // KVH), RMS_EPS, ALU.mult, ALU.add)\
             .then_inc(S["rms_dv"], 1)
            v.wait_ge(S["rms_ac"], 2)
            link(v.reciprocal(rstd[:, :, :], rstd[:, :, :]))
            for t in range(NT):
                r = tile_rows(t)
                for g in range(KVH):
                    s = slice(g * 256, (g + 1) * 256)
                    ins = v.scalar_tensor_tensor(Y[0:r, t, s], Y[0:r, t, s], rstd[0:r, t, g:g + 1], lnr[0:r, 0, s],
                                                 ALU.mult, ALU.mult)
            link(ins)

        def layer_norm(v, x, r, n, gain):
            link = dve_link[0]
            st, mv = lst[(n - 1) % 2], lmv[(n - 1) % 2]
            v.bn_stats(st[0:r, 0:6], x[:, 0:512])
            link(v.bn_stats(st[0:r, 6:12], x[:, 512:1024]))
            link(v.bn_aggr(mv[0:r, 0:2], st[0:r, :]))
            v.tensor_scalar(mv[0:r, 2:3], mv[0:r, 1:2], LN_EPS, None, ALU.add).then_inc(S["lv_dv"], 1)
            v.wait_ge(S["lv_ac"], n)
            link(v.reciprocal(mv[0:r, 3:4], mv[0:r, 2:3]))
            link(v.tensor_scalar(x, x, mv[0:r, 0:1], mv[0:r, 3:4], ALU.subtract, ALU.mult))
            return v.tensor_tensor(x, x, gain, ALU.mult)

        def dve_mix(v):
            link = dve_link[0]
            v.wait_ge(S["xt_in"], 32)

            def norm(t):
                r = tile_rows(t)
                v.wait_ge(S["w_mm"], t + 1)
                for n in range(2):
                    s = slice(512 * n, 512 * n + 512)
                    ins = v.scalar_tensor_tensor(h1[0:r, t, s], h1[0:r, t, s], ALPHA, pb[2 + 2 * (t % 2) + n][0:r, :],
                                                 ALU.mult, ALU.add)
                link(ins)
                layer_norm(v, h1[0:r, t, :], r, t + 1, lnr[0:r, 1, :]).then_inc(S["ln_dv"], 1)

            def logit(t):
                r = tile_rows(t)
                v.wait_ge(S["lg_mm"], t + 1)
                v.tensor_tensor(lg[0:r, t, :], pb[6 + t % 2][0:r, 0:NG + NE], pk("r_bias", r), ALU.add)\
                 .then_inc(S["lg_dv"], 1)

            for t in range(NT):
                norm(t)
                if t == NT - 2:
                    link(v.memset(lg[:, 0, :], 0.0))
                    logit(0)
            for t in range(1, NT):
                logit(t)

        def dve_route(v):
            link = dve_link[0]
            wide = lambda x, *shape: x.broadcast_to((P,) + shape)
            iota4 = wide(pk("iota4").unsqueeze(1), NT, NG)
            iota8 = wide(pk("iota8").unsqueeze(1), NT, EPG)
            iota16 = pk("iota16")

            def first_max(x, iota, n, mx, eq, ix, one):
                link(v.tensor_reduce(mx, x, AX, ALU.max))
                link(v.tensor_tensor(eq, x, bc(mx, n), ALU.is_equal))
                link(v.scalar_tensor_tensor(eq, eq, -64.0, iota, ALU.mult, ALU.add))
                link(v.tensor_reduce(ix, eq, AX, ALU.min))
                link(v.tensor_tensor(one, eq, bc(ix, n), ALU.is_equal))

            v.wait_ge(S["lg_dv"], NT)
            gl = lg[:, :, 0:NG]
            first_max(gl, iota4, NG, gmx, geq[:, :, :], gix, goh[:, :, :])
            v.tensor_tensor(ex[:, :, 0:NG], gl, bc(gmx, NG), ALU.subtract)
            link(v.tensor_tensor(ein_g[:, :, :, :], lg[:, :, NG:NG + NE].rearrange("p t (g j) -> p t g j", g=NG),
                                 wide(goh[:, :, :].unsqueeze(3), NT, NG, EPG), ALU.mult))
            link(v.tensor_reduce(ein[:, :, :], ein_g[:, :, :, :].rearrange("p t g j -> p t j g"), AX, ALU.add))
            first_max(ein[:, :, :], iota8, EPG, emx[:, 0, :], eeq[0][:, :, :], eix[:, 0, :], eoh[0][:, :, :])
            link(v.scalar_tensor_tensor(ein2[:, :, :], eoh[0][:, :, :], -3e38, ein[:, :, :], ALU.mult, ALU.add))
            first_max(ein2[:, :, :], iota8, EPG, emx[:, 1, :], eeq[1][:, :, :], eix[:, 1, :], eoh[1][:, :, :])
            v.tensor_tensor(ex[:, :, NG], emx[:, 1, :], emx[:, 0, :], ALU.subtract).then_inc(S["rt1_dv"], 1)
            link(v.scalar_tensor_tensor(eno[:, :, :], wide(gix.unsqueeze(1), 2, NT), float(EPG), eix[:, :, :],
                                        ALU.mult, ALU.add))
            link(v.tensor_scalar(eno[:, :, :], eno[:, :, :], 64.0 * EPG + 64.0, None, ALU.add))
            o10 = oh[:, :, :, :].rearrange("p k t e -> p (k t) e")
            e10 = eno[:, :, :].rearrange("p k t -> p (k t)")
            link(v.tensor_tensor(o10, wide(pk("iota32").unsqueeze(1), 2 * NT, NE), bc(e10, NE), ALU.is_equal))
            link(v.tensor_scalar(oh[:, :, 0, :], oh[:, :, 0, :], pk("valid")[:, 0:1], None, ALU.mult))
            v.tensor_tensor(chosen.rearrange("p (t e) -> p t e", e=NE), oh[:, 0, :, :], oh[:, 1, :, :], ALU.add)\
             .then_inc(S["ch_dv"], 1)
            for s in scan:
                v.memset(s, 0.0)
            v.memset(odd[:, :, :], 0.0)
            v.tensor_scalar(tb, pk("half32"), float(P), None, ALU.mult)
            v.tensor_scalar(thr8, pk("iota8"), float(P), float(P), ALU.mult, ALU.add)
            v.wait_ge(S["rt_ac"], 1)
            link(v.tensor_reduce(gws, ex[:, :, 0:NG], AX, ALU.add))
            link(v.tensor_scalar(den, ex[:, :, NG], 1.0, None, ALU.add))
            link(v.tensor_tensor(den, den, gws, ALU.mult))
            link(v.reciprocal(prob[:, 0, :], den))
            v.tensor_tensor(prob[:, 1, :], prob[:, 0, :], ex[:, :, NG], ALU.mult)
            v.wait_ge(S["rk_mm"], 1)
            link(v.tensor_copy(cnt[:, :, :].rearrange("p a b -> p (a b)"), pb[6][:, NT * NE:(NT + 1) * NE]))
            v.tensor_copy(odd[:, :, 1], cnt[:, :, 0])
            link(v.tensor_tensor(cpair, cnt[:, :, 0], cnt[:, :, 1], ALU.add))
            link(v.tensor_tensor(over[:, :, :], bc(cpair, EPG), wide(thr8.unsqueeze(1), NPAIR, EPG), ALU.is_gt))
            link(v.tensor_reduce(extra, over[:, :, :], AX, ALU.add))
            link(v.tensor_copy(scan[0][:, NPAIR:], extra))
            for n, step in enumerate((1, 2, 4, 8)):
                a, b = scan[n % 2], scan[(n + 1) % 2]
                link(v.tensor_tensor(b[:, NPAIR:], a[:, NPAIR:], a[:, NPAIR - step:2 * NPAIR - step], ALU.add))
            cum = scan[0][:, NPAIR:]
            link(v.tensor_tensor(obase, cum, extra, ALU.subtract))
            link(v.tensor_tensor(ccol, obase, iota16, ALU.subtract))
            link(v.tensor_scalar(ccol, ccol, float(P), float(P * (NPAIR - 1)), ALU.mult, ALU.add))
            v.tensor_copy(tc[:, :, :], bc(ccol, 2))
            link(v.tensor_tensor(rank[:, :, :], pb[6][:, 0:NT * NE].rearrange("p (t e) -> p t e", e=NE),
                                 wide(odd[:, :, :].rearrange("p a b -> p (a b)").unsqueeze(1), NT, NE), ALU.add))
            for n, w in enumerate((wide(rank[:, :, :].unsqueeze(1), 2, NT, NE), None, None)):
                if n == 0:
                    ins = v.tensor_tensor(pick[0][:, :, :, :], oh[:, :, :, :], w, ALU.mult)
                else:
                    w = (tb, tc[:, :, :].rearrange("p a b -> p (a b)"))[n - 1]
                    ins = v.tensor_tensor(pick[n][:, :, :, :].rearrange("p k t e -> p (k t) e"), o10,
                                          wide(w.unsqueeze(1), 2 * NT, NE), ALU.mult)
            link(ins)
            for n in range(3):
                ins = v.tensor_reduce(sel[n], pick[n][:, :, :, :].rearrange("p k t e -> p (k t) e"), AX, ALU.add)
            link(ins)
            v.tensor_tensor(sel[1], sel[1], sel[0], ALU.add)
            link(v.tensor_scalar(far, sel[0], float(P), None, ALU.is_ge))
            link(v.tensor_tensor(far, far, sel[2], ALU.mult))
            v.tensor_tensor(slot, far, sel[1], ALU.add).then_inc(S["slot_dv"], 1)
            link(v.tensor_tensor(below[:, :, :], wide(cum.unsqueeze(1), EPG, NPAIR), bc(pk("iota8"), NPAIR), ALU.is_le))
            v.tensor_copy(pair[:, 0:NPAIR], iota16)
            link(v.tensor_reduce(pair[:, NPAIR:], below[:, :, :], AX, ALU.add))
            link(v.tensor_scalar(pair[:, NPAIR:], pair[:, NPAIR:], float(NPAIR - 1), None, ALU.min))
            v.tensor_scalar(table[:, 0:1], cum[:, NPAIR - 1:NPAIR], float(NPAIR), None, ALU.add)
            v.tensor_scalar(table[:, 1:2], cum[:, NPAIR - 1:NPAIR], float(NPAIR - 1), None, ALU.add)
            two = table[:, 2:].rearrange("p (b u) -> p b u", u=2)
            v.tensor_scalar(two[:, :, 0], pair, 2.0, None, ALU.mult)
            v.tensor_scalar(two[:, :, 1], pair, 2.0, 1.0, ALU.mult, ALU.add).then_inc(S["tab_dv"], 1)
            v.scalar_tensor_tensor(c128, obase, float(P), cnt[:, :, 0], ALU.mult, ALU.add)
            link(v.tensor_tensor(thr_g[:, :, :], wide(iota16.unsqueeze(1), EPG, NPAIR), bc(pair[:, NPAIR:], NPAIR),
                                 ALU.is_equal))
            link(v.tensor_tensor(thr_g[:, :, :], thr_g[:, :, :], wide(c128.unsqueeze(1), EPG, NPAIR), ALU.mult))
            v.tensor_copy(thr[:, 0:NPAIR], cnt[:, :, 0])
            link(v.tensor_reduce(thr[:, NPAIR:], thr_g[:, :, :], AX, ALU.add))
            link(v.tensor_tensor(thr[:, NPAIR:], thr[:, NPAIR:], thr8, ALU.subtract))
            link(v.tensor_scalar(mask[:, :, 0], thr, pk("iota_p"), None, ALU.is_gt))
            link(v.tensor_scalar(mask[:, :, 1], mask[:, :, 0], -1.0, 1.0, ALU.mult, ALU.add))

        def dve_experts(v):

            def empty_x():
                v.tensor_copy(XT[:, 4:8, :].rearrange("p k c -> p (k c)"), pb[1][:, :]).then_inc(S["xt_d"], 1)

            v.wait_ge(S["xtr_mm"], 1)
            empty_x()
            v.wait_ge(S["tab_dv"], 1)
            blocks = v.value_load(table[0:1, 0:1], min_val=NPAIR, max_val=NBT)
            with v.Fori(0, blocks) as i:
                v.tensor_copy(mcol[:, :, :], mask[:, bass.ds(i, 1), :]).then_inc(S["mc_dv"], 1)
                v.wait_ge(S["mc_dv"], i + 1)
                for u in range(2):
                    v.wait_ge(S["sg_ac"], i * 2 + (u + 1))
                    v.scalar_tensor_tensor(hid[u], pb[2 + u][:, DE:2 * DE], mcol[:, 0, u:u + 1], sg[u],
                                           ALU.mult, ALU.mult).then_inc(S["hid_dv"], 1)
                v.wait_ge(S["htr_mm"], i * 2 + 2)
                v.tensor_copy(hidT[1][:, :, :].rearrange("p k c -> p (k c)"), pb[5][:, 0:DE]).then_inc(S["hte1"], 1)
                v.wait_ge(S["xtr_mm"], i + 2)
                empty_x()
                v.wait_ge(S["dn_mm"], i * 2 + 2)
                v.wait_ge(S["yw_out"], i * 16 + 16)
                v.tensor_copy(Yout[:, 512:1024], pb[7][:, :]).then_inc(S["y_d"], 1)
                v.wait_ge(S["y_d"], i + 1)

        def dve_final(v):
            link = dve_link[0]
            for t in range(NT):
                r = tile_rows(t)
                h = h1[0:r, t, :]
                v.wait_ge(S["gp_ac"], t + 1)
                link(v.scalar_tensor_tensor(h, h, ALPHA, G[0][0:r, t, :], ALU.mult, ALU.add))
                link(v.scalar_tensor_tensor(h, G[1][0:r, t, :], prob[0:r, 1, t:t + 1], h, ALU.mult, ALU.add))
                layer_norm(v, h, r, NT + t + 1, lnr[0:r, 3, :]).then_inc(S["ln_dv"], 1)

        def pool_projection(p):
            p.memset(xbc[:, :, 0:3], 0.0).then_inc(S["pool_init"], 1)
            p.memset(vd[:, 0, :], 0.0).then_inc(S["pool_init"], 1)
            p.memset(vd[:, META, :], 0.0).then_inc(S["pool_init"], 1)
            p.memset(zeros, 0.0).then_inc(S["zero_pl"], 1)
            p.wait_ge(S["sconv_dv"], 1)
            p.dma_start(io["o_pconv"], pconv).then_inc(S["small_out"], 16)
            p.dma_start(io["o_sconv"], xs4[:, :, 1:CW, :]).then_inc(S["small_out"], 16)
            for j in range(QT_TILES + KT_TILES):
                i = XT_TILES + 3 + j
                if i < FT:
                    p.wait_ge(S["wh_ac"], i + 1)
                    p.wait_ge(S["wl_dv"], i)
                    p.tensor_tensor(wfl[i % 4][:, :, :], wf[i % 4][:, :, :], wfh[i % 4][:, :, :].bitcast(F32),
                                    ALU.subtract).then_inc(S["wl_dv"], 1)
                p.wait_ge(S["f_ev"], XT_TILES + j + 1)
                p.wait_ge(S["rope_in"], 32)
                if j:
                    p.wait_ge(S["rope_dv"], j)
                p.tensor_tensor(rcs, raw[j % 2], cosT, ALU.mult).then_inc(S["rc_pl"], 1)

        def pool_outputs(p):
            p.wait_ge(S["rope_dv"], QT_TILES + KT_TILES)
            p.dma_start(io["o_k"], kd[0:HD, :, :]).then_inc(S["small_out"], 16)
            p.wait_ge(S["vd_ev"], NT)
            p.dma_start(io["o_v0"], vd[0:PR0, 0, 0:KVH * HD]).then_inc(S["small_out"], 16)
            p.dma_start(io["o_v1"], vd[:, NT - 1, 0:KVH * HD]).then_inc(S["small_out"], 16)

        def pool_ssd(p):
            link = pool_link[0]
            p.wait_ge(S["sp5_ac"], 1)
            for c in range(NBLK + 1):
                t, n = (c, P) if c else (META, NMETA)
                h3 = lambda a: a[0:n, :].rearrange("p (h d) -> p h d", d=HD)
                p.wait_ge(S["tr_ev"], c + 1)
                if c:
                    p.wait_ge(S["st_mm"], c)
                p.tensor_tensor(h3(xd), h3(xt), bc(dt[0:n, t, :], HD), ALU.mult).then_inc(S["pre_pl"], 1)
                p.wait_ge(S["pre_pl"], 2 * c + 1)
                p.tensor_tensor(h3(xdd), h3(xd), bc(dst[0:n, t, :], HD), ALU.mult).then_inc(S["pre_pl"], 1)
                if c:
                    if c > 1:
                        p.wait_ge(S["yx_pl"], c - 1)
                    link(p.tensor_tensor(h3(Dx), h3(xt), bc(pk("d_skip"), HD), ALU.mult))
                    p.wait_ge(S["h_dv"], c)
                    p.tensor_tensor(Ht.rearrange("p (h d) -> p h d", d=HD), Hs.rearrange("p (h d) -> p h d", d=HD),
                                    bc(etot[:, t, :], HD), ALU.mult).then_inc(S["ht_pl"], 1)
                    p.wait_ge(S["ya_dv"], 2 * c)
                    p.tensor_tensor(Y[:, c, :], Y[:, c, :], Dx, ALU.add).then_inc(S["yx_pl"], 1)
            p.wait_ge(S["h_dv"], NBLK + 1)
            p.dma_start(io["o_pssm"], Hs).then_inc(S["out_d"], 16)
            pool_outputs(p)

        def pool_sample_state(p):
            for t in range(KC):
                p.wait_ge(S["sh_dv"], t + 1)
                p.dma_start(io["o_sssm"][t], hst[t % 3]).then_inc(hs_out[t % 3], 16)

        def pool_meta(p):
            for i in range(NBLK * KVH):
                p.wait_ge(S["p_ac"], QPK * (i + 1))
                if i >= 2:
                    p.wait_ge(S["t_mm"], QPK * (i - 1))
                p.tensor_copy(pM[i % 2].rearrange("p (r m) -> p r m", r=QPK), pS4[i % 2][:, :, P:P + NMETA])\
                 .then_inc(S["pm_pl"], 1)
                b = i // KVH + 1
                if b < NBLK and i % KVH < 2:
                    (pool_block_high, pool_block_low)[i % KVH](p, b)

        def pool_block_high(p, b):
            for lo, hi, src in seen_keys(b):
                p.tensor_copy(kx[b - 1][:, :, lo:hi], kd[:, :, src:src + hi - lo])
            q = slice(PR0 + P * b, PR0 + P * (b + 1))
            p.tensor_copy(qh[b - 1][:, :, :], qT[:, :, q]).then_inc(S["kx_pl"], 1)

        def seen_keys(b):
            return ((0, P, PR0 + P * (b - 1)), (P, P + NMETA, SEQ0), (P + NMETA, AW, PR0 + P * b))

        def pool_block_low(p, b):
            p.wait_ge(S["kx_pl"], 2 * b)
            q = slice(PR0 + P * b, PR0 + P * (b + 1))
            for lo, hi, src in seen_keys(b):
                p.tensor_tensor(kl[b - 1][:, :, lo:hi], kd[:, :, src:src + hi - lo],
                                kx[b - 1][:, :, lo:hi].bitcast(F32), ALU.subtract)
            p.tensor_tensor(ql[:, :, q], qT[:, :, q], qh[b - 1][:, :, :].bitcast(F32), ALU.subtract)\
             .then_inc(S["kx_pl"], 1)

        def pool_keys(p):
            p.wait_ge(S["ysx_dv"], 1)
            p.wait_ge(S["out_d"], 16)
            p.wait_ge(S["yst_mm"], 1)
            p.wait_ge(S["c_mm"], N_Z)
            p.memset(vm[:, :, :], 0.0).then_inc(S["kx_pl"], 1)

        def pool_mix(p):
            p.wait_ge(S["ln_in"], 16)
            for t in range(NT):
                r = tile_rows(t)
                p.wait_ge(S["ln_dv"], t + 1)
                p.tensor_tensor(h1[0:r, t, :], h1[0:r, t, :], lnr[0:r, 2, :], ALU.add).then_inc(S["lnb_pl"], 1)

        def pool_scatter(p):
            p.wait_ge(S["slot_dv"], 1)
            p.wait_ge(S["lnb_pl"], NT)
            p.wait_ge(S["zero_out"], 32)
            for k in range(2):
                for t in range(NT):
                    r, c = tile_rows(t), k * NT + t
                    p.indirect_dma_start(scr_x, bass.IndirectOffsetOnAxis(ap=slot[0:r, c:c + 1].bitcast(U32), axis=0),
                                         h1[0:r, t, :], None).then_inc(S["sc_out"], 16)

        def pool_final(p):
            p.wait_ge(S["moe_ac"], 1)
            for t in range(NT):
                for k in range(2):
                    r, c = tile_rows(t), k * NT + t
                    p.indirect_dma_start(G[k][0:r, t, :], None, scr_y,
                                         bass.IndirectOffsetOnAxis(ap=slot[0:r, c:c + 1].bitcast(U32), axis=0))\
                     .then_inc(S[f"gt{t}"], 16)
            for t in range(NT):
                r = tile_rows(t)
                p.wait_ge(S["ln_dv"], NT + t + 1)
                p.tensor_tensor(h1[0:r, t, :], h1[0:r, t, :], lnr[0:r, 4, :], ALU.add).then_inc(S["o_pl"], 1)

        @block.sync
        def _(sp):
            sp_projection(sp)
            sp_sample_state(sp)
            sp_gates(sp)
            sp_experts(sp)
            sp_outputs(sp)

        @block.tensor
        def _(pe):
            pe_projection(pe)
            pe_ssd(pe)
            pe_sample_bc(pe)
            pe_gates(pe, 0, N_Z)
            pe_sample_y(pe)
            pe_attention(pe)
            pe_sample_attention(pe)
            pe_gates(pe, N_Z + 3, len(GATES))
            pe_mix(pe)
            pe_rank(pe)
            pe_experts(pe)

        @block.scalar
        def _(act):
            act_link.append(chained(act, S["act_chain"]))
            act_projection(act)
            act_ssd(act)
            act_sample_state(act)
            act_attention(act)
            act_sample_attention(act)
            act_gates(act)
            act_mix(act)
            act_route(act)
            act_experts(act)
            act_final(act)

        @block.vector
        def _(v):
            dve_link.append(chained(v, S["dve_chain"]))
            dve_projection(v)
            dve_ssd(v)
            dve_sample_state(v)
            dve_attention(v)
            dve_sample_attention(v)
            dve_gates(v)
            dve_mix(v)
            dve_route(v)
            dve_experts(v)
            dve_final(v)

        @block.gpsimd
        def _(p):
            pool_link.append(chained(p, S["pool_chain"]))
            pool_projection(p)
            pool_ssd(p)
            pool_sample_state(p)
            pool_keys(p)
            pool_meta(p)
            p.wait_ge(S["small_out"], 80)
            p.wait_ge(S["out_d"], 16)
            for k in range(3):
                p.wait_ge(hs_out[k], 16 * len(range(k, KC, 3)))
            pool_mix(p)
            pool_scatter(p)
            pool_final(p)


def constants():
    i = np.arange(P)
    tri = (i[:, None] <= i[None, :]).astype(np.float32)
    c = {
        "ident": np.eye(P), "upper": tri, "ones": np.ones((P, P)),
        "neg": np.where(tri > 0, 0.0, NEG), "strict": tri - np.eye(P),
        "amask": np.concatenate([np.where(i[None, :] > i[:, None], 0.0, NEG), np.zeros((P, NMETA)),
                                 np.where(i[None, :] <= i[:, None], 0.0, NEG)], 1),
        "iota_p": i[:, None], "iota4": np.tile(np.arange(NG), (P, 1)), "iota8": np.tile(np.arange(EPG), (P, 1)),
        "iota16": np.tile(np.arange(NPAIR), (P, 1)), "half32": np.tile(np.arange(NE) // 2, (P, 1)),
        "iota32": np.tile(np.arange(NE), (P, 1)),
        "valid": np.concatenate([(i[:, None] < NSAMP), np.ones((P, NBLK))], 1),
    }
    pos = np.concatenate([np.full(NSAMP, PAST), np.arange(NSEQ)]).astype(np.float32)
    half = HD // 2
    freq = np.exp(np.float32(-np.log(10000.0)) * np.arange(half, dtype=np.float32) * np.float32(2.0 / HD))
    ang = (pos[None, :] * freq[:, None].astype(np.float32)).astype(np.float32)
    cos, sin = np.cos(ang), np.sin(ang)
    rope = np.stack([np.concatenate([cos] * 4), np.concatenate([sin, -sin] * 2)]).astype(np.float32)
    return {k: np.asarray(v, np.float32) for k, v in c.items()}, rope


def lay_out(x):
    def cols(w):
        return w.reshape(KC, P, -1).transpose(1, 0, 2)

    def rows(v):
        return np.broadcast_to(v[None, :], (P, v.shape[0]))

    def pairs(k):
        n, s = k.shape[:2]
        return k.reshape(n, s, KVH // 2, 2, HD).transpose(3, 4, 0, 2, 1).reshape(P, n, KVH // 2, s)

    c, rope = constants()
    w = x["w_in"][0]
    edge = np.cumsum([0, H * HD, KVH * HD, KVH * HD, D, 2048, H, D, D])
    q, k, v, z, xbc, dt, ga, gs = (w[:, edge[i]:edge[i + 1]] for i in range(8))
    c["conv_w"] = x["conv_w"][0].reshape(CW, XT_TILES, P).transpose(2, 1, 0).reshape(P, -1)
    c["conv_b"] = x["conv_b"][0].reshape(XT_TILES, P).T
    for name in ("dt_bias", "a_log", "d_skip"):
        c[name] = rows(x[name][0])
    c["sinks"] = rows(x["attn_sinks"][0])
    c["sink_col"] = np.tile(x["attn_sinks"][0], NSAMP)[:, None]
    c["d_col"] = np.repeat(x["d_skip"][0], HD).reshape(KC, P).T
    c["r_bias"] = rows(np.concatenate([x["router_group_b"][0], x["router_expert_b"][0]]))
    tok = np.concatenate([x["x_sample"][:, 0], x["meta_tokens"], x["x_prompt"][0]])
    f = np.concatenate([xbc, q, k], 1)
    a = {
        "pack": np.concatenate([c[n] for n in PACK], 1),
        "x_t": tok.T.reshape(KC, P, NTOK).transpose(1, 0, 2),
        "x_tok": np.concatenate([x["x_sample"][:, 0], x["x_prompt"][0]]),
        "rope": rope,
        "w_f": f.reshape(KC, P, FT, P).transpose(2, 1, 0, 3),
        "w_vd": cols(np.concatenate([v, dt], 1)),
        "w_t": np.concatenate([z, gs, ga], 1).reshape(KC, P, 6, 512).transpose(2, 1, 0, 3),
        "w_o": cols(x["w_o"][0]),
        "w_r": cols(np.concatenate([x["router_group_w"][0], x["router_expert_w"][0]], 1)),
        "conv_state": x["state_conv"][0].reshape(NSAMP, CW - 1, XT_TILES, P).transpose(3, 2, 1, 0),
        "state": x["state_ssm"][0].reshape(NSAMP, KC, P, NST).transpose(1, 2, 0, 3),
        "win_k": pairs(x["cache_win_k"][0][:, 1:]),
        "win_v": x["cache_win_v"][0][:, 1:].reshape(NSAMP, NWK, KVH * HD).transpose(1, 0, 2),
        "meta_k": pairs(x["cache_meta_k"][0]),
        "meta_v": x["cache_meta_v"][0].reshape(NSAMP, NMETA, KVH * HD).transpose(1, 0, 2),
        "ln": np.stack([x[n][0] for n in ("ssm_norm_w", "ln1_g", "ln1_b", "ln2_g", "ln2_b")]),
        "w_gu": np.concatenate([x["w_gate"][0], x["w_up"][0]], 2).reshape(NE, KC, P, 2 * DE).transpose(0, 2, 1, 3),
        "w_d": x["w_down"][0].reshape(NE, DE // P, P, D).transpose(0, 2, 1, 3),
    }
    return {k: np.ascontiguousarray(v, dtype=np.float32) for k, v in a.items()}


OUTS = {
    "o_prompt": (NPROMPT, D), "o_sample": (NSAMP, D), "o_k": (HD, KVH, NTOK), "o_v0": (PR0, KVH * HD),
    "o_v1": (P, KVH * HD), "o_pconv": (P, XT_TILES, CW - 1), "o_sconv": (P, XT_TILES, CW - 1, NSAMP),
    "o_pssm": (P, D), "o_sssm": (KC, P, NSAMP, NST),
}


def kernel(**inputs):
    import concourse.bacc as bacc
    from concourse.bass_utils import run_bass_kernel_spmd as run

    arrays = lay_out({k: np.asarray(v) for k, v in inputs.items()})
    nc = bacc.Bacc("TRN2", target_bir_lowering=False, num_devices=1)
    io = {n: nc.dram_tensor(f"in_{n}", a.shape, F32, kind="ExternalInput").ap() for n, a in arrays.items()}
    io |= {n: nc.dram_tensor(n, s, F32, kind="ExternalOutput").ap() for n, s in OUTS.items()}
    build(nc, io)
    r = run(nc, [{f"in_{n}": a for n, a in arrays.items()}], core_ids=[0]).results[0]
    k = r["o_k"]
    head = lambda a: a.transpose(2, 1, 0)
    v4 = lambda a: a.reshape(-1, KVH, HD)
    conv = lambda a: a.transpose(2, 1, 0).reshape(CW - 1, XT_TILES * P)
    sconv = r["o_sconv"].transpose(3, 2, 1, 0).reshape(NSAMP, CW - 1, XT_TILES * P)
    pssm = r["o_pssm"].reshape(NST, H, HD).transpose(1, 2, 0)
    sssm = r["o_sssm"].reshape(H, HD, NSAMP, NST).transpose(2, 0, 1, 3)
    return (
        r["o_prompt"][None], r["o_sample"][:, None],
        head(k[:, :, SEQ0:PR0])[None, None], v4(r["o_v0"][SEQ0:])[None, None],
        head(k[:, :, NTOK - WIN:])[None, None], v4(r["o_v1"])[None, None],
        conv(r["o_pconv"])[None, None], pssm[None, None],
        head(k[:, :, :NSAMP])[None, :, None], v4(r["o_v0"][:SEQ0])[None, :, None],
        sconv[None], sssm[None],
    )
```
